# Optimizing a Trainium2 kernel written in Bass

```python
import jax, jax.numpy as jnp
from jax import lax
import numpy as np
import math

D_MODEL = 1024
BATCH = 1
SEQ = 512
DEPTH = 2

N_MIXERS = 2
EXPAND = 2
D_INNER = EXPAND * D_MODEL
HEAD_SIZE = 64
N_HEADS = D_INNER // HEAD_SIZE
LORA_DECAY = 64
LORA_A = 64
LORA_V = 32
N_LERP = 6
CONV_WIDTH = 3
N_RWKV = (DEPTH + 1) // 2
N_CONV = DEPTH // 2
RMS_EPS = 1e-6
GN_EPS = 64e-5
L2_EPS = 1e-12


def rms_norm(x, g):
    x32 = x.astype(jnp.float32)
    y = x32 * lax.rsqrt(jnp.mean(x32 * x32, axis=-1, keepdims=True) + RMS_EPS)
    return (y * g.astype(jnp.float32)).astype(x.dtype)

def token_shift(h):
    return jnp.pad(h, ((0, 0), (1, 0), (0, 0)))[:, :-1]

def head_group_norm(y, w, b):
    mu = jnp.mean(y, axis=-1, keepdims=True)
    var = jnp.mean(jnp.square(y - mu), axis=-1, keepdims=True)
    yn = (y - mu) * lax.rsqrt(var + GN_EPS)
    bsz, t = y.shape[0], y.shape[1]
    return yn.reshape(bsz, t, D_INNER) * w + b

def wkv7_scan(r, decay, k, v, kk, kka):
    bsz, _, nh, n = r.shape

    def step(S, inp):
        r_t, w_t, k_t, v_t, kk_t, kka_t = inp
        sa = jnp.einsum('bhvk,bhk->bhv', S, kk_t)
        S = (S * w_t[:, :, None, :]
             - sa[..., None] * kka_t[:, :, None, :]
             + v_t[..., None] * k_t[:, :, None, :])
        y_t = jnp.einsum('bhvk,bhk->bhv', S, r_t)
        return S, y_t

    seq_first = lambda z: jnp.moveaxis(z, 1, 0)
    S0 = jnp.zeros((bsz, nh, n, n), jnp.float32)
    _, ys = lax.scan(step, S0, (seq_first(r), seq_first(decay), seq_first(k),
                                seq_first(v), seq_first(kk), seq_first(kka)))
    return jnp.moveaxis(ys, 0, 1)

def rwkv7_time_mix(h, v_first, mu, w_in, w0, w1, w2, a0, a1, a2, k_k, k_a, r_k,
                   lnx_w, lnx_b, w_out, v_res):
    bsz, t, _ = h.shape
    f32 = jnp.float32
    xx = token_shift(h) - h
    lerp = lambda j: h + xx * mu[j]
    xr, xw, xk, xv, xa, xg = (lerp(j) for j in range(N_LERP))
    r = xr @ w_in[0]
    k = xk @ w_in[1]
    v = xv @ w_in[2]
    g = xg @ w_in[3]
    w_log = -jax.nn.softplus(-(w0 + jnp.tanh(xw @ w1) @ w2).astype(f32)) - 0.5
    decay = jnp.exp(-jnp.exp(w_log))
    a = jax.nn.sigmoid((a0 + (xa @ a1) @ a2).astype(f32))
    if v_res is None:
        v_first = v
    else:
        v0, v1, v2 = v_res
        v = v + (v_first - v) * jax.nn.sigmoid(v0 + (xv @ v1) @ v2)
    heads = lambda z: z.astype(f32).reshape(bsz, t, N_HEADS, HEAD_SIZE)
    kk = heads(k * k_k)
    kk = kk / jnp.maximum(jnp.linalg.norm(kk, axis=-1, keepdims=True), L2_EPS)
    k = k.astype(f32) * (1.0 + (a - 1.0) * k_a.astype(f32))
    rh, kh, vh, ah = heads(r), heads(k), heads(v), heads(a)
    y = wkv7_scan(rh, heads(decay), kh, vh, kk, kk * ah)
    y = head_group_norm(y, lnx_w.astype(f32), lnx_b.astype(f32))
    bonus = (jnp.sum(rh * kh * r_k.astype(f32), axis=-1, keepdims=True) * vh)
    y = (y + bonus.reshape(bsz, t, D_INNER)) * jax.nn.silu(g.astype(f32))
    return y.astype(h.dtype) @ w_out, v_first

def short_conv_mix(h, w_in, conv_w, w_out):
    z = h @ w_in
    c, b, u, g = jnp.split(z, 4, axis=-1)
    cu = c * u
    conv = lax.conv_general_dilated(
        cu, conv_w[:, None, :].astype(cu.dtype), window_strides=(1,),
        padding=[(CONV_WIDTH - 1, 0)], dimension_numbers=('NWC', 'WIO', 'NWC'),
        feature_group_count=D_INNER)
    y = b * conv * jax.nn.silu(g)
    return y @ w_out

def first_inputs(seed: int = 0) -> dict:
    key = jax.random.key(seed)
    ks = jax.random.split(key, 32)
    nrm = lambda i, shape, s: s * jax.random.normal(ks[i], shape, jnp.float32)
    uni = lambda i, shape, lo, hi: jax.random.uniform(ks[i], shape, jnp.float32, lo, hi)
    D, DI, NA, NB, NV = D_MODEL, D_INNER, N_RWKV, N_CONV, max(N_RWKV - 1, 0)
    return {
        "x": nrm(0, (BATCH, SEQ, D), 1.0),
        "a_norm": 1.0 + nrm(1, (NA, D), 0.02),
        "a_mu": uni(2, (NA, N_LERP, D), 0.0, 1.0),
        "a_w_in": nrm(3, (NA, 4, D, DI), D ** -0.5),
        "a_w0": uni(4, (NA, DI), -6.0, -1.0),
        "a_w1": nrm(5, (NA, D, LORA_DECAY), D ** -0.5),
        "a_w2": nrm(6, (NA, LORA_DECAY, DI), 0.5 * LORA_DECAY ** -0.5),
        "a_a0": nrm(7, (NA, DI), 0.1),
        "a_a1": nrm(8, (NA, D, LORA_A), D ** -0.5),
        "a_a2": nrm(9, (NA, LORA_A, DI), 0.5 * LORA_A ** -0.5),
        "a_kk": 0.85 + nrm(10, (NA, DI), 0.05),
        "a_ka": 1.0 + nrm(11, (NA, DI), 0.05),
        "a_rk": nrm(12, (NA, N_HEADS, HEAD_SIZE), 0.1),
        "a_lnw": 1.0 + nrm(13, (NA, DI), 0.02),
        "a_lnb": nrm(14, (NA, DI), 0.02),
        "a_w_out": nrm(15, (NA, DI, D), DI ** -0.5),
        "a_v0": 1.0 + nrm(16, (NV, DI), 0.1),
        "a_v1": nrm(17, (NV, D, LORA_V), D ** -0.5),
        "a_v2": nrm(18, (NV, LORA_V, DI), 0.5 * LORA_V ** -0.5),
        "b_norm": 1.0 + nrm(19, (NB, D), 0.02),
        "b_w_in": nrm(20, (NB, D, 4 * DI), D ** -0.5),
        "b_conv": nrm(21, (NB, CONV_WIDTH, DI), CONV_WIDTH ** -0.5),
        "b_w_out": nrm(22, (NB, DI, D), DI ** -0.5),
        "final_norm": 1.0 + nrm(23, (D,), 0.02),
    }

def first_block(x, a_norm, a_mu, a_w_in, a_w0, a_w1, a_w2, a_a0, a_a1, a_a2, a_kk, a_ka,
              a_rk, a_lnw, a_lnb, a_w_out, a_v0, a_v1, a_v2, b_norm, b_w_in, b_conv,
              b_w_out, final_norm):
    v_first = None
    for i in range(DEPTH):
        j = i // N_MIXERS
        if i % N_MIXERS == 0:
            h = rms_norm(x, a_norm[j])
            v_res = None if j == 0 else (a_v0[j - 1], a_v1[j - 1], a_v2[j - 1])
            out, v_first = rwkv7_time_mix(
                h, v_first, a_mu[j], a_w_in[j], a_w0[j], a_w1[j], a_w2[j],
                a_a0[j], a_a1[j], a_a2[j], a_kk[j], a_ka[j], a_rk[j],
                a_lnw[j], a_lnb[j], a_w_out[j], v_res)
        else:
            h = rms_norm(x, b_norm[j])
            out = short_conv_mix(h, b_w_in[j], b_conv[j], b_w_out[j])
        x = x + out
    return rms_norm(x, final_norm)


DEPTH_2 = 1

CHUNK = 64
CONV_DIM = D_MODEL // 2
CONV_WIDTH_2 = 31
N_HEADS_2 = 8
HEAD_DIM = 64
ATT_DIM = N_HEADS_2 * HEAD_DIM
QBLOCK = 128
D_FF = ((8 * D_MODEL + 3 * 256 - 1) // (3 * 256)) * 256
EPS = 1e-6
IN_COLS = 2 * CONV_DIM + 3 * ATT_DIM + 2 * D_MODEL


def rmsnorm(x, g):
    xf = x.astype(jnp.float32)
    y = xf * lax.rsqrt(jnp.mean(xf * xf, axis=-1, keepdims=True) + EPS)
    return (y * g.astype(jnp.float32)).astype(x.dtype)

def layernorm(x, g, b):
    xf = x.astype(jnp.float32)
    mu = jnp.mean(xf, axis=-1, keepdims=True)
    var = jnp.mean(jnp.square(xf - mu), axis=-1, keepdims=True)
    y = (xf - mu) * lax.rsqrt(var + EPS)
    return (y * g.astype(jnp.float32) + b.astype(jnp.float32)).astype(x.dtype)

def causal_depthwise_conv(u, w, b):
    k, c = w.shape
    up = jnp.pad(u, ((0, 0), (k - 1, 0), (0, 0)))
    y = lax.conv_general_dilated(
        up, w[:, None, :].astype(u.dtype), window_strides=(1,), padding='VALID',
        dimension_numbers=('NWC', 'WIO', 'NWC'), feature_group_count=c)
    return y + b.astype(u.dtype)

def stick_breaking_attention(q, k, v):
    s_len = q.shape[1]
    scale = 1.0 / math.sqrt(q.shape[-1])
    outs = []
    for i in range(s_len // QBLOCK):
        q0 = i * QBLOCK
        q1 = q0 + QBLOCK
        qb = q[:, q0:q1].astype(jnp.float32)
        kb = k[:, :q1].astype(jnp.float32)
        vb = v[:, :q1].astype(jnp.float32)
        z = jnp.einsum('bqhd,bkhd->bhqk', qb, kb) * scale
        t_idx = q0 + jnp.arange(QBLOCK)[:, None]
        s_idx = jnp.arange(q1)[None, :]
        mask = s_idx < t_idx
        log_1m = jnp.where(mask, jax.nn.log_sigmoid(-z), 0.0)
        rev_excl = lax.cumsum(log_1m, axis=3, reverse=True) - log_1m
        a = jnp.where(mask, jnp.exp(jax.nn.log_sigmoid(z) + rev_excl), 0.0)
        outs.append(jnp.einsum('bhqk,bkhd->bqhd', a, vb))
    return jnp.concatenate(outs, axis=1).astype(q.dtype)

def second_inputs(seed: int = 0) -> dict:
    key = jax.random.key(seed)
    ks = jax.random.split(key, 20)
    f32 = jnp.float32

    def w(k, shape, fan_in):
        return jax.random.normal(k, shape, f32) * (fan_in ** -0.5)

    def gain(k, n):
        return 1.0 + 0.05 * jax.random.normal(k, (n,), f32)

    def bias(k, n):
        return 0.02 * jax.random.normal(k, (n,), f32)

    return {
        'x': jax.random.normal(ks[0], (BATCH, SEQ, D_MODEL), f32),
        'norm_mix_pre': gain(ks[1], D_MODEL),
        'w_in': w(ks[2], (D_MODEL, IN_COLS), D_MODEL),
        'conv_dw_w': w(ks[3], (CONV_WIDTH_2, CONV_DIM), CONV_WIDTH_2),
        'conv_dw_b': bias(ks[4], CONV_DIM),
        'conv_ln_g': gain(ks[5], CONV_DIM),
        'conv_ln_b': bias(ks[6], CONV_DIM),
        'w_conv_branch': w(ks[7], (CONV_DIM, D_MODEL), CONV_DIM),
        'b_conv_branch': bias(ks[8], D_MODEL),
        'w_att_branch': w(ks[9], (ATT_DIM, D_MODEL), ATT_DIM),
        'w_out': w(ks[10], (D_MODEL, D_MODEL), D_MODEL),
        'norm_mix_post': gain(ks[11], D_MODEL),
        'norm_ffn_pre': gain(ks[12], D_MODEL),
        'w_ffn_up': w(ks[13], (D_MODEL, 2 * D_FF), D_MODEL),
        'w_ffn_down': w(ks[14], (D_FF, D_MODEL), D_FF),
        'norm_ffn_post': gain(ks[15], D_MODEL),
    }

def second_block(x, norm_mix_pre, w_in, conv_dw_w, conv_dw_b, conv_ln_g, conv_ln_b,
              w_conv_branch, b_conv_branch, w_att_branch, w_out, norm_mix_post,
              norm_ffn_pre, w_ffn_up, w_ffn_down, norm_ffn_post):
    b, s, d = x.shape
    for _ in range(DEPTH_2):
        h = rmsnorm(x, norm_mix_pre)
        proj = jnp.einsum('bsd,de->bse', h, w_in)
        splits = np.cumsum([2 * CONV_DIM, ATT_DIM, ATT_DIM, ATT_DIM, D_MODEL]).tolist()
        conv_in, q, k, v, g_conv, g_att = jnp.split(proj, splits, axis=-1)

        u = jax.nn.glu(conv_in, axis=-1)
        u = causal_depthwise_conv(u, conv_dw_w, conv_dw_b)
        u = jax.nn.silu(layernorm(u, conv_ln_g, conv_ln_b))
        conv_out = jnp.einsum('bsc,cd->bsd', u, w_conv_branch) + b_conv_branch

        q = q.reshape(b, s, N_HEADS_2, HEAD_DIM)
        k = k.reshape(b, s, N_HEADS_2, HEAD_DIM)
        v = v.reshape(b, s, N_HEADS_2, HEAD_DIM)
        att = stick_breaking_attention(q, k, v).reshape(b, s, ATT_DIM)
        att_out = jnp.einsum('bsc,cd->bsd', att, w_att_branch)

        merged = jax.nn.sigmoid(g_conv) * conv_out + jax.nn.sigmoid(g_att) * att_out
        mix = jnp.einsum('bsd,de->bse', merged, w_out)
        x = x + rmsnorm(mix, norm_mix_post)

        h = rmsnorm(x, norm_ffn_pre)
        gu = jnp.einsum('bsd,df->bsf', h, w_ffn_up)
        gate, up = jnp.split(gu, 2, axis=-1)
        ff = jnp.einsum('bsf,fd->bsd', jax.nn.silu(gate) * up, w_ffn_down)
        x = x + rmsnorm(ff, norm_ffn_post)
    return x


def setup_inputs(seed=0):
    out = dict(first_inputs(seed))
    for name, value in second_inputs(seed + 1).items():
        if name != "x":
            out[name + "_2"] = value
    return out


def reference(
    x, a_norm, a_mu, a_w_in, a_w0, a_w1, a_w2, a_a0, a_a1, a_a2, a_kk, a_ka, a_rk, a_lnw, a_lnb,
    a_w_out, a_v0, a_v1, a_v2, b_norm, b_w_in, b_conv, b_w_out, final_norm, norm_mix_pre_2,
    w_in_2, conv_dw_w_2, conv_dw_b_2, conv_ln_g_2, conv_ln_b_2, w_conv_branch_2,
    b_conv_branch_2, w_att_branch_2, w_out_2, norm_mix_post_2, norm_ffn_pre_2, w_ffn_up_2,
    w_ffn_down_2, norm_ffn_post_2,
):
    x = first_block(
        x, a_norm, a_mu, a_w_in, a_w0, a_w1, a_w2, a_a0, a_a1, a_a2, a_kk, a_ka, a_rk, a_lnw,
        a_lnb, a_w_out, a_v0, a_v1, a_v2, b_norm, b_w_in, b_conv, b_w_out, final_norm,
    )
    return second_block(
        x, norm_mix_pre_2, w_in_2, conv_dw_w_2, conv_dw_b_2, conv_ln_g_2, conv_ln_b_2,
        w_conv_branch_2, b_conv_branch_2, w_att_branch_2, w_out_2, norm_mix_post_2,
        norm_ffn_pre_2, w_ffn_up_2, w_ffn_down_2, norm_ffn_post_2,
    )


_drawn_inputs = setup_inputs


def setup_inputs(seed=0):
    import zlib

    import numpy as np

    out = dict(_drawn_inputs(seed))
    spreads = {}
    factors = {'a_w1': 3.381,
     'a_w2': 3.38,
     'a_lnw': 3.843,
     'a_lnb': 3.817,
     'conv_ln_b_2': 5.103,
     'b_conv_branch_2': 2.964,
     'b_norm': 3.903}
    for name, (base, spread) in spreads.items():
        noise = np.random.default_rng([zlib.crc32(name.encode()), seed]).standard_normal(out[name].shape)
        drawn = base * np.exp(spread * noise) if base else spread * noise
        out[name] = __import__('jax').numpy.asarray(drawn.astype(out[name].dtype))
    for name, factor in factors.items():
        out[name] = (out[name] * factor).astype(out[name].dtype)
    return out
```

```python
from contextlib import ExitStack

import concourse.bass as bass
from concourse import mybir

F32 = mybir.dt.float32
F32R = mybir.dt.float32r
F16 = mybir.dt.float16
ALU = mybir.AluOpType
ACT = mybir.ActivationFunctionType

P = 128
T = 512
D = 1024
DK = D // P
DI = 2048
CI = DI // P
LORA = 64
C = 64
NCH = T // C
W1 = C + 1
EDECAY = 0.6065306597126334
CLAMP = -43.0
LN2 = 0.6931471805599453
EXP_LN_SET = 6
NSHIFT = 30
RMS_EPS = 1e-6
GN_EPS = 64e-5
LN_EPS = 1e-6
AD = 512
AT = AD // P
NHEAD2 = 8
CT = 4
TAPS2 = 31
PAD2 = TAPS2 - 1
FT = 22
NT = T // P
ATT_AT = [sum(T - P * m for m in range(n)) for n in range(NT + 1)]
ATT_COLS = ATT_AT[NT]
KB = 8

PARAMS = [
    [("a_norm", 8), ("a_mu", 48), ("a_w0", 16), ("a_a0", 16), ("a_kk", 16), ("a_ka", 16)],
    [("a_rk", 16), ("a_lnw", 16), ("a_lnb", 16), ("b_norm", 8), ("b_conv", 48), ("final_norm", 8)],
    [("norm_mix_pre_2", 8), ("conv_dw_b_2", 4), ("conv_ln_g_2", 4), ("conv_ln_b_2", 4), ("b_conv_branch_2", 8),
     ("norm_mix_post_2", 8), ("norm_ffn_pre_2", 8), ("norm_ffn_post_2", 8)],
    [("conv_dw_w_2", 124)],
]
PAR_ROWS = [sum(n for _, n in rows) for rows in PARAMS]
PAR_AT = {name: (t, sum(n for _, n in rows[:i])) for t, rows in enumerate(PARAMS) for i, (name, _) in enumerate(rows)}

U_LORA1 = 0
U_GATE = U_LORA1 + 2
U_MIX = U_GATE + CI
U_OUT1 = U_MIX + 4 * CI
U_CONV = U_OUT1 + 2 * DK
U_GLU = U_CONV + 2 * (4 * 8 + DK)
U_QKV = U_GLU + 2 * CT
U_GATES2 = U_QKV + 3 * AT
U_MERGE = U_GATES2 + 2 * DK
U_WOUT2 = U_MERGE + DK
U_FFN = U_WOUT2 + DK
FPARTS = [(0, 8), (8, 8), (16, 6)]
U_END = U_FFN + sum(2 * n + DK for _, n in FPARTS)

X_LORA = 0
X_G = X_LORA + 2 * DK
X_RKV = X_G + DK
X_Y = X_RKV + 3 * DK
X_H2 = X_Y + CI
X_YC = X_H2 + DK
X_H3 = X_YC + CI
X_UC = X_H3 + DK
X_AT = X_UC + CT
X_MG = X_AT + AT
X_H4 = X_MG + DK
X_FF = X_H4 + DK


def made(q):
    if not isinstance(q, int) or q < X_Y:
        return q + 1
    if X_YC <= q < X_H3 or q < X_H2:
        return None
    return q + 1 - CI - (CI if q >= X_H3 else 0)


def panel_dmas(n):
    lora2 = U_MIX <= n < U_OUT1 and (n - U_MIX) % 4 == 0
    return 2 if lora2 or U_MERGE <= n < U_WOUT2 else 1


def panels_by(n):
    return 16 * sum(panel_dmas(m) for m in range(n % 2, n + 1, 2))


class Order:

    def __init__(self, eng, sem):
        self.eng, self.sem, self.base, self.k, self.i, self.per = eng, sem, 0, 0, None, 0

    def __call__(self, ins):
        ins.then_inc(self.sem, 1)
        self.k += 1
        n = self.base + self.k
        self.eng.wait_ge(self.sem, n if self.i is None else self.i * self.per + n)

    def enter(self, i, per):
        self.base, self.k, self.i, self.per = self.base + self.k, 0, i, per

    def leave(self, turns):
        assert self.k == self.per, (self.k, self.per)
        self.base, self.k, self.i = self.base + turns * self.per, 0, None


def program(nc, i, out):
    with ExitStack() as ctx:
        at = [16512]

        def place(name, shape, dt, where=None):
            size = 4 if dt in (F32, F32R) else 2
            for n in shape[1:]:
                size *= n
            size = (size + 31) // 32 * 32
            if where is None:
                where = at[0]
                at[0] += size
            return nc.alloc_sbuf_tensor_at(name, shape, dt, offset=where), where, where + size

        def sem(name):
            return ctx.enter_context(nc.semaphore(name))

        def dram(name, shape):
            return nc.dram_tensor(name, shape, F32, kind="Internal").ap()

        ident, _, _ = place("ident", [P, P], F32)
        mean_d, _, _ = place("mean_d", [P, P], F32)
        head_ones, _, _ = place("head_ones", [P, P], F32)
        head_rk, _, _ = place("head_rk", [P, P], F32)
        masks, _, _ = place("masks", [P, P + C], F32)
        par, _, _ = place("par", [P, 4, P], F32)
        neg_ka, _, _ = place("neg_ka", [P, CI], F32)
        eps, _, _ = place("eps", [P, 4], F32)
        w_raw, _, _ = place("w_raw", [P, 2, KB, P], F32)
        w_hi, _, _ = place("w_hi", [P, 2, KB, P], F32R)
        w_lo, _, _ = place("w_lo", [P, 2, KB, P], F32R)
        tmp, _, _ = place("tmp", [P, 2, T], F32)
        sq, _, _ = place("sq", [P, 2, T], F32)
        acc, _, _ = place("acc", [P, T], F32)
        rstd, _, _ = place("rstd", [P, 2, T], F32)
        att_from, _, _ = place("att_from", [P, P], F32)
        att_ones, _, _ = place("att_ones", [P, P], F32)
        att_keep, _, _ = place("att_keep", [P, P], F32)
        att_drop, _, _ = place("att_drop", [P, P], F32)
        xT, x_at, _ = place("xT", [P, DK, T], F32)
        xh, xh_at, _ = place("xh", [P, 2, DK, T], F32R)
        big_at = at[0]
        xl = [place(f"xl{n}", [P, 2, DK, T], F32R)[0] for n in range(3)]
        free_at = at[0]
        hT, hT_at, hT_end = place("hT", [P, DK, T + 1], F32)
        assert at[0] <= nc.sbuf_usable_end, (at[0], nc.sbuf_usable_end)
        x_raw, _, _ = place("x_raw", [P, 4, D], F32, big_at + 2 * 32768)
        par_raw, _, _ = place("par_raw", [P, 4, P], F32, big_at + 2 * 32768 + 16384)
        lora, lora_at, lora_end = place("lora", [LORA, 2, 2, T], F32R, x_at)
        spot = xh_at

        def over(name, shape, dt=F32):
            nonlocal spot
            t, a, spot = place(name, shape, dt, spot)
            return t

        zw, za = over("zw", [P, T]), over("za", [P, T])
        kk, kn, rn = over("kk", [P, T]), over("kn", [P, T]), over("rn", [P, T])
        kp, kka, rk = over("kp", [P, T]), over("kka", [P, T]), over("rk", [P, T])
        n2, sqk = over("n2", [P, T]), over("sqk", [P, T])
        o_r, o_v, o_bv = over("o_r", [P, T]), over("o_v", [P, T]), over("o_bv", [P, T])
        o_q, o_pc = over("o_q", [P, T]), over("o_pc", [P, NCH])
        assert spot <= xh_at + 32768
        spot = hT_at
        lw, cs = over("lw", [P, NCH, W1]), over("cs", [P, NCH, W1])
        pw, pinv = over("pw", [P, NCH, W1]), over("pinv", [P, NCH, W1])
        o_b, o_c = over("o_b", [P, T]), over("o_c", [P, T])
        scanm = over("scanm", [P, NCH, W1])
        assert spot <= hT_end

        spot = x_at
        Y = over("Y", [P, CI, T])
        st_q = [over(f"st_q{n}", [P, NCH, 3, C]) for n in range(3)]
        st_bc = [over(f"st_bc{n}", [P, NCH, 2, C]) for n in range(2)]
        st_v = [over(f"st_v{n}", [P, (NCH + 1) * C]) for n in range(2)]
        st_bv = [over(f"st_bv{n}", [P, T]) for n in range(2)]
        st_g = [over(f"st_g{n}", [P, T]) for n in range(2)]
        st_pc = [over(f"st_pc{n}", [P, NCH]) for n in range(3)]
        ra = [over(f"ra{n}", [P, NCH, 2, C]) for n in range(2)]
        bt = [over(f"bt{n}", [P, NCH, P]) for n in range(2)]
        sv = [over(f"sv{n}", [P, NCH, 2, C]) for n in range(2)]
        tt = [over(f"tt{n}", [P, NCH, C]) for n in range(2)]
        nix = over("nix", [P, NCH, C])
        nix16 = over("nix16", [P, NCH, C], F16)
        w16 = over("w16", [P, NCH, C], F16)
        r16 = over("r16", [P, NCH, C], F16)
        q16 = over("q16", [P, NCH, C], F16)
        r32 = over("r32", [P, NCH, C])
        rhs = over("rhs", [P, C])
        y0, yc, ysq, yr, y1, y2 = (over(n, [P, T]) for n in ("y0", "yc", "ysq", "yr", "y1", "y2"))
        bmask = over("bmask", [P, 5, C])
        eyes = over("eyes", [P, NCH, C])
        eyes16 = over("eyes16", [P, NCH, C], F16)
        two16 = over("two16", [P, P], F16)
        one16 = over("one16", [P, P], F16)
        center = over("center", [P, P])
        head_mean = over("head_mean", [P, P])
        assert spot <= nc.sbuf_usable_end, (spot, nc.sbuf_usable_end)

        xT2, _, _ = place("xT2", [P, DK, T], F32, hT_at)
        spot = xh_at
        c_sb, cu, conv3 = over("c_sb", [P, T]), over("cu", [P, 2 + T]), over("conv3", [P, 2, T])
        gate3 = over("gate3", [P, T])
        spot = big_at
        gates = over("gates", [P, 2, DK, T])
        uc = over("uc", [P, 2, CT, T], F32R)
        ah = over("ah", [P, 2, AT, T], F32R)
        vtok = over("vtok", [P, NT, AD])
        tail_at = spot
        glu = over("glu", [P, CT, PAD2 + T])
        dconv = over("dconv", [P, CT, T])
        spot = tail_at
        att_sp, att_a = over("att_sp", [P, 2, ATT_COLS]), over("att_a", [P, 2, ATT_COLS])
        att_zz = over("att_zz", [P, 2, T])
        att_z = [rstd[:, 0, :], rstd[:, 1, :], att_zz[:, 0, :], att_zz[:, 1, :]]
        assert spot <= hT_at, (spot, hT_at)
        spot = x_at
        qT, kT = over("qT", [P, AT, T]), over("kT", [P, AT, T])
        mixed, _, _ = place("mixed", [P, DK, T], F32, x_at)
        ffo, _, _ = place("ffo", [P, DK, T], F32, xh_at)
        staged, _, _ = place("staged", [P, T // P, D], F32, x_at)

        bank = [ctx.enter_context(nc.psum_tensor(f"bank{n}", [P, T], F32)) for n in range(8)]

        d_x = dram("d_x", [P, DK, T])
        d_g = dram("d_g", [CI, P, T])
        d_q, d_r, d_b, d_c, d_v, d_bv = (dram(f"d_{n}", [CI, P, T]) for n in ("q", "r", "b", "c", "v", "bv"))
        d_pc = dram("d_pc", [CI, P, NCH])

        def col(name, j):
            t, row = PAR_AT[name]
            return par[:, t, bass.ds(row + j, 1)]

        s_xin = sem("x_loaded")
        s_par = sem("params_loaded")
        s_const = sem("constants_made")
        s_part = sem("params_transposed")
        s_parok = sem("params_copied")
        s_tr = sem("x_transposed")
        s_xt = sem("xT_copied")
        s_raw = [sem("panel_in_slot0"), sem("panel_in_slot1")]
        s_hi = sem("panel_hi_made")
        s_lo = sem("panel_lo_made")
        s_unit = sem("unit_summed")
        s_free = [sem("unit_bank0_read"), sem("unit_bank1_read")]
        s_sq = sem("squares_made")
        s_sqa = sem("squares_added")
        s_ms = sem("mean_square_summed")
        s_rs = sem("rstd_made")
        s_tmp = sem("activation_made")
        s_xhi = sem("activation_hi_made")
        s_xlo = sem("activation_lo_made")
        s_xsaved = sem("xT_saved")
        s_spill = sem("spilled")
        s_lsig = sem("lora_sigmoid_made")
        s_lhid = sem("lora_hidden_made")
        s_lhi = sem("lora_hidden_hi_made")
        s_lt = sem("lora_hidden_lo_made")
        s_z = sem("gate_arg_made")
        s_sg = sem("gate_sigmoid_made")
        s_zw = sem("decay_arg_made")
        s_sw = sem("decay_sigmoid_made")
        s_sa = sem("rate_sigmoid_made")
        s_kk = sem("kk_made")
        s_sqk = sem("kk_squared")
        s_n2 = sem("kk_norm_summed")
        s_n2m = sem("kk_norm_clamped")
        s_rn = sem("kk_rnorm_made")
        s_cs = sem("log_decay_summed")
        s_pw = sem("decay_powers_made")
        s_rk = sem("bonus_terms_made")
        s_bon = sem("bonus_summed")
        s_fin = sem("tile_finished")
        s_vseq, s_aseq, s_gseq = sem("vector_order"), sem("scalar_order"), sem("gpsimd_order")
        s_back = sem("xT_reloaded")
        s_pad = sem("conv_pads_zeroed")
        s_zc = sem("conv_gate_arg_made")
        s_sc = sem("conv_gate_sigmoid_made")
        s_xn = sem("final_norm_applied")
        s_glu = sem("glu_sigmoid_made")
        s_gate2 = sem("branch_gate_made")
        s_vt = sem("v_turned")
        s_vtok = sem("v_turned_copied")
        s_dc = sem("depthwise_conv_summed")
        s_lnm = sem("layernorm_sum_made")
        s_cen = sem("layernorm_centered")
        s_lsq = sem("layernorm_squared")
        s_lacc = sem("layernorm_squares_added")
        s_lrs = sem("layernorm_rstd_made")
        s_lz = sem("layernorm_silu_arg_made")
        s_ls = sem("layernorm_silu_sigmoid_made")
        s_sc2 = sem("scores_summed")
        s_neg = sem("scores_copied")
        s_log = sem("log_term_made")
        s_sp = sem("softplus_made")
        s_cum = sem("softplus_summed")
        s_dif = sem("log_weights_made")
        s_wt = sem("weights_made")
        s_o = sem("attention_summed")
        s_mg = sem("mixed_added")
        s_ug = sem("ffn_gate_arg_made")
        s_us = sem("ffn_gate_sigmoid_made")
        s_ffn = sem("ffn_added")
        s_yt = sem("output_turned")
        s_yc = [sem("output_copied0"), sem("output_copied1")]
        s_out = sem("output_written")
        R = {n: sem(n) for n in (
            "products_summed", "products_masked", "turned", "turned_copied", "nix_made", "v_summed",
            "v_copied", "r_summed", "r_copied", "q_summed", "q_copied", "r32_made", "e_summed", "e_copied",
            "t_summed", "inverse_made", "rhs_summed", "u_summed", "s_summed", "y_summed", "y_bank_read", "centered",
            "centered_copied", "y_squared", "var_summed", "y_rstd_made", "y_finished")}
        for n in ("state_zeroed", "tiles_loaded", "ends_loaded", "rhs_copied", "u_copied", "s_copied"):
            R[n] = [sem(f"{n}{h}") for h in range(2)]

        block = ctx.enter_context(nc.Block())

        def repeat(eng, turns, body, order=None, per=0):
            with eng.Fori(0, turns) as n:
                if order is not None:
                    order.enter(n, per)
                body(n)
            if order is not None:
                order.leave(turns)

        w_in = i["a_w_in"].rearrange("a s d e -> (a s) d e")
        LOADS = 16 * 10
        SPILL_MIX = 16 + 16 * CI
        SPILL_TILE = 16 * 7
        FREE_MIX = 1 + CI // 2

        def panels(first, units, n, u):
            if isinstance(n, int):
                return panels_by(first + units * n + u)
            step = panels_by(first + units + u - 2 * (u == units)) - panels_by(first + u - 2 * (u == units))
            return n * step + panels_by(first + u)


        def when(turn, last):
            return 0 <= turn < last

        def recurrence_tensor(pe):
            mm, tr = nc.tensor.matmul, nc.tensor.transpose
            rows = [slice(0, C), slice(C, P)]

            def chain(j, b, c, phase):
                if phase == 0:
                    if c == 0:
                        pe.wait_ge(R["inverse_made"], j + 1)
                        pe.wait_ge(R["y_bank_read"], j) if j else None
                    for h in range(2):
                        pe.wait_ge(*((R["s_copied"][h], (NCH - 1) * j + c) if c else (R["state_zeroed"][h], j + 1)))
                    for h in range(2):
                        last = mm(bank[5][rows[h], 0:C], st_q[j % 3][:, c, 2 * h, :], sv[b][:, c, h, :],
                                  start=True, stop=True)
                    last.then_inc(R["rhs_summed"], 1)
                    for h in range(2):
                        mm(bank[7][rows[h], c * C:(c + 1) * C], sv[b][rows[h], c, h, :], st_q[j % 3][rows[h], c, 1, :],
                           start=True, stop=False)
                    for h in range(2):
                        mm(bank[6][rows[h], 0:C], ident[rows[h], rows[h]], sv[b][rows[h], c, h, :],
                           start=True, stop=False)
                elif phase == 1:
                    for h in range(2):
                        pe.wait_ge(R["rhs_copied"][h], NCH * j + c + 1)
                        last = mm(bank[5][rows[h], C:2 * C], tt[b][rows[h], c, :], rhs[rows[h], :],
                                  start=True, stop=True)
                    last.then_inc(R["u_summed"], 1)
                else:
                    for h in range(2):
                        pe.wait_ge(R["u_copied"][h], NCH * j + c + 1)
                        last = mm(bank[6][rows[h], 0:C], bt[b][:, c, rows[h]], sv[b][:, c, h, :],
                                  start=False, stop=True)
                    last.then_inc(R["s_summed"], 1)
                    for h in range(2):
                        last = mm(bank[7][rows[h], c * C:(c + 1) * C], sv[b][:, c, h, :], ra[b][:, c, h, :],
                                  start=False, stop=True)
                    if c == NCH - 1:
                        last.then_inc(R["y_summed"], 1)

            def products(j, b, c):
                if c == 0:
                    pe.wait_ge(R["tiles_loaded"][b], LOADS * (j // 2 + 1))
                    if j:
                        pe.wait_ge(R["inverse_made"], j)
                        pe.wait_ge(R["e_copied"], j)
                        pe.wait_ge(R["q_copied"], 6 * j)
                elif c == 4:
                    pe.wait_ge(R["products_masked"], 2 * j + 1)
                    pe.wait_ge(R["turned_copied"], 2 * j + 1)
                for h in range(2):
                    last = mm(bank[2 + h][:, (c % 4) * P:(c % 4 + 1) * P], st_bc[b][rows[h], c, :, :],
                              st_q[j % 3][rows[h], c, h:h + 2, :], start=True, stop=True)
                if c % 4 == 3:
                    last.then_inc(R["products_summed"], 1)
                tr(bank[0][:, (c % 4) * P:(c % 4 + 1) * P], st_bc[b][:, c, :, :], ident[:])
                last = tr(bank[1][:, (c % 4) * P:(c % 4 + 1) * P], st_v[b][:, c * C:(c + 2) * C], ident[:])
                if c % 4 == 3:
                    last.then_inc(R["turned"], 1)

            def each(bk, lhsT, rhs_, start=True, stop=True):
                for c in range(NCH):
                    for h in range(2):
                        last = mm(bank[bk][rows[h], c * C:(c + 1) * C], lhsT[rows[h], c, :], rhs_[rows[h], c, :],
                                  start=start, stop=stop, skip_group_check=True)
                return last

            def first_inverse(j):
                pe.wait_ge(R["q_copied"], 6 * j + 1)
                pe.wait_ge(R["turned_copied"], 2 * j + 2)
                each(1, q16, eyes16).then_inc(R["r_summed"], 1)

            def newton_v(j, level):
                pe.wait_ge(R["r_copied"], 6 * j + level)
                pe.wait_ge(R["q_copied"], 6 * j + level)
                if level == 1:
                    pe.wait_ge(R["nix_made"], j + 1)
                mm(bank[0][:], two16[:], eyes16[:].rearrange("p c t -> p (c t)"), start=True, stop=False,
                   skip_group_check=True)
                each(0, nix16, r16, start=False).then_inc(R["v_summed"], 1)

            def newton_r(j, level):
                pe.wait_ge(R["v_copied"], 5 * j + level)
                each(1, q16, w16).then_inc(R["r_summed"], 1)
                each(2, w16, q16).then_inc(R["q_summed"], 1)

            def residual(j):
                pe.wait_ge(R["r32_made"], j + 1)
                pe.wait_ge(R["q_copied"], 6 * j + 6)
                mm(bank[0][:], one16[:], eyes16[:].rearrange("p c t -> p (c t)"), start=True, stop=False,
                   skip_group_check=True)
                each(0, nix, r32, start=False).then_inc(R["e_summed"], 1)

            def last_inverse(j):
                pe.wait_ge(R["e_copied"], j + 1)
                for c in range(NCH):
                    for h in range(2):
                        where = bank[1][rows[h], c * C:(c + 1) * C]
                        mm(where, r16[rows[h], c, :], eyes16[rows[h], c, :], start=True, stop=False)
                        last = mm(where, w16[rows[h], c, :], q16[rows[h], c, :], start=False, stop=True)
                last.then_inc(R["t_summed"], 1)

            pe.wait_ge(s_const, 3)
            for j in range(CI + 2):
                for s in range(3 * NCH):
                    if when(j - 1, CI):
                        chain(j - 1, (j - 1) % 2, s // 3, s % 3)
                    if when(j, CI):
                        if s < 4:
                            products(j, j % 2, s)
                        elif 6 <= s < 10:
                            products(j, j % 2, s - 2)
                        elif s == 11:
                            first_inverse(j)
                        elif 12 <= s < 22:
                            (newton_v if s % 2 == 0 else newton_r)(j, (s - 10) // 2)
                        elif s == 22:
                            residual(j)
                        elif s == 23:
                            last_inverse(j)
                    if when(j - 2, CI):
                        if s == 2:
                            pe.wait_ge(R["y_bank_read"], j - 1)
                            mm(bank[4][:], center[:], y0[:], start=True, stop=True).then_inc(R["centered"], 1)
                        if s == 5:
                            pe.wait_ge(R["centered_copied"], j - 1)
                            pe.wait_ge(R["y_squared"], j - 1)
                            mm(bank[4][:], head_mean[:], ysq[:], start=True, stop=True).then_inc(R["var_summed"], 1)

        def recurrence_evac(eng, h, j, b, c, phase):
            hs = slice(h * C, (h + 1) * C)
            scaled = (lambda o_, i_, f: nc.vector.tensor_scalar(o_, i_, f, None, ALU.mult)) if h == 0 else \
                     (lambda o_, i_, f: nc.scalar.activation(o_, i_, ACT.Copy, scale=f))
            if phase == 0:
                eng.wait_ge(R["rhs_summed"], NCH * j + c + 1)
                scaled(rhs[hs, :], bank[5][hs, 0:C], 1.0).then_inc(R["rhs_copied"][h], 1)
            elif phase == 1:
                eng.wait_ge(R["u_summed"], NCH * j + c + 1)
                scaled(sv[b][hs, c, h, :], bank[5][hs, C:2 * C], -1.0).then_inc(R["u_copied"][h], 1)
            elif c < NCH - 1:
                eng.wait_ge(R["s_summed"], NCH * j + c + 1)
                scaled(sv[b][hs, c + 1, h, :], bank[6][hs, 0:C], st_pc[j % 3][hs, c:c + 1]).then_inc(R["s_copied"][h], 1)

        def recurrence_scalar(act, o):
            A = nc.scalar.activation
            act.wait_ge(s_const, 3)
            for j in range(CI + 2):
                b = j % 2
                for s in range(3 * NCH):
                    if when(j - 1, CI):
                        recurrence_evac(act, 1, j - 1, 1 - b, s // 3, s % 3)
                    if when(j, CI):
                        if s in (3, 9):
                            g = s // 6
                            act.wait_ge(R["turned"], 2 * j + g + 1)
                            o(A(bt[b][:, 4 * g:4 * g + 4, :], bank[0][:].rearrange("p (c k) -> p c k", c=4), ACT.Copy))
                            v = bank[1][:].rearrange("p (c k) -> p c k", c=4)
                            o(A(sv[b][0:C, 4 * g:4 * g + 4, 1, :], v[0:C, :, C:P], ACT.Copy))
                            n = 4 - g
                            copy = A(sv[b][C:P, 4 * g + 1:4 * g + 1 + n, 0, :], v[C:P, 0:n, 0:C], ACT.Copy)
                            if g == 1:
                                o(copy)
                                copy = A(sv[b][C:P, 0, 0, :], v[C:P, 3, 0:C], ACT.Copy)
                            copy.then_inc(R["turned_copied"], 1)
                            if g == 1:
                                act.wait_ge(R["turned_copied"], 2 * j + 2)
                                A(sv[b][C:P, 0, 1, :], sv[b][C:P, 0, 0, :], ACT.Copy, scale=0.0).then_inc(
                                    R["state_zeroed"][1], 1)
                        elif s == 11 or (12 <= s < 22 and s % 2 == 1):
                            level = 1 if s == 11 else (s - 9) // 2
                            act.wait_ge(R["r_summed"], 6 * j + level)
                            A(r16[:], bank[1][:].rearrange("p (c k) -> p c k", c=NCH), ACT.Copy).then_inc(
                                R["r_copied"], 1)
                            if level == 6:
                                act.wait_ge(R["r_copied"], 6 * j + 6)
                                A(r32[:], r16[:], ACT.Copy).then_inc(R["r32_made"], 1)
                        elif s == 22:
                            act.wait_ge(R["e_summed"], j + 1)
                            A(w16[:], bank[0][:].rearrange("p (c k) -> p c k", c=NCH), ACT.Copy).then_inc(
                                R["e_copied"], 1)
                    if when(j - 2, CI):
                        if s == 2:
                            act.wait_ge(R["centered_copied"], j - 1)
                            A(ysq[:], yc[:], ACT.Square).then_inc(R["y_squared"], 1)
                        if s == 6:
                            act.wait_ge(R["var_summed"], j - 1)
                            o(A(yr[:], bank[4][:], ACT.Ln, bias=eps[:, 1:2]))
                            A(yr[:], yr[:], ACT.Exp, scale=-0.5).then_inc(R["y_rstd_made"], 1)

        def recurrence_vector(dve, o):
            V = nc.vector
            incl, strict = masks[:, 0:C], masks[:, P:P + C]
            dve.wait_ge(s_const, 3)

            def wide(m, lo, hi, n):
                return m[lo:hi].unsqueeze(1).to_broadcast([hi - lo, n, C])

            for j in range(CI + 2):
                b = j % 2
                for s in range(3 * NCH):
                    if s == 0 and when(j - 2, CI):
                        dve.wait_ge(R["y_summed"], j - 1)
                        V.tensor_copy(y0[:], bank[7][:]).then_inc(R["y_bank_read"], 1)
                    if when(j - 1, CI):
                        recurrence_evac(dve, 0, j - 1, 1 - b, s // 3, s % 3)
                    if when(j, CI):
                        if s in (3, 9):
                            g = s // 6
                            cr = slice(4 * g, 4 * g + 4)
                            dve.wait_ge(R["products_summed"], 2 * j + g + 1)
                            p0, p1 = (bank[2 + h][:].rearrange("p (c a k) -> p c a k", c=4, a=2) for h in range(2))
                            TT = V.tensor_tensor
                            TT(ra[b][:, cr, 0, :], p0[:, :, 1, :], wide(incl, 0, P, 4), ALU.mult)
                            TT(ra[b][:, cr, 1, :], p1[:, :, 0, :], wide(incl, 0, P, 4), ALU.mult)
                            TT(st_q[j % 3][C:P, cr, 0, :], p0[C:P, :, 0, :], wide(strict, C, P, 4), ALU.mult)
                            TT(st_q[j % 3][0:C, cr, 2, :], p1[0:C, :, 1, :], wide(strict, 0, C, 4), ALU.mult)
                            TT(nix[0:C, cr, :], p0[0:C, :, 0, :], wide(strict, 0, C, 4), ALU.mult)
                            TT(nix[C:P, cr, :], p1[C:P, :, 1, :], wide(strict, C, P, 4), ALU.mult).then_inc(
                                R["products_masked"], 1)
                            if g == 1:
                                dve.wait_ge(R["products_masked"], 2 * j + 2)
                                V.memset(sv[b][0:C, 0, 0, :], 0.0).then_inc(R["state_zeroed"][0], 1)
                                o(TT(y1[:].rearrange("p (c k) -> p c k", c=NCH), eyes[:], nix[:], ALU.subtract))
                                TT(q16[:], y1[:].rearrange("p (c k) -> p c k", c=NCH), wide(bmask[:, 0, :], 0, P, NCH),
                                   ALU.mult).then_inc(R["q_copied"], 1)
                                o(V.scalar_tensor_tensor(out=nix[:], in0=nix[:], scalar=-1.0, in1=eyes[:],
                                                         op0=ALU.mult, op1=ALU.subtract))
                                V.tensor_copy(nix16[:], nix[:]).then_inc(R["nix_made"], 1)
                        elif 12 <= s < 22 and s % 2 == 0:
                            level = (s - 10) // 2
                            dve.wait_ge(R["v_summed"], 5 * j + level)
                            src = bank[0][:].rearrange("p (c k) -> p c k", c=NCH)
                            (TT(w16[:], src, wide(bmask[:, level, :], 0, P, NCH), ALU.mult) if level < 5 else
                             V.tensor_copy(w16[:], src)).then_inc(R["v_copied"], 1)
                        elif 12 <= s < 22:
                            level = (s - 11) // 2
                            dve.wait_ge(R["q_summed"], 5 * j + level)
                            V.tensor_copy(q16[:], bank[2][:].rearrange("p (c k) -> p c k", c=NCH)).then_inc(
                                R["q_copied"], 1)
                        elif s == 23:
                            dve.wait_ge(R["t_summed"], j + 1)
                            V.tensor_copy(tt[b][:], bank[1][:].rearrange("p (c k) -> p c k", c=NCH)).then_inc(
                                R["inverse_made"], 1)
                    if when(j - 2, CI):
                        if s == 2:
                            dve.wait_ge(R["centered"], j - 1)
                            V.tensor_copy(yc[:], bank[4][:]).then_inc(R["centered_copied"], 1)
                        if s == 7:
                            dve.wait_ge(R["y_rstd_made"], j - 1)
                            dve.wait_ge(R["ends_loaded"][b], 32 * (j // 2))
                            o(V.tensor_tensor(y2[:], yc[:], yr[:], ALU.mult))
                            o(V.tensor_scalar(y2[:], y2[:], col("a_lnw", j - 2), col("a_lnb", j - 2), ALU.mult, ALU.add))
                            o(V.tensor_tensor(y2[:], y2[:], st_bv[b][:], ALU.add))
                            V.tensor_tensor(Y[:, j - 2, :], y2[:], st_g[b][:], ALU.mult).then_inc(R["y_finished"], 1)

        ITEMS = NHEAD2 * NT

        def item(m):
            h, n = m // NT, NT - 1 - m % NT
            return h, n, slice((h % 2) * C, (h % 2 + 1) * C), slice(n * P, T), slice(ATT_AT[n], ATT_AT[n + 1])

        def attention_tensor(pe):
            mm = nc.tensor.matmul

            def scores(m):
                h, n, rows, seen, _ = item(m)
                if m == 0:
                    pe.wait_ge(s_free[0], U_MERGE // 2)
                    pe.wait_ge(s_free[1], U_MERGE // 2)
                    pe.wait_ge(s_vtok, NT)
                    pe.wait_ge(s_lrs, 1)
                if m >= 4:
                    pe.wait_ge(s_neg, m - 3)
                mm(bank[m % 4][:, seen], kT[rows, h // 2, n * P:(n + 1) * P], qT[rows, h // 2, seen], start=True,
                   stop=True).then_inc(s_sc2, 1)

            def sums(m):
                h, n, _, seen, cols = item(m)
                pe.wait_ge(s_sp, m + 1)
                if m >= 2:
                    pe.wait_ge(s_dif, m - 1)
                last = mm(bank[4 + m % 2][:, seen], att_from[:], att_sp[:, h % 2, cols], start=True, stop=n == NT - 1)
                for later in range(n + 1, NT):
                    last = mm(bank[4 + m % 2][:, later * P:T], att_ones[:],
                              att_sp[:, h % 2, ATT_AT[later]:ATT_AT[later + 1]], start=False, stop=later == NT - 1)
                last.then_inc(s_cum, 1)

            def values(h):
                pe.wait_ge(s_wt, NT * (h + 1))
                if h >= 4:
                    pe.wait_ge(s_tmp, made(X_AT + h // 2 - 2))
                for n in range(NT):
                    last = mm(bank[6 + h // 2 % 2][(h % 2) * C:(h % 2 + 1) * C, n * P:T], vtok[:, n, h * C:(h + 1) * C],
                              att_a[:, h % 2, ATT_AT[n]:ATT_AT[n + 1]], start=n == 0, stop=n == NT - 1)
                last.then_inc(s_o, 1)

            for s in range(-1, ITEMS + 3):
                if when(s + 1, ITEMS):
                    scores(s + 1)
                if when(s - 1, ITEMS):
                    sums(s - 1)
                if when(s - 3, ITEMS) and (s - 3) % NT == NT - 1:
                    values((s - 3) // NT)

        def attention_scalar(act, o, x_high):
            A = nc.scalar.activation
            for s in range(ITEMS + 5):
                if when(s, ITEMS):
                    seen = item(s)[3]
                    z, t = att_z[s % 4][:, seen], sq[:, s % 2, seen]
                    act.wait_ge(s_sc2, s + 1)
                    if s >= 4:
                        act.wait_ge(s_dif, s - 3)
                    A(z, bank[s % 4][:, seen], ACT.Copy).then_inc(s_neg, 1)
                    act.wait_ge(s_neg, s + 1)
                    if s >= 2:
                        act.wait_ge(s_sp, s - 1)
                    o(A(t, z, ACT.Abs))
                    o(A(t, t, ACT.Exp, scale=-1.0))
                    A(t, t, ACT.Ln, bias=1.0).then_inc(s_log, 1)
                if when(s - 2, ITEMS):
                    h, n, _, seen, cols = item(s - 2)
                    t = att_a[:, h % 2, cols]
                    act.wait_ge(s_dif, s - 1)
                    A(t, t, ACT.Exp).then_inc(s_wt, 1)
                if when(s - 4, ITEMS) and (s - 4) % (2 * NT) == 2 * NT - 1:
                    pair = (s - 4) // (2 * NT)
                    x_high(X_AT + pair, ah[:, 0, pair, :], pair % 2)

        def attention_vector(dve, o, finish):
            V = nc.vector
            for s in range(ITEMS + 5):
                if when(s - 1, ITEMS):
                    m = s - 1
                    h, n, rows, seen, cols = item(m)
                    dve.wait_ge(s_log, m + 1)
                    o(V.scalar_tensor_tensor(out=att_sp[:, h % 2, cols], in0=att_z[m % 4][:, seen], scalar=0.0,
                                             in1=sq[:, m % 2, seen], op0=ALU.max, op1=ALU.add))
                    t = att_sp[:, h % 2, ATT_AT[n]:ATT_AT[n] + P]
                    V.tensor_tensor(t, t, att_keep[:], ALU.mult).then_inc(s_sp, 1)
                if when(s - 2, ITEMS):
                    m = s - 2
                    h, n, rows, seen, cols = item(m)
                    dve.wait_ge(s_cum, m + 1)
                    if m % NT == 0 and h >= 2:
                        dve.wait_ge(s_o, h - 1)
                    o(V.tensor_tensor(att_a[:, h % 2, cols], att_z[m % 4][:, seen], bank[4 + m % 2][:, seen],
                                      ALU.subtract))
                    t = att_a[:, h % 2, ATT_AT[n]:ATT_AT[n] + P]
                    V.scalar_tensor_tensor(out=t, in0=t, scalar=0.0, in1=att_drop[:], op0=ALU.min,
                                           op1=ALU.add).then_inc(s_dif, 1)
                if when(s - 4, ITEMS) and (s - 4) % (2 * NT) == 2 * NT - 1:
                    pair = (s - 4) // (2 * NT)
                    dve.wait_ge(s_o, 2 * pair + 2)
                    finish(pair, lambda where: V.tensor_copy(where, bank[6 + pair % 2][:]))

        def tail_sync(sp, panel):
            sp.wait_ge(R["y_finished"], CI)
            sp.dma_start(xT2[:], d_x).then_inc(s_back, 16)
            w_out1, w_conv, w_out_conv = i["a_w_out"][0], i["b_w_in"][0], i["b_w_out"][0]

            def even(base, turns, mat, row, nkb, col0, first=0):
                def turn(t):
                    for u in range(2):
                        panel(2 * t + (base + u + 2 * first), u, mat, row, nkb, t * (2 * P) + (col0 + (u + 2 * first) * P))
                repeat(sp, turns - first, turn)

            def pairs(base, turns, mat, nkb, col_a, col_b):
                def turn(t):
                    for u, c0 in enumerate((col_a, col_b)):
                        panel(2 * t + (base + u), u, mat, 0, nkb, t * P + c0)
                repeat(sp, turns, turn)

            even(U_OUT1, DK // 2, w_out1, 0, KB, 0, first=1)
            even(U_OUT1 + DK, DK // 2, w_out1, D, KB, 0)
            for half in range(2):
                base = U_CONV + half * (4 * KB + DK)

                def conv(t):
                    for u, part in enumerate((0, 2, 3, 1)):
                        panel(4 * t + (base + u), u % 2, w_conv, 0, KB, t * P + (part * DI + half * D))
                repeat(sp, KB, conv)
                even(base + 4 * KB, DK // 2, w_out_conv, half * D, KB, 0)
            w2 = i["w_in_2"]
            pairs(U_GLU, CT, w2, KB, 0, CT * P)
            even(U_QKV, 3 * AT // 2, w2, 0, KB, 2 * CT * P)
            gate_col = 2 * CT * P + 3 * AD
            pairs(U_GATES2, DK, w2, KB, gate_col, gate_col + D)

            def merge(t):
                for u in range(2):
                    n, c0 = 2 * t + (U_MERGE + u), t * (2 * P) + u * P
                    panel(n, u, i["w_conv_branch_2"], 0, CT, c0)
                    panel(n, u, i["w_att_branch_2"], 0, AT, c0, kb0=CT, first=False)
            repeat(sp, DK // 2, merge)
            even(U_WOUT2, DK // 2, i["w_out_2"], 0, KB, 0)
            base = U_FFN
            for j0, n in FPARTS:
                pairs(base, n, i["w_ffn_up_2"], KB, j0 * P, (FT + j0) * P)
                even(base + 2 * n, DK // 2, i["w_ffn_down_2"], j0 * P, n, 0)
                base += 2 * n + DK
            for q in range(NT):
                for half in range(2):
                    sp.wait_ge(s_yc[half], q + 1)
                sp.dma_start(out[0, q * P:(q + 1) * P, :], staged[:, q, :]).then_inc(s_out, 16)
            sp.wait_ge(s_out, 16 * NT)

        @block.sync
        def _(sp):
            def panel(n, slot, mat, row, nkb, col, ncol=P, kb0=0, first=True, rows=P):
                if first and not (isinstance(n, int) and n < 2):
                    sp.wait_ge(s_lo, n - 1)
                src = mat[row:row + nkb * rows, bass.ds(col, ncol)].rearrange("(k p) c -> p k c", p=rows)
                sp.dma_start(w_raw[0:rows, slot, kb0:kb0 + nkb, 0:ncol], src).then_inc(s_raw[slot], 16)

            sp.dma_start(x_raw[:], i["x"].rearrange("b (q p) d -> p (b q) d", p=P)).then_inc(s_xin, 16)
            panel(0, 0, i["a_w1"][0], 0, KB, 0, LORA)
            panel(1, 1, i["a_a1"][0], 0, KB, 0, LORA)

            def gate(t, u):
                panel(2 * t + (U_GATE + u), u, w_in[3], 0, KB, t * (2 * P) + u * P)

            def spill_gate(t, u):
                sp.wait_ge(s_free[u], t + 2)
                sp.dma_start(d_g[2 * t + u], sq[:, u, :]).then_inc(s_spill, 16)

            def mix(j, u):
                if u == 0:
                    panel(4 * j + U_MIX, 0, i["a_w2"][0], 0, 1, j * P, rows=LORA)
                    panel(4 * j + U_MIX, 0, i["a_a2"][0], 0, 1, j * P, kb0=1, first=False, rows=LORA)
                else:
                    panel(4 * j + (U_MIX + u), u % 2, w_in[(None, 1, 0, 2)[u]], 0, KB, j * P)

            def spill_mix(j):
                sp.wait_ge(s_free[0], 2 * j + (FREE_MIX + 2))
                sp.dma_start(d_r[j], o_r[:]).then_inc(s_spill, 16)
                sp.dma_start(d_pc[j], o_pc[:]).then_inc(s_spill, 16)
                for n, (dst, src) in enumerate(((d_q, o_q), (d_b, o_b), (d_c, o_c))):
                    sp.wait_ge(s_fin, 4 * j + (n + 1))
                    sp.dma_start(dst[j], src[:]).then_inc(s_spill, 16)
                sp.wait_ge(s_free[1], 2 * j + (FREE_MIX + 2))
                sp.dma_start(d_v[j], o_v[:]).then_inc(s_spill, 16)
                sp.wait_ge(s_fin, 4 * j + 4)
                sp.dma_start(d_bv[j], o_bv[:]).then_inc(s_spill, 16)

            sp.wait_ge(s_xt, DK)
            sp.dma_start(d_x, xT[:]).then_inc(s_spill, 16)
            for u in range(4):
                gate(u // 2, u % 2)

            def gate_turn(t):
                for u in range(2):
                    spill_gate(t, u)
                    gate(t + 2, u)
            repeat(sp, CI // 2 - 2, gate_turn)
            for u in range(4):
                spill_gate(CI // 2 - 2 + u // 2, u % 2)
                mix(0, u)

            def mix_turn(j):
                for u in range(4):
                    if u == 3:
                        spill_mix(j)
                    mix(j + 1, u)
            repeat(sp, CI - 1, mix_turn)
            panel(U_OUT1, 0, i["a_w_out"][0], 0, KB, 0)
            spill_mix(CI - 1)
            panel(U_OUT1 + 1, 1, i["a_w_out"][0], 0, KB, P)

            def load(j):
                b, b3 = j % 2, j % 3
                if j >= 2:
                    sp.wait_ge(R["turned"], 2 * (j - 1))
                if j >= 3:
                    sp.wait_ge(R["y_summed"], j - 2)
                half = lambda a, h: a[j, h * C:(h + 1) * C, :].rearrange("p (c t) -> p c t", c=NCH)
                for h, (slot_b, slot_c) in enumerate(((0, 1), (1, 0))):
                    hs = slice(h * C, (h + 1) * C)
                    for dst, src in ((st_q[b3][hs, :, 2 * h, :], d_q), (st_bc[b][hs, :, slot_b, :], d_b),
                                     (st_bc[b][hs, :, slot_c, :], d_c)):
                        sp.dma_start(dst, half(src, h)).then_inc(R["tiles_loaded"][b], 16)
                whole = d_r[j].rearrange("p (c t) -> p c t", c=NCH)
                for dst, src in ((st_q[b3][:, :, 1, :], whole), (st_v[b][:, 0:T], d_v[j]),
                                 (st_v[b][:, T:T + C], d_v[j, :, 0:C]), (st_pc[b3][:], d_pc[j])):
                    sp.dma_start(dst, src).then_inc(R["tiles_loaded"][b], 16)

            sp.wait_ge(s_spill, SPILL_MIX + SPILL_TILE * CI)
            sp.wait_ge(s_unit, U_OUT1)
            load(0)
            load(1)
            for j in range(CI):
                if j >= 2:
                    sp.wait_ge(R["y_finished"], j - 1)
                sp.dma_start(st_bv[j % 2][:], d_bv[j]).then_inc(R["ends_loaded"][j % 2], 16)
                sp.dma_start(st_g[j % 2][:], d_g[j]).then_inc(R["ends_loaded"][j % 2], 16)
                if j + 2 < CI:
                    load(j + 2)
            tail_sync(sp, panel)

        @block.gpsimd
        def _(gp):
            o = Order(gp, s_gseq)
            gt = nc.gpsimd
            o(gt.memset(ident[:], 0.0))
            o(gt.affine_select(out=ident[:], in_=ident[:], compare_op=ALU.not_equal, fill=1.0, base=0,
                               pattern=[[-1, P]], channel_multiplier=1))
            o(gt.memset(mean_d[:], 1.0 / D))
            o(gt.memset(head_ones[:], 0.0))
            o(gt.memset(head_ones[0:C, 0:C], 1.0))
            o(gt.memset(head_ones[C:P, C:P], 1.0))
            o(gt.memset(eps[:, 0:1], RMS_EPS))
            o(gt.memset(eps[:, 1:2], GN_EPS))
            o(gt.memset(eps[:, 2:3], 0.5 * NSHIFT * LN2))
            o(gt.memset(masks[:], 1.0))
            for m in (att_ones, att_from, att_keep, att_drop):
                o(gt.memset(m[:], 0.0 if m is att_drop else 1.0))
            o(gt.affine_select(out=att_from[:], in_=att_from[:], compare_op=ALU.is_ge, fill=0.0, base=0,
                               pattern=[[-1, P]], channel_multiplier=1))
            o(gt.affine_select(out=att_keep[:], in_=att_keep[:], compare_op=ALU.is_gt, fill=0.0, base=0,
                               pattern=[[1, P]], channel_multiplier=-1))
            o(gt.affine_select(out=att_drop[:], in_=att_drop[:], compare_op=ALU.is_gt, fill=-1e30, base=0,
                               pattern=[[1, P]], channel_multiplier=-1))
            for h in range(2):
                hs = slice(h * C, (h + 1) * C)
                incl = masks[hs, 0:P].rearrange("p (a t) -> p a t", a=2)
                o(gt.affine_select(out=incl, in_=incl, compare_op=ALU.is_ge, fill=0.0, base=0,
                                   pattern=[[0, 2], [1, C]], channel_multiplier=-1))
                o(gt.affine_select(out=masks[hs, P:P + C], in_=masks[hs, P:P + C], compare_op=ALU.is_gt,
                                   fill=0.0, base=0, pattern=[[1, C]], channel_multiplier=-1))
            gt.memset(hT[:, :, 0:1], 0.0).then_inc(s_const, 1)
            gp.wait_ge(s_xlo, X_Y)
            o(gt.memset(scanm[:], 1.0))
            o(gt.memset(scanm[:, :, 0:1], 0.0))
            gt.memset(lw[:, :, 0:1], 0.0).then_inc(s_const, 1)

            gp.wait_ge(s_unit, U_OUT1)
            gp.wait_ge(s_spill, SPILL_MIX + SPILL_TILE * CI)
            o(gt.memset(bmask[:], 1.0))
            for n, m in enumerate((2, 4, 8, 16, 32)):
                for h in range(2):
                    v = bmask[h * C:(h + 1) * C, n, :].rearrange("p (a b) -> p a b", b=m)
                    o(gt.affine_select(out=v, in_=v, compare_op=ALU.is_ge, fill=0.0, base=0,
                                       pattern=[[-m, C // m], [0, m]], channel_multiplier=1))
                    o(gt.affine_select(out=v, in_=v, compare_op=ALU.is_ge, fill=0.0, base=m - 1,
                                       pattern=[[m, C // m], [0, m]], channel_multiplier=-1))
            o(gt.memset(eyes[:], 0.0))
            for h in range(2):
                v = eyes[h * C:(h + 1) * C]
                o(gt.affine_select(out=v, in_=v, compare_op=ALU.not_equal, fill=1.0, base=0,
                                   pattern=[[0, NCH], [-1, C]], channel_multiplier=1))
            o(gt.tensor_copy(eyes16[:], eyes[:]))
            o(gt.tensor_copy(one16[:], ident[:]))
            o(gt.tensor_scalar(two16[:], ident[:], 2.0, 0.0, ALU.mult, ALU.add))
            o(gt.tensor_scalar(head_mean[:], head_ones[:], 1.0 / C, 0.0, ALU.mult, ALU.add))
            gt.tensor_tensor(center[:], ident[:], head_mean[:], ALU.subtract).then_inc(s_const, 1)

        @block.scalar
        def _(act):
            o = Order(act, s_aseq)
            A = nc.scalar.activation
            nc.scalar.add_instruction(mybir.InstLoadActFuncSet(
                name=nc.get_next_instruction_name(), act_func_set_id=EXP_LN_SET, ins=[], outs=[]))
            for t, rows in enumerate(PARAMS):
                row = 0
                for name, n in rows:
                    src = i[name]
                    letters = " ".join("abcd"[:len(src.shape)])
                    flat = src.rearrange(f"{letters} -> ({letters})") if len(src.shape) > 1 else src
                    act.dma_start(par_raw[row:row + n, t, :], flat.rearrange("(r c) -> r c", c=P)).then_inc(s_par, 16)
                    row += n

            def w_high(n, slot, count, ncol=P):
                act.wait_ge(s_raw[slot], count)
                if not (isinstance(n, int) and n < 2):
                    act.wait_ge(s_unit, n - 1)
                A(w_hi[:, slot, :, 0:ncol], w_raw[:, slot, :, 0:ncol], ACT.Copy).then_inc(s_hi, 1)

            def x_high(q, hi, buf):
                act.wait_ge(s_tmp, made(q))
                A(hi, tmp[:, buf, :], ACT.Copy).then_inc(s_xhi, 1)

            def sigmoid(z):
                o(A(z, z, ACT.Exp, scale=-1.0))
                o(A(z, z, ACT.Ln, bias=1.0))
                return A(z, z, ACT.Exp, scale=-1.0)

            def norm(n, x=xT, ready=None):
                for k in range(DK):
                    if ready is not None:
                        act.wait_ge(*ready(k))
                    if n or k >= 2:
                        act.wait_ge(s_sqa, n * DK + k - 1)
                    A(sq[:, k % 2, :], x[:, k, :], ACT.Square).then_inc(s_sq, 1)
                act.wait_ge(s_ms, n + 1)
                o(A(rstd[:, 0, :], bank[4][:], ACT.Ln, bias=eps[:, 0:1]))
                A(rstd[:, 1, :], rstd[:, 0, :], ACT.Exp, scale=-0.5).then_inc(s_rs, 1)

            for k in range(DK):
                act.wait_ge(s_tr, k + 1)
                A(xT[:, k, :], bank[k % 4][:], ACT.Copy).then_inc(s_xt, 1)
            act.wait_ge(s_const, 1)
            act.wait_ge(s_xt, DK)
            norm(0)
            w_high(0, 0, panels_by(0), LORA)
            w_high(1, 1, panels_by(1), LORA)
            for k in range(DK):
                x_high(2 * k, xl[0][:, 0, k, :], 0)
                x_high(2 * k + 1, xl[1][:, 0, k, :], 1)
            for k in range(DK):
                x_high(X_G + k, xh[:, 0, k, :], k % 2)
            act.wait_ge(s_free[0], 1)
            z = rstd[0:LORA, 0, :]
            o(A(z, z, ACT.Exp, scale=-2.0))
            o(A(z, z, ACT.Ln, bias=1.0))
            A(z, z, ACT.Exp, scale=-1.0).then_inc(s_lsig, 1)
            w_high(U_GATE, 0, panels_by(U_GATE))
            act.wait_ge(s_spill, 16)
            act.wait_ge(s_lhid, 1)
            A(lora[:, 0, 0, :], rstd[0:LORA, 0, :], ACT.Copy).then_inc(s_lhi, 1)
            act.wait_ge(s_free[1], 1)
            A(lora[:, 1, 0, :], rstd[0:LORA, 1, :], ACT.Copy).then_inc(s_lhi, 1)

            def gate(t):
                for u in range(2):
                    w_high(2 * t + (U_GATE + u + 1), 1 - u, panels(U_GATE, 2, t, u + 1))
                    act.wait_ge(s_z, 2 * t + (u + 1))
                    sigmoid(rstd[:, u, :]).then_inc(s_sg, 1)
                    for n in (range(2) if u == 0 else range(2, 3)):
                        x_high(3 * t + (X_RKV + n), xl[n][:, 0, bass.ds(t, 1), :], n % 2)
            repeat(act, CI // 2 - 1, gate, o, 4)
            gate(CI // 2 - 1)

            def mix(j):
                n0 = 4 * j + U_MIX
                w_high(n0 + 1, 1, panels(U_MIX, 4, j, 1))
                act.wait_ge(s_zw, j + 1)
                sigmoid(zw[:]).then_inc(s_sw, 1)
                act.wait_ge(s_free[0], 2 * j + (FREE_MIX + 1))
                sigmoid(za[:]).then_inc(s_sa, 1)
                w_high(n0 + 2, 0, panels(U_MIX, 4, j, 2))
                act.wait_ge(s_kk, j + 1)
                A(sqk[:], kk[:], ACT.Square).then_inc(s_sqk, 1)
                act.wait_ge(s_cs, j + 1)
                act.wait_ge(s_spill, j * SPILL_TILE + SPILL_MIX)
                o(A(pw[:], cs[:], ACT.Exp))
                A(o_pc[:], cs[:, :, C], ACT.Exp)
                A(pinv[:], cs[:], ACT.Exp, scale=-1.0).then_inc(s_pw, 1)
                w_high(n0 + 3, 1, panels(U_MIX, 4, j, 3))
                act.wait_ge(s_n2m, j + 1)
                o(A(n2[:], n2[:], ACT.Ln, scale=float(2 ** NSHIFT)))
                A(rn[:], n2[:], ACT.Exp, scale=-0.5, bias=eps[:, 2:3]).then_inc(s_rn, 1)
                w_high(n0 + 4, 0, panels(U_MIX, 4, j, 4))
                act.wait_ge(s_unit, n0 + 4)
                A(o_v[:], bank[1][:], ACT.Copy).then_inc(s_free[1], 1)
            repeat(act, CI - 1, mix, o, 6)
            mix(CI - 1)
            recurrence_scalar(act, o)

            act.wait_ge(R["y_finished"], CI)
            for k in range(CI):
                A(xl[k // DK][:, 0, k % DK, :], Y[:, k, :], ACT.Copy).then_inc(s_xhi, 1)

            def ahead(base, per, t, u, last=False):
                n = panels(base, per, t, u + 1) if not last else panels_by(base + per * t + u + 1)
                w_high(per * t + (base + u + 1), (u + 1) % 2, n)

            def even(base, turns, final=False):
                def turn(t):
                    ahead(base, 2, t, 0)
                    ahead(base, 2, t, 1)
                repeat(act, turns - final, turn)
                if final:
                    ahead(base, 2, turns - 1, 0)
            even(U_OUT1, DK)

            def all_read(base):
                act.wait_ge(s_free[0], base // 2)
                act.wait_ge(s_free[1], base // 2)

            all_read(U_CONV)
            norm(1, xT2)
            for k in range(DK):
                x_high(X_H2 + k, xl[2][:, 0, k, :], k % 2)
            for half in range(2):
                base = U_CONV + half * (4 * KB + DK)

                def conv(t):
                    for u in range(4):
                        ahead(base, 4, t, u)
                        if u == 2:
                            act.wait_ge(s_zc, t + (KB * half + 1))
                            sigmoid(gate3[:]).then_inc(s_sc, 1)
                    act.wait_ge(s_free[1], 2 * t + (base // 2 + 2))
                    A(xl[half][:, 0, bass.ds(t, 1), :], tmp[:, 0, :], ACT.Copy).then_inc(s_xhi, 1)
                repeat(act, KB, conv, o, 2)
                even(base + 4 * KB, DK // 2)

            all_read(U_GLU)
            norm(2, xT2)
            norm(3, xT2, lambda k: (s_xn, k + 1))
            for k in range(DK):
                x_high(X_H3 + k, xh[:, 0, k, :], k % 2)
            for j in range(CT):
                ahead(U_GLU, 2, j, 0)
                ahead(U_GLU, 2, j, 1)
                act.wait_ge(s_free[1], U_GLU // 2 + j + 1)
                sigmoid(rstd[:, j % 2, :]).then_inc(s_glu, 1)
            for n in range(3 * AT):
                ahead(U_QKV, 2, n // 2, n % 2)
            for q in range(NT):
                act.wait_ge(s_vt, q + 1)
                A(vtok[:, q, :], bank[2 + q][:], ACT.Copy).then_inc(s_vtok, 1)
            for n in range(2 * DK):
                ahead(U_GATES2, 2, n // 2, n % 2, last=True)
                act.wait_ge(s_free[n % 2], U_GATES2 // 2 + n // 2 + 1)
                sigmoid(gates[:, n % 2, n // 2, :]).then_inc(s_gate2, 1)
            for j in range(CT):
                act.wait_ge(s_cen, j + 1)
                if j >= 2:
                    act.wait_ge(s_lacc, j - 1)
                A(sq[:, j % 2, :], dconv[:, j, :], ACT.Square).then_inc(s_lsq, 1)
            act.wait_ge(s_lnm, 2)
            o(A(rstd[:, 0, :], bank[4][:], ACT.Ln, bias=eps[:, 0:1], scale=2.0))
            A(rstd[:, 1, :], rstd[:, 0, :], ACT.Exp, scale=-0.5).then_inc(s_lrs, 1)
            for j in range(CT):
                act.wait_ge(s_lz, j + 1)
                sigmoid(sq[:, j % 2, :]).then_inc(s_ls, 1)
                x_high(X_UC + j, uc[:, 0, j, :], j % 2)
            attention_scalar(act, o, x_high)
            for n in range(DK):
                ahead(U_MERGE, 2, n // 2, n % 2, last=True)
                x_high(X_MG + n, xh[:, 0, n, :], n % 2)
            even(U_WOUT2, DK // 2)
            all_read(U_FFN)
            norm(4, mixed)
            norm(5, xT2, lambda k: (s_mg, k + 1))
            for k in range(DK):
                x_high(X_H4 + k, xl[0][:, 0, k, :], k % 2)
            base = U_FFN
            for part, (j0, n) in enumerate(FPARTS):
                dst = xl[1 + part % 2]

                def ffn(t):
                    ahead(base, 2, t, 0)
                    act.wait_ge(s_ug, t + (j0 + 1))
                    sigmoid(rstd[:, 0, :]).then_inc(s_us, 1)
                    ahead(base, 2, t, 1)
                    act.wait_ge(s_free[1], t + (base // 2 + 1))
                    A(dst[:, 0, bass.ds(t, 1), :], tmp[:, 0, :], ACT.Copy).then_inc(s_xhi, 1)
                repeat(act, n, ffn, o, 2)
                even(base + 2 * n, DK // 2, final=part == len(FPARTS) - 1)
                base += 2 * n + DK
            all_read(U_END)
            norm(6, ffo)
            for k in range(NT):
                act.wait_ge(s_yt, 2 * k + 2)
                A(staged[:, k, T:D], bank[(2 * k + 1) % 8][:], ACT.Copy).then_inc(s_yc[1], 1)

        @block.tensor
        def _(pe):
            mm, tr = nc.tensor.matmul, nc.tensor.transpose

            def three(outp, wh, wl, xhi, xlo, start, stop):
                mm(outp, wh, xlo, start=start, stop=False)
                mm(outp, wl, xhi, start=False, stop=False)
                return mm(outp, wh, xhi, start=False, stop=stop)

            def unit(n, slot, x, nkb=KB, m=P, kx=0, xcount=None, free=None):
                pe.wait_ge(s_lo, n + 1)
                if not (isinstance(n, int) and n < 2):
                    pe.wait_ge(s_free[slot], free)
                for k in range(nkb):
                    if xcount is not None:
                        pe.wait_ge(s_xlo, xcount(k))
                    last = three(bank[slot][0:m, :], w_hi[:, slot, k, 0:m], w_lo[:, slot, k, 0:m],
                                 x[:, 0, kx + k, :], x[:, 1, kx + k, :], k == 0, k == nkb - 1)
                last.then_inc(s_unit, 1)

            def norm(n):
                pe.wait_ge(s_sqa, (n + 1) * DK)
                mm(bank[4][:], mean_d[:], acc[:], start=True, stop=True).then_inc(s_ms, 1)

            pe.wait_ge(s_const, 1)
            pe.wait_ge(s_xin, 16)
            for k in range(DK):
                if k >= 4:
                    pe.wait_ge(s_xt, k - 3)
                for q in range(4):
                    last = tr(bank[k % 4][:, q * P:(q + 1) * P], x_raw[:, q, k * P:(k + 1) * P], ident[:])
                last.then_inc(s_tr, 1)
            pe.wait_ge(s_par, 16 * sum(len(rows) for rows in PARAMS))
            for t in range(4):
                n = PAR_ROWS[t]
                last = tr(bank[5][:, t * P:t * P + n], par_raw[0:n, t, :], ident[0:n, 0:n])
            last.then_inc(s_part, 1)
            norm(0)
            for n in range(2):
                unit(n, n, xl[n], m=LORA, xcount=lambda k: 2 * k + n + 1)

            def gate(t):
                for u in range(2):
                    unit(2 * t + (U_GATE + u), u, xh, free=t + 1)
            pe.wait_ge(s_xlo, X_G + DK)
            repeat(pe, CI // 2, gate)

            def mix(j):
                n0 = 4 * j + U_MIX
                pe.wait_ge(s_lo, n0 + 1)
                pe.wait_ge(s_free[0], 2 * j + FREE_MIX)
                for n in range(2):
                    last = three(bank[2 * n][:], w_hi[0:LORA, 0, n, :], w_lo[0:LORA, 0, n, :],
                                 lora[:, n, 0, :], lora[:, n, 1, :], True, True)
                last.then_inc(s_unit, 1)
                unit(n0 + 1, 1, xl[0], free=2 * j + FREE_MIX)
                unit(n0 + 2, 0, xl[1], free=2 * j + (FREE_MIX + 1))
                pe.wait_ge(s_sqk, j + 1)
                mm(bank[4][:], head_ones[:], sqk[:], start=True, stop=True).then_inc(s_n2, 1)
                unit(n0 + 3, 1, xl[2], free=2 * j + (FREE_MIX + 1))
                pe.wait_ge(s_rk, j + 1)
                mm(bank[5][:], head_rk[:], rk[:], start=True, stop=True).then_inc(s_bon, 1)
            pe.wait_ge(s_xlo, X_Y)
            pe.wait_ge(s_lt, 2)
            repeat(pe, CI, mix)
            recurrence_tensor(pe)

            def even(base, turns, x, nkb=KB):
                def turn(t):
                    for u in range(2):
                        unit(2 * t + (base + u), u, x, nkb=nkb, free=t + base // 2)
                repeat(pe, turns, turn)

            for half in range(2):
                pe.wait_ge(s_xlo, X_Y + DK * (half + 1))
                even(U_OUT1 + half * DK, DK // 2, xl[half])
            norm(1)
            pe.wait_ge(s_xlo, X_H2 + DK)
            for half in range(2):
                base = U_CONV + half * (4 * KB + DK)

                def conv(t):
                    for u in range(4):
                        unit(4 * t + (base + u), u % 2, xl[2], free=2 * t + (base // 2 + u // 2))
                repeat(pe, KB, conv)
                pe.wait_ge(s_xlo, X_YC + KB * (half + 1))
                even(base + 4 * KB, DK // 2, xl[half])
            norm(2)
            norm(3)
            pe.wait_ge(s_xlo, X_H3 + DK)
            even(U_GLU, CT + 3 * AT // 2, xh)
            v_ch = [sq[:, 0, :], sq[:, 1, :], rstd[:, 0, :], rstd[:, 1, :]]
            pe.wait_ge(s_free[1], (U_GATES2 - 1) // 2 + 1)
            for q in range(NT):
                for n in range(AT):
                    last = tr(bank[2 + q][:, n * P:(n + 1) * P], v_ch[n][:, q * P:(q + 1) * P], ident[:])
                last.then_inc(s_vt, 1)
            even(U_GATES2, DK, xh)
            pe.wait_ge(s_dc, 2)
            mm(bank[4][:], mean_d[:], acc[:], start=True, stop=True).then_inc(s_lnm, 1)
            pe.wait_ge(s_lacc, CT)
            mm(bank[4][:], mean_d[:], acc[:], start=True, stop=True).then_inc(s_lnm, 1)
            attention_tensor(pe)
            for n in range(DK):
                pe.wait_ge(s_lo, U_MERGE + n + 1)
                pe.wait_ge(s_free[n % 2], (U_MERGE + n) // 2)
                if n == 0:
                    pe.wait_ge(s_xlo, X_AT + AT)
                for part, (x, where) in enumerate(((uc, bank[n % 2]), (ah, bank[2 + n % 2]))):
                    for k in range(4):
                        kb = 4 * part + k
                        last = three(where[:], w_hi[:, n % 2, kb, :], w_lo[:, n % 2, kb, :], x[:, 0, k, :],
                                     x[:, 1, k, :], k == 0, k == 3)
                last.then_inc(s_unit, 1)
            pe.wait_ge(s_xlo, X_MG + DK)
            even(U_WOUT2, DK // 2, xh)
            norm(4)
            norm(5)
            pe.wait_ge(s_xlo, X_H4 + DK)
            base = U_FFN
            for part, (j0, n) in enumerate(FPARTS):
                even(base, n, xl[0])
                pe.wait_ge(s_xlo, X_FF + j0 + n)
                even(base + 2 * n, DK // 2, xl[1 + part % 2], nkb=n)
                base += 2 * n + DK
            norm(6)
            pe.wait_ge(s_ffn, DK)
            for q in range(NT):
                for half in range(2):
                    b = 2 * q + half
                    if b == 4:
                        pe.wait_ge(s_rs, 7)
                    for k in range(4):
                        last = tr(bank[b][:, k * P:(k + 1) * P], xT2[:, 4 * half + k, q * P:(q + 1) * P], ident[:])
                    last.then_inc(s_yt, 1)

        @block.vector
        def _(dve):
            o = Order(dve, s_vseq)
            V = nc.vector

            def w_low(n, slot, ncol=P):
                dve.wait_ge(s_hi, n + 1)
                V.tensor_tensor(w_lo[:, slot, :, 0:ncol], w_raw[:, slot, :, 0:ncol],
                                w_hi[:, slot, :, 0:ncol].bitcast(F32), ALU.subtract).then_inc(s_lo, 1)

            def x_low(q, lo, hi, buf):
                dve.wait_ge(s_xhi, q + 1)
                V.tensor_tensor(lo, tmp[:, buf, :], hi.bitcast(F32), ALU.subtract).then_inc(s_xlo, 1)

            def norm(n, gain, dst, x=xT):
                for k in range(DK):
                    dve.wait_ge(s_sq, n * DK + k + 1)
                    if k == 0:
                        V.tensor_copy(acc[:], sq[:, 0, :]).then_inc(s_sqa, 1)
                    else:
                        dve.wait_ge(s_sqa, n * DK + k)
                        V.tensor_tensor(acc[:], acc[:], sq[:, k % 2, :], ALU.add).then_inc(s_sqa, 1)
                dve.wait_ge(s_rs, n + 1)
                for k in range(DK):
                    dst(k, lambda where: V.scalar_tensor_tensor(
                        out=where, in0=x[:, k, :], scalar=col(gain, k), in1=rstd[:, 1, :], op0=ALU.mult, op1=ALU.mult))

            dve.wait_ge(s_part, 1)
            for t in range(4):
                o(V.tensor_copy(par[:, t, 0:PAR_ROWS[t]], bank[5][:, t * P:t * P + PAR_ROWS[t]]))
            t_ka, r_ka = PAR_AT["a_ka"]
            o(V.tensor_scalar(neg_ka[:], par[:, t_ka, r_ka:r_ka + CI], -1.0, 1.0, ALU.mult, ALU.add))
            dve.wait_ge(s_xt, DK)
            dve.wait_ge(s_const, 1)
            norm(0, "a_norm", lambda k, h: o(h(hT[:, k, 1:T + 1])))

            def lerp(k, mu, buf, done):
                if not (isinstance(done, int) and done < 1):
                    dve.wait_ge(s_xlo, done)
                V.scalar_tensor_tensor(out=tmp[:, buf, :], in0=acc[:], scalar=col("a_mu", k + mu * DK),
                                       in1=hT[:, bass.ds(k, 1), 1:T + 1], op0=ALU.mult,
                                       op1=ALU.add).then_inc(s_tmp, 1)

            def shift_difference(k):
                o(V.tensor_tensor(acc[:], hT[:, bass.ds(k, 1), 0:T], hT[:, bass.ds(k, 1), 1:T + 1], ALU.subtract))

            w_low(0, 0, LORA)
            w_low(1, 1, LORA)
            for k in range(DK):
                shift_difference(k)
                lerp(k, 1, 0, 2 * k - 1)
                lerp(k, 4, 1, 2 * k)
                x_low(2 * k, xl[0][:, 1, k, :], xl[0][:, 0, k, :], 0)
                x_low(2 * k + 1, xl[1][:, 1, k, :], xl[1][:, 0, k, :], 1)
            for k in range(DK):
                shift_difference(k)
                lerp(k, 5, k % 2, X_G + k - 1)
                x_low(X_G + k, xh[:, 1, k, :], xh[:, 0, k, :], k % 2)
            z = rstd[0:LORA, 0, :]
            dve.wait_ge(s_unit, 1)
            V.tensor_scalar(z, bank[0][0:LORA, :], 0.5 * CLAMP, None, ALU.max).then_inc(s_free[0], 1)
            dve.wait_ge(s_lsig, 1)
            V.tensor_scalar(z, z, 2.0, -1.0, ALU.mult, ALU.add).then_inc(s_lhid, 1)
            dve.wait_ge(s_unit, 2)
            V.tensor_copy(rstd[0:LORA, 1, :], bank[1][0:LORA, :]).then_inc(s_free[1], 1)
            w_low(U_GATE, 0)
            for n in range(2):
                dve.wait_ge(s_lhi, n + 1)
                V.tensor_tensor(lora[:, n, 1, :], rstd[0:LORA, n, :], lora[:, n, 0, :].bitcast(F32),
                                ALU.subtract).then_inc(s_lt, 1)

            def gate(t):
                n0 = 2 * t + U_GATE
                for u in range(2):
                    w_low(n0 + (u + 1), 1 - u)
                    dve.wait_ge(s_unit, n0 + (u + 1))
                    V.tensor_scalar(rstd[:, u, :], bank[u][:], CLAMP, None, ALU.max).then_inc(s_z, 1)
                    if u == 0:
                        shift_difference(t)
                    for n, mu in ((0, 2), (1, 0)) if u == 0 else ((2, 3),):
                        lerp(t, mu, n % 2, 3 * t + (X_RKV + n - (n > 0)))
                    for n in (range(2) if u == 0 else range(2, 3)):
                        x_low(3 * t + (X_RKV + n), xl[n][:, 1, bass.ds(t, 1), :], xl[n][:, 0, bass.ds(t, 1), :],
                              n % 2)
                    dve.wait_ge(s_sg, 2 * t + (u + 1))
                    dve.wait_ge(s_spill, 32 * t + 16)
                    V.tensor_tensor(sq[:, u, :], rstd[:, u, :], bank[u][:], ALU.mult).then_inc(s_free[u], 1)
            dve.wait_ge(s_lt, 2)
            repeat(dve, CI // 2, gate, o, 1)
            dve.wait_ge(s_const, 2)

            def by_chunk(x):
                return x.rearrange("p (c t) -> p c t", c=NCH)

            def mix(j):
                n0 = 4 * j + U_MIX
                w_low(n0 + 1, 1)
                dve.wait_ge(s_unit, n0 + 1)
                V.tensor_scalar(zw[:], bank[0][:], col("a_w0", j), CLAMP, ALU.add, ALU.max).then_inc(s_zw, 1)
                V.tensor_scalar(za[:], bank[2][:], col("a_a0", j), CLAMP, ALU.add, ALU.max).then_inc(s_free[0], 1)
                o(V.tensor_scalar(head_rk[:], head_ones[:], col("a_rk", j), None, ALU.mult))
                w_low(n0 + 2, 0)
                dve.wait_ge(s_unit, n0 + 2)
                V.tensor_scalar(kk[:], bank[1][:], col("a_kk", j), None, ALU.mult).then_inc(s_kk, 1)
                dve.wait_ge(s_sw, j + 1)
                o(V.tensor_scalar(lw[:, :, 1:W1], by_chunk(zw[:]), -EDECAY, None, ALU.mult))
                V.tensor_tensor_scan(out=cs[:].rearrange("p c t -> p (c t)"),
                                     data0=scanm[:].rearrange("p c t -> p (c t)"),
                                     data1=lw[:].rearrange("p c t -> p (c t)"), initial=0.0,
                                     op0=ALU.mult, op1=ALU.add).then_inc(s_cs, 1)
                dve.wait_ge(s_sa, j + 1)
                o(V.tensor_scalar(kp[:], za[:], col("a_ka", j), neg_ka[:, bass.ds(j, 1)], ALU.mult, ALU.add))
                V.tensor_tensor(kp[:], kp[:], bank[1][:], ALU.mult).then_inc(s_free[1], 1)
                w_low(n0 + 3, 1)
                dve.wait_ge(s_unit, n0 + 3)
                dve.wait_ge(s_free[1], 2 * j + (FREE_MIX + 1))
                V.tensor_tensor(rk[:], kp[:], bank[0][:], ALU.mult).then_inc(s_rk, 1)
                dve.wait_ge(s_pw, j + 1)
                dve.wait_ge(s_spill, j * SPILL_TILE + SPILL_MIX)
                V.tensor_tensor(by_chunk(o_r[:]), pw[:, :, 1:W1], by_chunk(bank[0][:]), ALU.mult).then_inc(s_free[0], 1)
                dve.wait_ge(s_n2, j + 1)
                V.tensor_scalar(n2[:], bank[4][:], 1e-24, None, ALU.max).then_inc(s_n2m, 1)
                w_low(n0 + 4, 0)
                dve.wait_ge(s_rn, j + 1)
                o(V.tensor_tensor(kn[:], kk[:], rn[:], ALU.mult))
                o(V.tensor_tensor(kka[:], kn[:], za[:], ALU.mult))
                V.tensor_tensor(by_chunk(o_q[:]), by_chunk(kn[:]), pw[:, :, 0:C], ALU.mult).then_inc(s_fin, 1)
                V.tensor_tensor(by_chunk(o_b[:]), by_chunk(kka[:]), pinv[:, :, 1:W1], ALU.mult).then_inc(s_fin, 1)
                V.tensor_tensor(by_chunk(o_c[:]), by_chunk(kp[:]), pinv[:, :, 1:W1], ALU.mult).then_inc(s_fin, 1)
                dve.wait_ge(s_bon, j + 1)
                dve.wait_ge(s_free[1], 2 * j + (FREE_MIX + 2))
                V.tensor_tensor(o_bv[:], o_v[:], bank[5][:], ALU.mult).then_inc(s_fin, 1)
            repeat(dve, CI, mix, o, 5)
            recurrence_vector(dve, o)

            for k in range(CI):
                dve.wait_ge(s_xhi, X_Y + k + 1)
                half = xl[k // DK]
                V.tensor_tensor(half[:, 1, k % DK, :], Y[:, k, :], half[:, 0, k % DK, :].bitcast(F32),
                                ALU.subtract).then_inc(s_xlo, 1)
            dve.wait_ge(s_back, 16)

            def even(base, turns, dst, add, final=False):
                def turn(t, last=False):
                    for u in range(2):
                        if not (last and u == 1):
                            w_low(2 * t + (base + u + 1), 1 - u)
                        dve.wait_ge(s_unit, 2 * t + (base + u + 1))
                        where = dst[:, bass.ds(2 * t + u, 1), :]
                        (V.tensor_tensor(where, where, bank[u][:], ALU.add) if add else
                         V.tensor_copy(where, bank[u][:])).then_inc(s_free[u], 1)
                repeat(dve, turns - final, turn)
                if final:
                    turn(turns - 1, last=True)

            def split(x0, dst, n):
                def step(k, make):
                    if x0 + k >= 2:
                        dve.wait_ge(s_xlo, x0 + k - 1)
                    make(tmp[:, k % 2, :]).then_inc(s_tmp, 1)
                    if k:
                        x_low(x0 + k - 1, dst[:, 1, k - 1, :], dst[:, 0, k - 1, :], (k - 1) % 2)
                    if k == n - 1:
                        x_low(x0 + k, dst[:, 1, k, :], dst[:, 0, k, :], k % 2)
                return step

            for half in range(2):
                even(U_OUT1 + half * DK, DK // 2, xT2, True)

            o(V.memset(cu[:, 0:2], 0.0))
            dve.wait_ge(s_xlo, X_H2)
            norm(1, "b_norm", split(X_H2, xl[2], DK), xT2)
            for half in range(2):
                base = U_CONV + half * (4 * KB + DK)

                def conv(t):
                    n0 = 4 * t + base
                    w_low(n0 + 1, 1)
                    dve.wait_ge(s_unit, n0 + 1)
                    V.tensor_copy(c_sb[:], bank[0][:]).then_inc(s_free[0], 1)
                    w_low(n0 + 2, 0)
                    dve.wait_ge(s_unit, n0 + 2)
                    dve.wait_ge(s_free[0], 2 * t + (base // 2 + 1))
                    V.tensor_tensor(cu[:, 2:2 + T], c_sb[:], bank[1][:], ALU.mult).then_inc(s_free[1], 1)
                    dve.wait_ge(s_free[1], 2 * t + (base // 2 + 1))
                    ct = t + KB * half
                    o(V.tensor_scalar(conv3[:, 0, :], cu[:, 0:T], col("b_conv", ct), None, ALU.mult))
                    for tap in (1, 2):
                        o(V.scalar_tensor_tensor(out=conv3[:, tap % 2, :], in0=cu[:, tap:tap + T],
                                                 scalar=col("b_conv", ct + tap * CI), in1=conv3[:, 1 - tap % 2, :],
                                                 op0=ALU.mult, op1=ALU.add))
                    w_low(n0 + 3, 1)
                    dve.wait_ge(s_unit, n0 + 3)
                    V.tensor_scalar(gate3[:], bank[0][:], CLAMP, None, ALU.max).then_inc(s_zc, 1)
                    dve.wait_ge(s_sc, ct + 1)
                    V.tensor_tensor(gate3[:], gate3[:], bank[0][:], ALU.mult).then_inc(s_free[0], 1)
                    dve.wait_ge(s_free[0], 2 * t + (base // 2 + 2))
                    o(V.tensor_tensor(gate3[:], gate3[:], conv3[:, 0, :], ALU.mult))
                    w_low(n0 + 4, 0)
                    dve.wait_ge(s_unit, n0 + 4)
                    V.tensor_tensor(tmp[:, 0, :], gate3[:], bank[1][:], ALU.mult).then_inc(s_free[1], 1)
                    x_low(t + (X_YC + KB * half), xl[half][:, 1, bass.ds(t, 1), :], xl[half][:, 0, bass.ds(t, 1), :], 0)
                repeat(dve, KB, conv, o, 4)
                even(base + 4 * KB, DK // 2, xT2, True)

            norm(2, "final_norm", lambda k, scaled: scaled(xT2[:, k, :]).then_inc(s_xn, 1), xT2)
            o(V.memset(glu[:, :, 0:PAD2], 0.0))
            norm(3, "norm_mix_pre_2", split(X_H3, xh, DK), xT2)
            for j in range(CT):
                n0 = U_GLU + 2 * j
                w_low(n0 + 1, 1)
                w_low(n0 + 2, 0)
                dve.wait_ge(s_unit, n0 + 2)
                if j >= 2:
                    dve.wait_ge(s_free[0], n0 // 2 - 1)
                V.tensor_scalar(rstd[:, j % 2, :], bank[1][:], CLAMP, None, ALU.max).then_inc(s_free[1], 1)
                dve.wait_ge(s_glu, j + 1)
                V.tensor_tensor(glu[:, j, PAD2:], rstd[:, j % 2, :], bank[0][:], ALU.mult).then_inc(s_free[0], 1)
            dve.wait_ge(s_free[0], U_QKV // 2)

            def taps():
                for j in range(CT):
                    y = dconv[:, j, :]
                    o(V.tensor_scalar(y, glu[:, j, 0:T], col("conv_dw_w_2", j), col("conv_dw_b_2", j), ALU.mult,
                                      ALU.add))
                    yield
                    for tap in range(1, TAPS2):
                        o(V.scalar_tensor_tensor(out=y, in0=glu[:, j, tap:tap + T], scalar=col("conv_dw_w_2", tap * CT + j),
                                                 in1=y, op0=ALU.mult, op1=ALU.add))
                        yield
            tap = taps()
            v_ch = [sq[:, 0, :], sq[:, 1, :], rstd[:, 0, :], rstd[:, 1, :]]
            for n in range(3 * AT + 2 * DK):
                u = U_QKV + n
                w_low(u + 1, (n + 1) % 2)
                dve.wait_ge(s_unit, u + 1)
                src = bank[n % 2][:]
                if n < AT:
                    ins = V.tensor_scalar(qT[:, n, :], src, 0.125, None, ALU.mult)
                elif n < 2 * AT:
                    ins = V.tensor_copy(kT[:, n - AT, :], src)
                elif n < 3 * AT:
                    ins = V.tensor_copy(v_ch[n - 2 * AT], src)
                else:
                    m = n - 3 * AT
                    ins = V.tensor_scalar(gates[:, m % 2, m // 2, :], src, CLAMP, None, ALU.max)
                ins.then_inc(s_free[n % 2], 1)
                for _ in range(5):
                    next(tap, None)

            dve.wait_ge(s_vt, NT)
            o(V.tensor_tensor(acc[:], dconv[:, 0, :], dconv[:, 1, :], ALU.add))
            V.tensor_tensor(acc[:], acc[:], dconv[:, 2, :], ALU.add).then_inc(s_dc, 1)
            dve.wait_ge(s_dc, 1)
            V.tensor_tensor(acc[:], acc[:], dconv[:, 3, :], ALU.add).then_inc(s_dc, 1)
            dve.wait_ge(s_lnm, 1)
            for j in range(CT):
                V.scalar_tensor_tensor(out=dconv[:, j, :], in0=bank[4][:], scalar=-2.0, in1=dconv[:, j, :],
                                       op0=ALU.mult, op1=ALU.add).then_inc(s_cen, 1)
            for j in range(CT):
                dve.wait_ge(s_lsq, j + 1)
                if j == 0:
                    V.tensor_copy(acc[:], sq[:, 0, :]).then_inc(s_lacc, 1)
                else:
                    dve.wait_ge(s_lacc, j)
                    V.tensor_tensor(acc[:], acc[:], sq[:, j % 2, :], ALU.add).then_inc(s_lacc, 1)
            dve.wait_ge(s_lrs, 1)
            finish = split(X_UC, uc, CT)
            for j in range(CT):
                y = dconv[:, j, :]
                o(V.tensor_tensor(y, y, rstd[:, 1, :], ALU.mult))
                o(V.tensor_scalar(y, y, col("conv_ln_g_2", j), col("conv_ln_b_2", j), ALU.mult, ALU.add))
                V.tensor_scalar(sq[:, j % 2, :], y, CLAMP, None, ALU.max).then_inc(s_lz, 1)
                dve.wait_ge(s_ls, j + 1)
                finish(j, lambda where: V.tensor_tensor(where, y, sq[:, j % 2, :], ALU.mult))
            attention_vector(dve, o, split(X_AT, ah, AT))

            finish = split(X_MG, xh, DK)
            for n in range(DK):
                w_low(U_MERGE + n + 1, (n + 1) % 2)
                dve.wait_ge(s_unit, U_MERGE + n + 1)
                if n == 0:
                    dve.wait_ge(s_gate2, 2 * DK)
                o(V.scalar_tensor_tensor(out=sq[:, 0, :], in0=bank[n % 2][:], scalar=col("b_conv_branch_2", n),
                                         in1=gates[:, 0, n, :], op0=ALU.add, op1=ALU.mult))
                V.tensor_tensor(sq[:, 1, :], bank[2 + n % 2][:], gates[:, 1, n, :], ALU.mult).then_inc(s_free[n % 2], 1)
                dve.wait_ge(s_free[n % 2], (U_MERGE + n) // 2 + 1)
                finish(n, lambda where: V.tensor_tensor(where, sq[:, 0, :], sq[:, 1, :], ALU.add))
            even(U_WOUT2, DK // 2, mixed, False)

            def residual(n, gain, src, signal):
                norm(n, gain, lambda k, scaled: o(scaled(src[:, k, :])), src)
                for k in range(DK):
                    V.tensor_tensor(xT2[:, k, :], xT2[:, k, :], src[:, k, :], ALU.add).then_inc(signal, 1)
            residual(4, "norm_mix_post_2", mixed, s_mg)

            norm(5, "norm_ffn_pre_2", split(X_H4, xl[0], DK), xT2)
            base = U_FFN
            for part, (j0, n) in enumerate(FPARTS):
                dst = xl[1 + part % 2]

                def ffn(t):
                    n0 = 2 * t + base
                    w_low(n0 + 1, 1)
                    dve.wait_ge(s_unit, n0 + 1)
                    V.tensor_scalar(rstd[:, 0, :], bank[0][:], CLAMP, None, ALU.max).then_inc(s_ug, 1)
                    w_low(n0 + 2, 0)
                    dve.wait_ge(s_us, t + (j0 + 1))
                    V.tensor_tensor(rstd[:, 0, :], rstd[:, 0, :], bank[0][:], ALU.mult).then_inc(s_free[0], 1)
                    dve.wait_ge(s_unit, n0 + 2)
                    dve.wait_ge(s_free[0], t + (base // 2 + 1))
                    V.tensor_tensor(tmp[:, 0, :], rstd[:, 0, :], bank[1][:], ALU.mult).then_inc(s_free[1], 1)
                    x_low(t + (X_FF + j0), dst[:, 1, bass.ds(t, 1), :], dst[:, 0, bass.ds(t, 1), :], 0)
                repeat(dve, n, ffn)
                even(base + 2 * n, DK // 2, ffo, part > 0, final=part == len(FPARTS) - 1)
                base += 2 * n + DK
            residual(6, "norm_ffn_post_2", ffo, s_ffn)
            for q in range(NT):
                dve.wait_ge(s_yt, 2 * q + 1)
                V.tensor_copy(staged[:, q, 0:T], bank[(2 * q) % 8][:]).then_inc(s_yc[0], 1)


_INS = ['x', 'a_norm', 'a_mu', 'a_w_in', 'a_w0', 'a_w1', 'a_w2', 'a_a0', 'a_a1', 'a_a2', 'a_kk', 'a_ka', 'a_rk',
        'a_lnw', 'a_lnb', 'a_w_out', 'b_norm', 'b_w_in', 'b_conv', 'b_w_out', 'final_norm', 'norm_mix_pre_2',
        'w_in_2', 'conv_dw_w_2', 'conv_dw_b_2', 'conv_ln_g_2', 'conv_ln_b_2', 'w_conv_branch_2', 'b_conv_branch_2',
        'w_att_branch_2', 'w_out_2', 'norm_mix_post_2', 'norm_ffn_pre_2', 'w_ffn_up_2', 'w_ffn_down_2',
        'norm_ffn_post_2']


def kernel(**inputs):
    import numpy as _np
    import concourse.bacc as _bacc
    from concourse import mybir as _mybir
    from concourse.bass_utils import run_bass_kernel_spmd as _run

    nc = _bacc.Bacc("TRN2", target_bir_lowering=False, num_devices=1)
    arrays, args = {}, {}
    for name in _INS:
        a = _np.ascontiguousarray(inputs[name])
        arrays[f"in_{name}"] = a
        args[name] = nc.dram_tensor(f"in_{name}", a.shape, _mybir.dt.from_np(a.dtype), kind="ExternalInput").ap()
    out = nc.dram_tensor("out_0", (1, T, D), F32, kind="ExternalOutput").ap()
    program(nc, args, out)
    r = _run(nc, [arrays], core_ids=[0])
    return r.results[0]["out_0"]
```

```python
from contextlib import ExitStack

import concourse.bass as bass
from concourse import mybir

F32 = mybir.dt.float32
F32R = mybir.dt.float32r
F16 = mybir.dt.float16
ALU = mybir.AluOpType
ACT = mybir.ActivationFunctionType

P = 128
T = 512
D = 1024
DK = D // P
DI = 2048
CI = DI // P
LORA = 64
C = 64
NCH = T // C
W1 = C + 1
EDECAY = 0.6065306597126334
CLAMP = -43.0
LN2 = 0.6931471805599453
EXP_LN_SET = 6
NSHIFT = 30
RMS_EPS = 1e-6
GN_EPS = 64e-5
LN_EPS = 1e-6
AD = 512
AT = AD // P
NHEAD2 = 8
CT = 4
TAPS2 = 31
PAD2 = TAPS2 - 1
FT = 22
NT = T // P
ATT_AT = [sum(T - P * m for m in range(n)) for n in range(NT + 1)]
ATT_COLS = ATT_AT[NT]
KB = 8

PARAMS = [
    [("a_norm", 8), ("a_mu", 48), ("a_w0", 16), ("a_a0", 16), ("a_kk", 16), ("a_ka", 16)],
    [("a_rk", 16), ("a_lnw", 16), ("a_lnb", 16), ("b_norm", 8), ("b_conv", 48), ("final_norm", 8)],
    [("norm_mix_pre_2", 8), ("conv_dw_b_2", 4), ("conv_ln_g_2", 4), ("conv_ln_b_2", 4), ("b_conv_branch_2", 8),
     ("norm_mix_post_2", 8), ("norm_ffn_pre_2", 8), ("norm_ffn_post_2", 8)],
    [("conv_dw_w_2", 124)],
]
PAR_ROWS = [sum(n for _, n in rows) for rows in PARAMS]
PAR_AT = {name: (t, sum(n for _, n in rows[:i])) for t, rows in enumerate(PARAMS) for i, (name, _) in enumerate(rows)}

U_LORA1 = 0
U_GATE = U_LORA1 + 2
U_MIX = U_GATE + CI
U_OUT1 = U_MIX + 4 * CI
U_CONV = U_OUT1 + 2 * DK
U_GLU = U_CONV + 2 * (4 * 8 + DK)
U_QKV = U_GLU + 2 * CT
U_GATES2 = U_QKV + 3 * AT
U_MERGE = U_GATES2 + 2 * DK
U_WOUT2 = U_MERGE + DK
U_FFN = U_WOUT2 + DK
FPARTS = [(0, 8), (8, 8), (16, 6)]
U_END = U_FFN + sum(2 * n + DK for _, n in FPARTS)

X_LORA = 0
X_G = X_LORA + 2 * DK
X_RKV = X_G + DK
X_Y = X_RKV + 3 * DK
X_H2 = X_Y + CI
X_YC = X_H2 + DK
X_H3 = X_YC + CI
X_UC = X_H3 + DK
X_AT = X_UC + CT
X_MG = X_AT + AT
X_H4 = X_MG + DK
X_FF = X_H4 + DK


def made(q):
    if not isinstance(q, int) or q < X_Y:
        return q + 1
    if X_YC <= q < X_H3 or q < X_H2:
        return None
    return q + 1 - CI - (CI if q >= X_H3 else 0)


def panel_dmas(n):
    lora2 = U_MIX <= n < U_OUT1 and (n - U_MIX) % 4 == 0
    return 2 if lora2 or U_MERGE <= n < U_WOUT2 else 1


def panels_by(n):
    return 16 * sum(panel_dmas(m) for m in range(n % 2, n + 1, 2))


class Order:

    def __init__(self, eng, sem):
        self.eng, self.sem, self.base, self.k, self.i, self.per = eng, sem, 0, 0, None, 0

    def __call__(self, ins):
        ins.then_inc(self.sem, 1)
        self.k += 1
        n = self.base + self.k
        self.eng.wait_ge(self.sem, n if self.i is None else self.i * self.per + n)

    def enter(self, i, per):
        self.base, self.k, self.i, self.per = self.base + self.k, 0, i, per

    def leave(self, turns):
        assert self.k == self.per, (self.k, self.per)
        self.base, self.k, self.i = self.base + turns * self.per, 0, None


def program(nc, i, out):
    with ExitStack() as ctx:
        at = [16512]

        def place(name, shape, dt, where=None):
            size = 4 if dt in (F32, F32R) else 2
            for n in shape[1:]:
                size *= n
            size = (size + 31) // 32 * 32
            if where is None:
                where = at[0]
                at[0] += size
            return nc.alloc_sbuf_tensor_at(name, shape, dt, offset=where), where, where + size

        def sem(name):
            return ctx.enter_context(nc.semaphore(name))

        def dram(name, shape):
            return nc.dram_tensor(name, shape, F32, kind="Internal").ap()

        ident, _, _ = place("ident", [P, P], F32)
        mean_d, _, _ = place("mean_d", [P, P], F32)
        head_ones, _, _ = place("head_ones", [P, P], F32)
        head_rk, _, _ = place("head_rk", [P, P], F32)
        masks, _, _ = place("masks", [P, P + C], F32)
        par, _, _ = place("par", [P, 4, P], F32)
        neg_ka, _, _ = place("neg_ka", [P, CI], F32)
        eps, _, _ = place("eps", [P, 4], F32)
        w_raw, _, _ = place("w_raw", [P, 2, KB, P], F32)
        w_hi, _, _ = place("w_hi", [P, 2, KB, P], F32R)
        w_lo, _, _ = place("w_lo", [P, 2, KB, P], F32R)
        tmp, _, _ = place("tmp", [P, 2, T], F32)
        sq, _, _ = place("sq", [P, 2, T], F32)
        acc, _, _ = place("acc", [P, T], F32)
        rstd, _, _ = place("rstd", [P, 2, T], F32)
        att_from, _, _ = place("att_from", [P, P], F32)
        att_ones, _, _ = place("att_ones", [P, P], F32)
        att_keep, _, _ = place("att_keep", [P, P], F32)
        att_drop, _, _ = place("att_drop", [P, P], F32)
        xT, x_at, _ = place("xT", [P, DK, T], F32)
        xh, xh_at, _ = place("xh", [P, 2, DK, T], F32R)
        big_at = at[0]
        xl = [place(f"xl{n}", [P, 2, DK, T], F32R)[0] for n in range(3)]
        free_at = at[0]
        hT, hT_at, hT_end = place("hT", [P, DK, T + 1], F32)
        assert at[0] <= nc.sbuf_usable_end, (at[0], nc.sbuf_usable_end)
        x_raw, _, _ = place("x_raw", [P, 4, D], F32, big_at + 2 * 32768)
        par_raw, _, _ = place("par_raw", [P, 4, P], F32, big_at + 2 * 32768 + 16384)
        lora, lora_at, lora_end = place("lora", [LORA, 2, 2, T], F32R, x_at)
        spot = xh_at

        def over(name, shape, dt=F32):
            nonlocal spot
            t, a, spot = place(name, shape, dt, spot)
            return t

        zw, za = over("zw", [P, T]), over("za", [P, T])
        kk, kn, rn = over("kk", [P, T]), over("kn", [P, T]), over("rn", [P, T])
        kp, kka, rk = over("kp", [P, T]), over("kka", [P, T]), over("rk", [P, T])
        n2, sqk = over("n2", [P, T]), over("sqk", [P, T])
        o_r, o_v, o_bv = over("o_r", [P, T]), over("o_v", [P, T]), over("o_bv", [P, T])
        o_q, o_pc = over("o_q", [P, T]), over("o_pc", [P, NCH])
        assert spot <= xh_at + 32768
        spot = hT_at
        lw, cs = over("lw", [P, NCH, W1]), over("cs", [P, NCH, W1])
        pw, pinv = over("pw", [P, NCH, W1]), over("pinv", [P, NCH, W1])
        o_b, o_c = over("o_b", [P, T]), over("o_c", [P, T])
        scanm = over("scanm", [P, NCH, W1])
        assert spot <= hT_end

        spot = lora_end
        bmask = over("bmask", [P, 5, P])
        eyes = over("eyes", [P, NCH, C])
        eyes16 = over("eyes16", [P, 4, P], F16)
        two16 = over("two16", [P, P], F16)
        one16 = over("one16", [P, P], F16)
        center = over("center", [P, P])
        head_mean = over("head_mean", [P, P])
        assert spot <= xh_at
        spot = xh_at
        Y = over("Y", [P, CI, T])
        st_q = [over(f"st_q{n}", [P, NCH, 3, C]) for n in range(3)]
        st_bc = [over(f"st_bc{n}", [P, NCH, 2, C]) for n in range(2)]
        st_v = [over(f"st_v{n}", [P, (NCH + 1) * C]) for n in range(2)]
        st_bv = [over(f"st_bv{n}", [P, T]) for n in range(2)]
        st_g = [over(f"st_g{n}", [P, T]) for n in range(2)]
        st_pc = [over(f"st_pc{n}", [P, NCH]) for n in range(3)]
        ra = [over(f"ra{n}", [P, NCH, 2, C]) for n in range(2)]
        bt = [over(f"bt{n}", [P, NCH, P]) for n in range(2)]
        sv = [over(f"sv{n}", [P, NCH, 2, C]) for n in range(2)]
        tt = [over(f"tt{n}", [P, NCH, P]) for n in range(2)]
        nix, nixe = over("nix", [P, NCH, C]), over("nixe", [P, NCH, C])
        nix16, nixlo16, w16 = (over(n, [P, NCH, P], F16) for n in ("nix16", "nixlo16", "w16"))
        inv16, inv_t16 = over("inv16", [P, NCH, P], F16), over("inv_t16", [P, NCH, P], F16)
        rhs = over("rhs", [P, C])
        y0, yc, ysq, yr, y2 = (over(n, [P, T]) for n in ("y0", "yc", "ysq", "yr", "y2"))
        assert spot <= nc.sbuf_usable_end, (spot, nc.sbuf_usable_end)

        xT2, _, _ = place("xT2", [P, DK, T], F32, hT_at)
        spot = xh_at
        c_sb, cu, conv3 = over("c_sb", [P, T]), over("cu", [P, 2 + T]), over("conv3", [P, 2, T])
        gate3 = over("gate3", [P, T])
        spot = big_at
        gates = over("gates", [P, 2, DK, T])
        uc = over("uc", [P, 2, CT, T], F32R)
        ah = over("ah", [P, 2, AT, T], F32R)
        vtok = over("vtok", [P, NT, AD])
        tail_at = spot
        glu = over("glu", [P, CT, PAD2 + T])
        dconv, tapped = over("dconv", [P, CT, T]), over("tapped", [P, T])
        spot = tail_at
        att_sp, att_a = over("att_sp", [P, 2, ATT_COLS]), over("att_a", [P, 2, ATT_COLS])
        att_zz = over("att_zz", [P, 2, T])
        att_z = [rstd[:, 0, :], rstd[:, 1, :], att_zz[:, 0, :], att_zz[:, 1, :]]
        assert spot <= hT_at, (spot, hT_at)
        spot = x_at
        qT, kT = over("qT", [P, AT, T]), over("kT", [P, AT, T])
        mixed, _, _ = place("mixed", [P, DK, T], F32, x_at)
        ffo, _, _ = place("ffo", [P, DK, T], F32, xh_at)
        staged, _, _ = place("staged", [P, T // P, D], F32, x_at)

        bank = [ctx.enter_context(nc.psum_tensor(f"bank{n}", [P, T], F32)) for n in range(8)]

        d_x = dram("d_x", [P, DK, T])
        d_g = dram("d_g", [CI, P, T])
        d_q, d_r, d_b, d_c, d_v, d_bv = (dram(f"d_{n}", [CI, P, T]) for n in ("q", "r", "b", "c", "v", "bv"))
        d_pc = dram("d_pc", [CI, P, NCH])

        def col(name, j):
            t, row = PAR_AT[name]
            return par[:, t, bass.ds(row + j, 1)]

        s_xin = sem("x_loaded")
        s_par = sem("params_loaded")
        s_const = sem("constants_made")
        s_part = sem("params_transposed")
        s_parok = sem("params_copied")
        s_tr = sem("x_transposed")
        s_xt = sem("xT_copied")
        s_raw = [sem("panel_in_slot0"), sem("panel_in_slot1")]
        s_hi = sem("panel_hi_made")
        s_lo = sem("panel_lo_made")
        s_unit = sem("unit_summed")
        s_free = [sem("unit_bank0_read"), sem("unit_bank1_read")]
        s_sq = sem("squares_made")
        s_sqa = sem("squares_added")
        s_ms = sem("mean_square_summed")
        s_rs = sem("rstd_made")
        s_tmp = sem("activation_made")
        s_xhi = sem("activation_hi_made")
        s_xlo = sem("activation_lo_made")
        s_xsaved = sem("xT_saved")
        s_spill = sem("spilled")
        s_lsig = sem("lora_sigmoid_made")
        s_lhid = sem("lora_hidden_made")
        s_lhi = sem("lora_hidden_hi_made")
        s_lt = sem("lora_hidden_lo_made")
        s_z = sem("gate_arg_made")
        s_sg = sem("gate_sigmoid_made")
        s_zw = sem("decay_arg_made")
        s_sw = sem("decay_sigmoid_made")
        s_sa = sem("rate_sigmoid_made")
        s_kk = sem("kk_made")
        s_sqk = sem("kk_squared")
        s_n2 = sem("kk_norm_summed")
        s_n2m = sem("kk_norm_clamped")
        s_rn = sem("kk_rnorm_made")
        s_cs = sem("log_decay_summed")
        s_pw = sem("decay_powers_made")
        s_rk = sem("bonus_terms_made")
        s_bon = sem("bonus_summed")
        s_fin = sem("tile_finished")
        s_vseq, s_aseq, s_gseq = sem("vector_order"), sem("scalar_order"), sem("gpsimd_order")
        s_back = sem("xT_reloaded")
        s_pad = sem("conv_pads_zeroed")
        s_zc = sem("conv_gate_arg_made")
        s_sc = sem("conv_gate_sigmoid_made")
        s_xn = sem("final_norm_applied")
        s_glu = sem("glu_sigmoid_made")
        s_gate2 = sem("branch_gate_made")
        s_vt = sem("v_turned")
        s_vtok = sem("v_turned_copied")
        s_tap3 = sem("gpsimd_channels_convolved")
        s_dc = sem("depthwise_conv_summed")
        s_lnm = sem("layernorm_sum_made")
        s_cen = sem("layernorm_centered")
        s_lsq = sem("layernorm_squared")
        s_lacc = sem("layernorm_squares_added")
        s_lrs = sem("layernorm_rstd_made")
        s_lz = sem("layernorm_silu_arg_made")
        s_ls = sem("layernorm_silu_sigmoid_made")
        s_sc2 = sem("scores_summed")
        s_neg = sem("scores_copied")
        s_log = sem("log_term_made")
        s_sp = sem("softplus_made")
        s_cum = sem("softplus_summed")
        s_dif = sem("log_weights_made")
        s_wt = sem("weights_made")
        s_o = sem("attention_summed")
        s_scaled = sem("mixed_or_ffn_scaled")
        s_mg = sem("mixed_added")
        s_ug = sem("ffn_gate_arg_made")
        s_us = sem("ffn_gate_sigmoid_made")
        s_ffn = sem("ffn_added")
        s_yt = sem("output_turned")
        s_yc = [sem("output_copied0"), sem("output_copied1")]
        s_out = sem("output_written")
        R = {n: sem(n) for n in (
            "products_summed", "products_masked", "turned", "turned_copied", "nix_made", "nix16_made", "q0_made", "r0_summed", "r0_copied",
            "low_made", "v_summed", "v_copied", "rq_summed", "rq_copied", "q1_copied", "e_summed", "t_summed",
            "rhs_summed", "u_summed", "s_summed", "y_summed", "y_bank_read", "centered",
            "centered_copied", "y_squared", "var_summed", "y_rstd_made", "y_finished")}
        for n in ("e_copied", "inverse_made", "state_zeroed", "tiles_loaded", "ends_loaded", "rhs_copied", "u_copied", "s_copied"):
            R[n] = [sem(f"{n}{h}") for h in range(2)]

        block = ctx.enter_context(nc.Block())

        def repeat(eng, turns, body, order=None, per=0):
            with eng.Fori(0, turns) as n:
                if order is not None:
                    order.enter(n, per)
                body(n)
            if order is not None:
                order.leave(turns)

        w_in = i["a_w_in"].rearrange("a s d e -> (a s) d e")
        LOADS = 16 * 10
        SPILL_MIX = 16 + 16 * CI
        SPILL_TILE = 16 * 7
        FREE_MIX = 1 + CI // 2

        def panels(first, units, n, u):
            if isinstance(n, int):
                return panels_by(first + units * n + u)
            step = panels_by(first + units + u - 2 * (u == units)) - panels_by(first + u - 2 * (u == units))
            return n * step + panels_by(first + u)


        S_NEWTON = 10

        def when(turn, last):
            return 0 <= turn < last

        def recurrence_tensor(pe):
            mm, tr = nc.tensor.matmul, nc.tensor.transpose
            rows = [slice(0, C), slice(C, P)]

            def chain(j, b, c, phase):
                if phase == 0:
                    if c == 0:
                        for g in range(2):
                            pe.wait_ge(R["inverse_made"][g], j + 1)
                    for h in range(2):
                        pe.wait_ge(*((R["s_copied"][h], (NCH - 1) * j + c) if c else (R["state_zeroed"][h], j + 1)))
                    for h in range(2):
                        last = mm(bank[5][rows[h], 0:C], st_q[j % 3][:, c, 2 * h, :], sv[b][:, c, h, :],
                                  start=True, stop=True)
                    last.then_inc(R["rhs_summed"], 1)
                    if c == 0 and j:
                        pe.wait_ge(R["y_bank_read"], j)
                    for h in range(2):
                        mm(bank[7][rows[h], c * C:(c + 1) * C], sv[b][rows[h], c, h, :], st_q[j % 3][rows[h], c, 1, :],
                           start=True, stop=False)
                    for h in range(2):
                        mm(bank[6][rows[h], 0:C], ident[rows[h], rows[h]], sv[b][rows[h], c, h, :],
                           start=True, stop=False)
                elif phase == 1:
                    for h in range(2):
                        pe.wait_ge(R["rhs_copied"][h], NCH * j + c + 1)
                    mm(bank[5][:, C:2 * C], tt[b][:, c, :], rhs[:], start=True, stop=True).then_inc(R["u_summed"], 1)
                else:
                    for h in range(2):
                        pe.wait_ge(R["u_copied"][h], NCH * j + c + 1)
                        last = mm(bank[6][rows[h], 0:C], bt[b][:, c, rows[h]], sv[b][:, c, h, :],
                                  start=False, stop=True)
                    last.then_inc(R["s_summed"], 1)
                    for h in range(2):
                        last = mm(bank[7][rows[h], c * C:(c + 1) * C], sv[b][:, c, h, :], ra[b][:, c, h, :],
                                  start=False, stop=True)
                    if c == NCH - 1:
                        last.then_inc(R["y_summed"], 1)

            def products(j, b, c):
                if c == 0:
                    pe.wait_ge(R["tiles_loaded"][b], LOADS * (j // 2 + 1))
                    if j:
                        for g in range(2):
                            pe.wait_ge(R["inverse_made"][g], j)
                elif c == 4:
                    pe.wait_ge(R["products_masked"], 2 * j + 1)
                    pe.wait_ge(R["turned_copied"], 2 * j + 1)
                for h in range(2):
                    last = mm(bank[2 + h][:, (c % 4) * P:(c % 4 + 1) * P], st_bc[b][rows[h], c, :, :],
                              st_q[j % 3][rows[h], c, h:h + 2, :], start=True, stop=True)
                if c % 4 == 3:
                    last.then_inc(R["products_summed"], 1)
                tr(bank[0][:, (c % 4) * P:(c % 4 + 1) * P], st_bc[b][:, c, :, :], ident[:])
                last = tr(bank[1][:, (c % 4) * P:(c % 4 + 1) * P], st_v[b][:, c * C:(c + 2) * C], ident[:])
                if c % 4 == 3:
                    last.then_inc(R["turned"], 1)

            eyes4 = eyes16[:].rearrange("p c t -> p (c t)")
            pair = [(1, 2), (0, 3)]

            def each(bk, g, lhsT, rhs_, start=True, stop=True):
                for c in range(4):
                    last = mm(bank[bk][:, c * P:(c + 1) * P], lhsT[:, 4 * g + c, :], rhs_[:, c if rhs_ is eyes16 else
                              4 * g + c, :], start=start, stop=stop, skip_group_check=True)
                return last

            def first_inverse(j):
                pe.wait_ge(R["turned_copied"], 2 * j + 2)
                for g in range(2):
                    pe.wait_ge(R["q0_made"], 2 * j + g + 1)
                    if g == 1:
                        pe.wait_ge(R["products_masked"], 2 * j + 2)
                    each(1 + g, g, inv_t16, eyes16).then_inc(R["r0_summed"], 1)

            def newton_v(j, level):
                for g in range(2):
                    if level == 1:
                        pe.wait_ge(R["r0_copied"], 2 * j + g + 1)
                    else:
                        pe.wait_ge(R["rq_copied"], 15 * j + 3 * (level - 2) + (1, 3)[g])
                    bk = pair[level % 2][g]
                    mm(bank[bk][:], two16[:], eyes4, start=True, stop=False, skip_group_check=True)
                    each(bk, g, nix16, inv16, start=False).then_inc(R["v_summed"], 1)

            def newton_r(j, level):
                for g in range(2):
                    pe.wait_ge(R["v_copied"], 10 * j + 2 * (level - 1) + g + 1)
                    if g == 0 and level == 1:
                        pe.wait_ge(R["r0_copied"], 2 * j + 2)
                    if g == 0 and level > 1:
                        pe.wait_ge(R["rq_copied"], 15 * j + 3 * (level - 1))
                        pe.wait_ge(R["q1_copied"], 5 * j + level - 1)
                    banks = pair[(level + 1 + g) % 2]
                    if g == 1:
                        pe.wait_ge(R["v_copied"], 10 * j + 2 * level)
                    each(banks[0], g, inv_t16, w16).then_inc(R["rq_summed"], 1)
                    each(banks[1], g, w16, inv_t16).then_inc(R["rq_summed"], 1)

            def residual(j):
                pe.wait_ge(R["low_made"], 2 * j + 2)
                for g in range(2):
                    pe.wait_ge(R["rq_copied"], 15 * j + (14, 15)[g])
                    mm(bank[1 + g][:], one16[:], eyes4, start=True, stop=False, skip_group_check=True)
                    each(1 + g, g, nixlo16, inv16, start=False, stop=False)
                    each(1 + g, g, nix16, inv16, start=False).then_inc(R["e_summed"], 1)

            def last_inverse(j):
                pe.wait_ge(R["q1_copied"], 5 * j + 5)
                for g in range(2):
                    pe.wait_ge(R["e_copied"][g], j + 1)
                    for c in range(4):
                        where = bank[3 * g][:, c * P:(c + 1) * P]
                        mm(where, inv16[:, 4 * g + c, :], eyes16[:, 0, :], start=True, stop=False)
                        last = mm(where, w16[:, 4 * g + c, :], inv_t16[:, 4 * g + c, :], start=False, stop=True)
                    last.then_inc(R["t_summed"], 1)

            pe.wait_ge(s_const, 3)
            for j in range(CI + 2):
                for s in range(3 * NCH):
                    if when(j - 1, CI):
                        chain(j - 1, (j - 1) % 2, s // 3, s % 3)
                    if when(j, CI):
                        if s in (0, 1, 4, 5):
                            for c in range(2):
                                products(j, j % 2, 2 * (s % 4) + 4 * (s // 4) + c)
                        elif s == S_NEWTON - 1:
                            first_inverse(j)
                        elif S_NEWTON <= s < S_NEWTON + 10:
                            (newton_r if (s - S_NEWTON) % 2 else newton_v)(j, (s - S_NEWTON) // 2 + 1)
                        elif s == S_NEWTON + 10:
                            residual(j)
                        elif s == S_NEWTON + 11:
                            last_inverse(j)
                    if when(j - 2, CI):
                        if s == 2:
                            pe.wait_ge(R["y_bank_read"], j - 1)
                            mm(bank[4][:], center[:], y0[:], start=True, stop=True).then_inc(R["centered"], 1)
                        if s == 6:
                            pe.wait_ge(R["centered_copied"], j - 1)
                            pe.wait_ge(R["y_squared"], j - 1)
                            mm(bank[4][:], head_mean[:], ysq[:], start=True, stop=True).then_inc(R["var_summed"], 1)

        def recurrence_evac(eng, h, j, b, c, phase):
            hs = slice(h * C, (h + 1) * C)
            scaled = (lambda o_, i_, f: nc.vector.tensor_scalar(o_, i_, f, None, ALU.mult)) if h == 0 else \
                     (lambda o_, i_, f: nc.scalar.activation(o_, i_, ACT.Copy, scale=f))
            if phase == 0:
                eng.wait_ge(R["rhs_summed"], NCH * j + c + 1)
                scaled(rhs[hs, :], bank[5][hs, 0:C], 1.0).then_inc(R["rhs_copied"][h], 1)
            elif phase == 1:
                eng.wait_ge(R["u_summed"], NCH * j + c + 1)
                scaled(sv[b][hs, c, h, :], bank[5][hs, C:2 * C], -1.0).then_inc(R["u_copied"][h], 1)
            elif c < NCH - 1:
                eng.wait_ge(R["s_summed"], NCH * j + c + 1)
                scaled(sv[b][hs, c + 1, h, :], bank[6][hs, 0:C], st_pc[j % 3][hs, c:c + 1]).then_inc(R["s_copied"][h], 1)

        def blocks(bk):
            return bank[bk][:].rearrange("p (c k) -> p c k", c=4)

        def recurrence_scalar(act, o):
            A = nc.scalar.activation
            act.wait_ge(s_const, 3)
            for j in range(CI + 2):
                b = j % 2
                for s in range(3 * NCH):
                    if s == 0 and when(j - 2, CI):
                        act.wait_ge(R["y_summed"], j - 1)
                        A(y0[:], bank[7][:], ACT.Copy).then_inc(R["y_bank_read"], 1)
                    if when(j - 1, CI):
                        recurrence_evac(act, 1, j - 1, 1 - b, s // 3, s % 3)
                    if when(j, CI):
                        if s in (1, 5):
                            g = s // 4
                            act.wait_ge(R["turned"], 2 * j + g + 1)
                            o(A(bt[b][:, 4 * g:4 * g + 4, :], bank[0][:].rearrange("p (c k) -> p c k", c=4), ACT.Copy))
                            v = bank[1][:].rearrange("p (c k) -> p c k", c=4)
                            o(A(sv[b][0:C, 4 * g:4 * g + 4, 1, :], v[0:C, :, C:P], ACT.Copy))
                            n = 4 - g
                            copy = A(sv[b][C:P, 4 * g + 1:4 * g + 1 + n, 0, :], v[C:P, 0:n, 0:C], ACT.Copy)
                            if g == 1:
                                o(copy)
                                copy = A(sv[b][C:P, 0, 0, :], v[C:P, 3, 0:C], ACT.Copy)
                            copy.then_inc(R["turned_copied"], 1)
                            if g == 1:
                                act.wait_ge(R["turned_copied"], 2 * j + 2)
                                A(sv[b][C:P, 0, 1, :], sv[b][C:P, 0, 0, :], ACT.Copy, scale=0.0).then_inc(
                                    R["state_zeroed"][1], 1)
                        elif s == S_NEWTON - 1:
                            for g in range(2):
                                act.wait_ge(R["r0_summed"], 2 * j + g + 1)
                                A(inv16[:, 4 * g:4 * g + 4, :], blocks(1 + g), ACT.Copy).then_inc(R["r0_copied"], 1)
                        elif S_NEWTON <= s < S_NEWTON + 10 and (s - S_NEWTON) % 2:
                            level = (s - S_NEWTON + 1) // 2
                            first, second = ((1, 2), (0, 3)) if level % 2 else ((0, 3), (1, 2))
                            for n, (dst, bk) in enumerate(((inv16[:, 0:4, :], first[0]), (inv_t16[:, 0:4, :], first[1]),
                                                           (inv16[:, 4:8, :], second[0]))):
                                act.wait_ge(R["rq_summed"], 20 * j + 4 * (level - 1) + n + 1)
                                A(dst, blocks(bk), ACT.Copy).then_inc(R["rq_copied"], 1)
                        elif s == S_NEWTON + 10:
                            act.wait_ge(R["e_summed"], 2 * j + 1)
                            A(w16[:, 0:4, :], blocks(1), ACT.Copy).then_inc(R["e_copied"][0], 1)
                        elif s == S_NEWTON + 11:
                            act.wait_ge(R["t_summed"], 2 * j + 1)
                            A(tt[b][:, 0:4, :], blocks(0), ACT.Copy).then_inc(R["inverse_made"][0], 1)
                    if when(j - 2, CI):
                        if s == 2:
                            act.wait_ge(R["centered"], j - 1)
                            if j >= 3:
                                act.wait_ge(R["y_finished"], j - 2)
                            A(yc[:], bank[4][:], ACT.Copy).then_inc(R["centered_copied"], 1)
                            act.wait_ge(R["centered_copied"], j - 1)
                            A(ysq[:], yc[:], ACT.Square).then_inc(R["y_squared"], 1)
                        if s == 7:
                            act.wait_ge(R["var_summed"], j - 1)
                            o(A(yr[:], bank[4][:], ACT.Ln, bias=eps[:, 1:2]))
                            A(yr[:], yr[:], ACT.Exp, scale=-0.5).then_inc(R["y_rstd_made"], 1)

        def recurrence_vector(dve, o):
            V = nc.vector
            incl, strict = masks[:, 0:C], masks[:, P:P + C]
            dve.wait_ge(s_const, 4)

            def wide(m, lo, hi, n):
                return m[lo:hi].unsqueeze(1).to_broadcast([hi - lo, n, C])

            for j in range(CI + 2):
                b = j % 2
                for s in range(3 * NCH):
                    if when(j - 1, CI):
                        recurrence_evac(dve, 0, j - 1, 1 - b, s // 3, s % 3)
                    if not when(j, CI):
                        continue
                    TT = V.tensor_tensor
                    g = int(s >= 5)
                    cr = slice(4 * g, 4 * g + 4)
                    p0, p1 = (bank[2 + h][:].rearrange("p (c a k) -> p c a k", c=4, a=2) for h in range(2))
                    if s in (1, 5):
                        dve.wait_ge(R["products_summed"], 2 * j + g + 1)
                        for hs, p in ((slice(0, C), p0[0:C, :, 0, :]), (slice(C, P), p1[C:P, :, 1, :])):
                            V.scalar_tensor_tensor(out=nix[hs, cr, :], in0=p, scalar=-1.0,
                                                   in1=wide(strict, hs.start, hs.stop, 4), op0=ALU.mult,
                                                   op1=ALU.mult).then_inc(R["nix_made"], 1)
                    if s in (2, 6):
                        for h in range(2):
                            hs = slice(h * C, (h + 1) * C)
                            dve.wait_ge(R["nix_made"], 4 * j + 2 * g + h + 1)
                            TT(nix16[hs, cr, hs], nix[hs, cr, :], eyes[hs, cr, :], ALU.subtract).then_inc(
                                R["nix16_made"], 1)
                    if s in (4, 7):
                        g = s // 7
                        cr = slice(4 * g, 4 * g + 4)
                        dve.wait_ge(R["nix16_made"], 4 * j + 2 * g + 2)
                        TT(inv_t16[:, cr, :], nix16[:, cr, :],
                           bmask[:, 0, :].unsqueeze(1).to_broadcast([P, 4, P]), ALU.mult).then_inc(R["q0_made"], 1)
                    if s in (2, 8):
                        TT(st_q[j % 3][C:P, cr, 0, :], p0[C:P, :, 0, :], wide(strict, C, P, 4), ALU.mult)
                        TT(st_q[j % 3][0:C, cr, 2, :], p1[0:C, :, 1, :], wide(strict, 0, C, 4), ALU.mult)
                    if s in (3, 8):
                        TT(ra[b][:, cr, 0, :], p0[:, :, 1, :], wide(incl, 0, P, 4), ALU.mult)
                        TT(ra[b][:, cr, 1, :], p1[:, :, 0, :], wide(incl, 0, P, 4), ALU.mult).then_inc(
                            R["products_masked"], 1)
                    if s == 8:
                        dve.wait_ge(R["products_masked"], 2 * j + 2)
                        V.memset(sv[b][0:C, 0, 0, :], 0.0).then_inc(R["state_zeroed"][0], 1)
                    if S_NEWTON <= s < S_NEWTON + 10 and (s - S_NEWTON) % 2 == 0:
                        level = (s - S_NEWTON) // 2 + 1
                        for g in range(2):
                            dve.wait_ge(R["v_summed"], 10 * j + 2 * (level - 1) + g + 1)
                            src = blocks(((1, 2), (0, 3))[level % 2][g])
                            dst = w16[:, 4 * g:4 * g + 4, :]
                            (TT(dst, src, bmask[:, level, :].unsqueeze(1).to_broadcast([P, 4, P]), ALU.mult)
                             if level < 5 else V.tensor_copy(dst, src)).then_inc(R["v_copied"], 1)
                    elif S_NEWTON <= s < S_NEWTON + 10:
                        level = (s - S_NEWTON + 1) // 2
                        dve.wait_ge(R["rq_summed"], 20 * j + 4 * level)
                        V.tensor_copy(inv_t16[:, 4:8, :], blocks(3 if level % 2 else 2)).then_inc(R["q1_copied"], 1)
                    elif s == S_NEWTON + 10:
                        dve.wait_ge(R["e_summed"], 2 * j + 2)
                        V.tensor_copy(w16[:, 4:8, :], blocks(2)).then_inc(R["e_copied"][1], 1)
                    elif s == S_NEWTON + 11:
                        dve.wait_ge(R["t_summed"], 2 * j + 2)
                        V.tensor_copy(tt[b][:, 4:8, :], blocks(3)).then_inc(R["inverse_made"][1], 1)

        def recurrence_gpsimd(gp, o):
            G = nc.gpsimd
            for j in range(CI + 2):
                b = j % 2
                if when(j - 2, CI):
                    gp.wait_ge(R["y_rstd_made"], j - 1)
                    gp.wait_ge(R["ends_loaded"][b], 32 * (j // 2))
                    o(G.tensor_tensor(y2[:], yc[:], yr[:], ALU.mult))
                    o(G.tensor_scalar(y2[:], y2[:], col("a_lnw", j - 2), col("a_lnb", j - 2), ALU.mult, ALU.add))
                    o(G.tensor_tensor(y2[:], y2[:], st_bv[b][:], ALU.add))
                    G.tensor_tensor(Y[:, j - 2, :], y2[:], st_g[b][:], ALU.mult).then_inc(R["y_finished"], 1)
                    gp.wait_ge(R["y_finished"], j - 1)
                if when(j, CI):
                    gp.wait_ge(R["q0_made"], 2 * j + 2)
                    o(G.tensor_tensor(nixe[:], nix[:], eyes[:], ALU.subtract))
                    for h in range(2):
                        hs = slice(h * C, (h + 1) * C)
                        G.tensor_tensor(nixlo16[hs, :, hs], nixe[hs], nix16[hs, :, hs], ALU.subtract).then_inc(
                            R["low_made"], 1)
                        gp.wait_ge(R["low_made"], 2 * j + h + 1)

        ITEMS = NHEAD2 * NT

        def item(m):
            h, n = m // NT, NT - 1 - m % NT
            return h, n, slice((h % 2) * C, (h % 2 + 1) * C), slice(n * P, T), slice(ATT_AT[n], ATT_AT[n + 1])

        def attention_tensor(pe):
            mm = nc.tensor.matmul

            def scores(m):
                h, n, rows, seen, _ = item(m)
                if m == 0:
                    pe.wait_ge(s_free[0], U_MERGE // 2)
                    pe.wait_ge(s_free[1], U_MERGE // 2)
                    pe.wait_ge(s_vtok, NT)
                    pe.wait_ge(s_lrs, 1)
                if m >= 4:
                    pe.wait_ge(s_neg, m - 3)
                mm(bank[m % 4][:, seen], kT[rows, h // 2, n * P:(n + 1) * P], qT[rows, h // 2, seen], start=True,
                   stop=True).then_inc(s_sc2, 1)

            def sums(m):
                h, n, _, seen, cols = item(m)
                pe.wait_ge(s_sp, m + 1)
                if m >= 2:
                    pe.wait_ge(s_dif, m - 1)
                last = mm(bank[4 + m % 2][:, seen], att_from[:], att_sp[:, h % 2, cols], start=True, stop=n == NT - 1)
                for later in range(n + 1, NT):
                    last = mm(bank[4 + m % 2][:, later * P:T], att_ones[:],
                              att_sp[:, h % 2, ATT_AT[later]:ATT_AT[later + 1]], start=False, stop=later == NT - 1)
                last.then_inc(s_cum, 1)

            def values(h):
                pe.wait_ge(s_wt, NT * (h + 1))
                if h >= 4:
                    pe.wait_ge(s_tmp, made(X_AT + h // 2 - 2))
                for n in range(NT):
                    last = mm(bank[6 + h // 2 % 2][(h % 2) * C:(h % 2 + 1) * C, n * P:T], vtok[:, n, h * C:(h + 1) * C],
                              att_a[:, h % 2, ATT_AT[n]:ATT_AT[n + 1]], start=n == 0, stop=n == NT - 1)
                last.then_inc(s_o, 1)

            for s in range(-1, ITEMS + 3):
                if when(s + 1, ITEMS):
                    scores(s + 1)
                if when(s - 1, ITEMS):
                    sums(s - 1)
                if when(s - 3, ITEMS) and (s - 3) % NT == NT - 1:
                    values((s - 3) // NT)

        def attention_scalar(act, o, x_high):
            A = nc.scalar.activation
            for s in range(ITEMS + 5):
                if when(s, ITEMS):
                    seen = item(s)[3]
                    z, t = att_z[s % 4][:, seen], sq[:, s % 2, seen]
                    act.wait_ge(s_sc2, s + 1)
                    if s >= 4:
                        act.wait_ge(s_dif, s - 3)
                    A(z, bank[s % 4][:, seen], ACT.Copy).then_inc(s_neg, 1)
                    act.wait_ge(s_neg, s + 1)
                    if s >= 2:
                        act.wait_ge(s_sp, s - 1)
                    o(A(t, z, ACT.Abs))
                    o(A(t, t, ACT.Exp, scale=-1.0))
                    A(t, t, ACT.Ln, bias=1.0).then_inc(s_log, 1)
                if when(s - 2, ITEMS):
                    h, n, _, seen, cols = item(s - 2)
                    t = att_a[:, h % 2, cols]
                    act.wait_ge(s_dif, s - 1)
                    A(t, t, ACT.Exp).then_inc(s_wt, 1)
                if when(s - 4, ITEMS) and (s - 4) % (2 * NT) == 2 * NT - 1:
                    pair = (s - 4) // (2 * NT)
                    x_high(X_AT + pair, ah[:, 0, pair, :], pair % 2)

        def attention_vector(dve, o, finish):
            V = nc.vector
            for s in range(ITEMS + 5):
                if when(s - 1, ITEMS):
                    m = s - 1
                    h, n, rows, seen, cols = item(m)
                    dve.wait_ge(s_log, m + 1)
                    o(V.scalar_tensor_tensor(out=att_sp[:, h % 2, cols], in0=att_z[m % 4][:, seen], scalar=0.0,
                                             in1=sq[:, m % 2, seen], op0=ALU.max, op1=ALU.add))
                    t = att_sp[:, h % 2, ATT_AT[n]:ATT_AT[n] + P]
                    V.tensor_tensor(t, t, att_keep[:], ALU.mult).then_inc(s_sp, 1)
                if when(s - 2, ITEMS):
                    m = s - 2
                    h, n, rows, seen, cols = item(m)
                    dve.wait_ge(s_cum, m + 1)
                    if m % NT == 0 and h >= 2:
                        dve.wait_ge(s_o, h - 1)
                    o(V.tensor_tensor(att_a[:, h % 2, cols], att_z[m % 4][:, seen], bank[4 + m % 2][:, seen],
                                      ALU.subtract))
                    t = att_a[:, h % 2, ATT_AT[n]:ATT_AT[n] + P]
                    V.scalar_tensor_tensor(out=t, in0=t, scalar=0.0, in1=att_drop[:], op0=ALU.min,
                                           op1=ALU.add).then_inc(s_dif, 1)
                if when(s - 4, ITEMS) and (s - 4) % (2 * NT) == 2 * NT - 1:
                    pair = (s - 4) // (2 * NT)
                    dve.wait_ge(s_o, 2 * pair + 2)
                    finish(pair, lambda where: V.tensor_copy(where, bank[6 + pair % 2][:]))

        def tail_sync(sp, panel):
            sp.wait_ge(R["y_finished"], CI)
            sp.dma_start(xT2[:], d_x).then_inc(s_back, 16)
            w_out1, w_conv, w_out_conv = i["a_w_out"][0], i["b_w_in"][0], i["b_w_out"][0]

            def even(base, turns, mat, row, nkb, col0, first=0):
                def turn(t):
                    for u in range(2):
                        panel(2 * t + (base + u + 2 * first), u, mat, row, nkb, t * (2 * P) + (col0 + (u + 2 * first) * P))
                repeat(sp, turns - first, turn)

            def pairs(base, turns, mat, nkb, col_a, col_b):
                def turn(t):
                    for u, c0 in enumerate((col_a, col_b)):
                        panel(2 * t + (base + u), u, mat, 0, nkb, t * P + c0)
                repeat(sp, turns, turn)

            even(U_OUT1, DK // 2, w_out1, 0, KB, 0, first=1)
            even(U_OUT1 + DK, DK // 2, w_out1, D, KB, 0)
            for half in range(2):
                base = U_CONV + half * (4 * KB + DK)

                def conv(t):
                    for u, part in enumerate((0, 2, 3, 1)):
                        panel(4 * t + (base + u), u % 2, w_conv, 0, KB, t * P + (part * DI + half * D))
                repeat(sp, KB, conv)
                even(base + 4 * KB, DK // 2, w_out_conv, half * D, KB, 0)
            w2 = i["w_in_2"]
            pairs(U_GLU, CT, w2, KB, 0, CT * P)
            even(U_QKV, 3 * AT // 2, w2, 0, KB, 2 * CT * P)
            gate_col = 2 * CT * P + 3 * AD
            pairs(U_GATES2, DK, w2, KB, gate_col, gate_col + D)

            def merge(t):
                for u in range(2):
                    n, c0 = 2 * t + (U_MERGE + u), t * (2 * P) + u * P
                    panel(n, u, i["w_conv_branch_2"], 0, CT, c0)
                    panel(n, u, i["w_att_branch_2"], 0, AT, c0, kb0=CT, first=False)
            repeat(sp, DK // 2, merge)
            even(U_WOUT2, DK // 2, i["w_out_2"], 0, KB, 0)
            base = U_FFN
            for j0, n in FPARTS:
                pairs(base, n, i["w_ffn_up_2"], KB, j0 * P, (FT + j0) * P)
                even(base + 2 * n, DK // 2, i["w_ffn_down_2"], j0 * P, n, 0)
                base += 2 * n + DK
            for q in range(NT):
                for half in range(2):
                    sp.wait_ge(s_yc[half], q + 1)
                sp.dma_start(out[0, q * P:(q + 1) * P, :], staged[:, q, :]).then_inc(s_out, 16)
            sp.wait_ge(s_out, 16 * NT)

        @block.sync
        def _(sp):
            def panel(n, slot, mat, row, nkb, col, ncol=P, kb0=0, first=True, rows=P):
                if first and not (isinstance(n, int) and n < 2):
                    sp.wait_ge(s_lo, n - 1)
                src = mat[row:row + nkb * rows, bass.ds(col, ncol)].rearrange("(k p) c -> p k c", p=rows)
                sp.dma_start(w_raw[0:rows, slot, kb0:kb0 + nkb, 0:ncol], src).then_inc(s_raw[slot], 16)

            sp.dma_start(x_raw[:], i["x"].rearrange("b (q p) d -> p (b q) d", p=P)).then_inc(s_xin, 16)
            panel(0, 0, i["a_w1"][0], 0, KB, 0, LORA)
            panel(1, 1, i["a_a1"][0], 0, KB, 0, LORA)

            def gate(t, u):
                panel(2 * t + (U_GATE + u), u, w_in[3], 0, KB, t * (2 * P) + u * P)

            def spill_gate(t, u):
                sp.wait_ge(s_free[u], t + 2)
                sp.dma_start(d_g[2 * t + u], sq[:, u, :]).then_inc(s_spill, 16)

            def mix(j, u):
                if u == 0:
                    panel(4 * j + U_MIX, 0, i["a_w2"][0], 0, 1, j * P, rows=LORA)
                    panel(4 * j + U_MIX, 0, i["a_a2"][0], 0, 1, j * P, kb0=1, first=False, rows=LORA)
                else:
                    panel(4 * j + (U_MIX + u), u % 2, w_in[(None, 1, 0, 2)[u]], 0, KB, j * P)

            def spill_mix(j):
                sp.wait_ge(s_free[0], 2 * j + (FREE_MIX + 2))
                sp.dma_start(d_r[j], o_r[:]).then_inc(s_spill, 16)
                sp.dma_start(d_pc[j], o_pc[:]).then_inc(s_spill, 16)
                for n, (dst, src) in enumerate(((d_q, o_q), (d_b, o_b), (d_c, o_c))):
                    sp.wait_ge(s_fin, 4 * j + (n + 1))
                    sp.dma_start(dst[j], src[:]).then_inc(s_spill, 16)
                sp.wait_ge(s_free[1], 2 * j + (FREE_MIX + 2))
                sp.dma_start(d_v[j], o_v[:]).then_inc(s_spill, 16)
                sp.wait_ge(s_fin, 4 * j + 4)
                sp.dma_start(d_bv[j], o_bv[:]).then_inc(s_spill, 16)

            sp.wait_ge(s_xt, DK)
            sp.dma_start(d_x, xT[:]).then_inc(s_spill, 16)
            for u in range(4):
                gate(u // 2, u % 2)

            def gate_turn(t):
                for u in range(2):
                    spill_gate(t, u)
                    gate(t + 2, u)
            repeat(sp, CI // 2 - 2, gate_turn)
            for u in range(4):
                spill_gate(CI // 2 - 2 + u // 2, u % 2)
                mix(0, u)

            def mix_turn(j):
                for u in range(4):
                    if u == 3:
                        spill_mix(j)
                    mix(j + 1, u)
            repeat(sp, CI - 1, mix_turn)
            panel(U_OUT1, 0, i["a_w_out"][0], 0, KB, 0)
            spill_mix(CI - 1)
            panel(U_OUT1 + 1, 1, i["a_w_out"][0], 0, KB, P)

            def load(j):
                b, b3 = j % 2, j % 3
                if j >= 2:
                    sp.wait_ge(R["turned"], 2 * (j - 1))
                if j >= 3:
                    sp.wait_ge(R["y_summed"], j - 2)
                half = lambda a, h: a[j, h * C:(h + 1) * C, :].rearrange("p (c t) -> p c t", c=NCH)
                for h, (slot_b, slot_c) in enumerate(((0, 1), (1, 0))):
                    hs = slice(h * C, (h + 1) * C)
                    for dst, src in ((st_q[b3][hs, :, 2 * h, :], d_q), (st_bc[b][hs, :, slot_b, :], d_b),
                                     (st_bc[b][hs, :, slot_c, :], d_c)):
                        sp.dma_start(dst, half(src, h)).then_inc(R["tiles_loaded"][b], 16)
                whole = d_r[j].rearrange("p (c t) -> p c t", c=NCH)
                for dst, src in ((st_q[b3][:, :, 1, :], whole), (st_v[b][:, 0:T], d_v[j]),
                                 (st_v[b][:, T:T + C], d_v[j, :, 0:C]), (st_pc[b3][:], d_pc[j])):
                    sp.dma_start(dst, src).then_inc(R["tiles_loaded"][b], 16)

            sp.wait_ge(s_spill, SPILL_MIX + SPILL_TILE * CI)
            sp.wait_ge(s_unit, U_OUT1)
            load(0)
            load(1)
            for j in range(CI):
                if j >= 2:
                    sp.wait_ge(R["y_finished"], j - 1)
                sp.dma_start(st_bv[j % 2][:], d_bv[j]).then_inc(R["ends_loaded"][j % 2], 16)
                sp.dma_start(st_g[j % 2][:], d_g[j]).then_inc(R["ends_loaded"][j % 2], 16)
                if j + 2 < CI:
                    load(j + 2)
            tail_sync(sp, panel)

        @block.gpsimd
        def _(gp):
            o = Order(gp, s_gseq)
            gt = nc.gpsimd
            o(gt.memset(ident[:], 0.0))
            o(gt.affine_select(out=ident[:], in_=ident[:], compare_op=ALU.not_equal, fill=1.0, base=0,
                               pattern=[[-1, P]], channel_multiplier=1))
            o(gt.memset(mean_d[:], 1.0 / D))
            o(gt.memset(head_ones[:], 0.0))
            o(gt.memset(head_ones[0:C, 0:C], 1.0))
            o(gt.memset(head_ones[C:P, C:P], 1.0))
            o(gt.memset(eps[:, 0:1], RMS_EPS))
            o(gt.memset(eps[:, 1:2], GN_EPS))
            o(gt.memset(eps[:, 2:3], 0.5 * NSHIFT * LN2))
            o(gt.memset(masks[:], 1.0))
            for m in (att_ones, att_from, att_keep, att_drop):
                o(gt.memset(m[:], 0.0 if m is att_drop else 1.0))
            o(gt.affine_select(out=att_from[:], in_=att_from[:], compare_op=ALU.is_ge, fill=0.0, base=0,
                               pattern=[[-1, P]], channel_multiplier=1))
            o(gt.affine_select(out=att_keep[:], in_=att_keep[:], compare_op=ALU.is_gt, fill=0.0, base=0,
                               pattern=[[1, P]], channel_multiplier=-1))
            o(gt.affine_select(out=att_drop[:], in_=att_drop[:], compare_op=ALU.is_gt, fill=-1e30, base=0,
                               pattern=[[1, P]], channel_multiplier=-1))
            for h in range(2):
                hs = slice(h * C, (h + 1) * C)
                incl = masks[hs, 0:P].rearrange("p (a t) -> p a t", a=2)
                o(gt.affine_select(out=incl, in_=incl, compare_op=ALU.is_ge, fill=0.0, base=0,
                                   pattern=[[0, 2], [1, C]], channel_multiplier=-1))
                o(gt.affine_select(out=masks[hs, P:P + C], in_=masks[hs, P:P + C], compare_op=ALU.is_gt,
                                   fill=0.0, base=0, pattern=[[1, C]], channel_multiplier=-1))
            gt.memset(hT[:, :, 0:1], 0.0).then_inc(s_const, 1)
            gp.wait_ge(s_xlo, X_Y)
            o(gt.memset(scanm[:], 1.0))
            o(gt.memset(scanm[:, :, 0:1], 0.0))
            gt.memset(lw[:, :, 0:1], 0.0).then_inc(s_const, 1)

            gp.wait_ge(s_spill, 16)
            o(gt.memset(bmask[:], 1.0))
            for n, m in enumerate((2, 4, 8, 16, 32)):
                v = bmask[:, n, :].rearrange("p (a b) -> p a b", b=m)
                o(gt.affine_select(out=v, in_=v, compare_op=ALU.is_ge, fill=0.0, base=0,
                                   pattern=[[-m, P // m], [0, m]], channel_multiplier=1))
                o(gt.affine_select(out=v, in_=v, compare_op=ALU.is_ge, fill=0.0, base=m - 1,
                                   pattern=[[m, P // m], [0, m]], channel_multiplier=-1))
            o(gt.affine_select(out=bmask[:, 0, :], in_=bmask[:, 0, :], compare_op=ALU.not_equal, fill=-1.0, base=0,
                               pattern=[[-1, P]], channel_multiplier=1))
            o(gt.memset(eyes[:], 0.0))
            for h in range(2):
                v = eyes[h * C:(h + 1) * C]
                o(gt.affine_select(out=v, in_=v, compare_op=ALU.not_equal, fill=1.0, base=0,
                                   pattern=[[0, NCH], [-1, C]], channel_multiplier=1))
            for c in range(4):
                o(gt.tensor_copy(eyes16[:, c, :], ident[:]))
            o(gt.tensor_copy(one16[:], ident[:]))
            o(gt.tensor_scalar(two16[:], ident[:], 2.0, 0.0, ALU.mult, ALU.add))
            o(gt.tensor_scalar(head_mean[:], head_ones[:], 1.0 / C, 0.0, ALU.mult, ALU.add))
            gt.tensor_tensor(center[:], ident[:], head_mean[:], ALU.subtract).then_inc(s_const, 1)
            gp.wait_ge(s_unit, U_OUT1)
            o(gt.memset(nix16[:], 0.0))
            gt.memset(nixlo16[:], 0.0).then_inc(s_const, 1)
            recurrence_gpsimd(gp, o)
            gp.wait_ge(s_free[0], U_QKV // 2)
            y = dconv[:, CT - 1, :]
            o(gt.tensor_scalar(y, glu[:, CT - 1, 0:T], col("conv_dw_w_2", CT - 1), col("conv_dw_b_2", CT - 1), ALU.mult,
                               ALU.add))
            for tap in range(1, TAPS2):
                o(gt.tensor_scalar(tapped[:], glu[:, CT - 1, tap:tap + T], col("conv_dw_w_2", tap * CT + CT - 1), None,
                                   ALU.mult))
                ins = gt.tensor_tensor(y, y, tapped[:], ALU.add)
                ins.then_inc(s_tap3, 1) if tap == TAPS2 - 1 else o(ins)

        @block.scalar
        def _(act):
            o = Order(act, s_aseq)
            A = nc.scalar.activation
            nc.scalar.add_instruction(mybir.InstLoadActFuncSet(
                name=nc.get_next_instruction_name(), act_func_set_id=EXP_LN_SET, ins=[], outs=[]))
            for t, rows in enumerate(PARAMS):
                row = 0
                for name, n in rows:
                    src = i[name]
                    letters = " ".join("abcd"[:len(src.shape)])
                    flat = src.rearrange(f"{letters} -> ({letters})") if len(src.shape) > 1 else src
                    act.dma_start(par_raw[row:row + n, t, :], flat.rearrange("(r c) -> r c", c=P)).then_inc(s_par, 16)
                    row += n

            def w_high(n, slot, count, ncol=P):
                act.wait_ge(s_raw[slot], count)
                if not (isinstance(n, int) and n < 2):
                    act.wait_ge(s_unit, n - 1)
                A(w_hi[:, slot, :, 0:ncol], w_raw[:, slot, :, 0:ncol], ACT.Copy).then_inc(s_hi, 1)

            def x_high(q, hi, buf):
                act.wait_ge(s_tmp, made(q))
                A(hi, tmp[:, buf, :], ACT.Copy).then_inc(s_xhi, 1)

            def sigmoid(z):
                o(A(z, z, ACT.Exp, scale=-1.0))
                o(A(z, z, ACT.Ln, bias=1.0))
                return A(z, z, ACT.Exp, scale=-1.0)

            def norm(n, x=xT, ready=None):
                for k in range(DK if x is not None else 0):
                    if ready is not None:
                        act.wait_ge(*ready(k))
                    if n or k >= 2:
                        act.wait_ge(s_sqa, n * DK + k - 1)
                    A(sq[:, k % 2, :], x[:, k, :], ACT.Square).then_inc(s_sq, 1)
                act.wait_ge(s_ms, n + 1)
                o(A(rstd[:, 0, :], bank[4][:], ACT.Ln, bias=eps[:, 0:1]))
                A(rstd[:, 1, :], rstd[:, 0, :], ACT.Exp, scale=-0.5).then_inc(s_rs, 1)

            for k in range(DK):
                act.wait_ge(s_tr, k + 1)
                A(xT[:, k, :], bank[k % 4][:], ACT.Copy).then_inc(s_xt, 1)
            act.wait_ge(s_const, 1)
            act.wait_ge(s_xt, DK)
            norm(0)
            w_high(0, 0, panels_by(0), LORA)
            w_high(1, 1, panels_by(1), LORA)
            for k in range(DK):
                x_high(2 * k, xl[0][:, 0, k, :], 0)
                x_high(2 * k + 1, xl[1][:, 0, k, :], 1)
            for k in range(DK):
                x_high(X_G + k, xh[:, 0, k, :], k % 2)
            act.wait_ge(s_free[0], 1)
            z = rstd[0:LORA, 0, :]
            o(A(z, z, ACT.Exp, scale=-2.0))
            o(A(z, z, ACT.Ln, bias=1.0))
            A(z, z, ACT.Exp, scale=-1.0).then_inc(s_lsig, 1)
            w_high(U_GATE, 0, panels_by(U_GATE))
            act.wait_ge(s_spill, 16)
            act.wait_ge(s_lhid, 1)
            A(lora[:, 0, 0, :], rstd[0:LORA, 0, :], ACT.Copy).then_inc(s_lhi, 1)
            act.wait_ge(s_free[1], 1)
            A(lora[:, 1, 0, :], rstd[0:LORA, 1, :], ACT.Copy).then_inc(s_lhi, 1)

            def gate(t):
                for u in range(2):
                    w_high(2 * t + (U_GATE + u + 1), 1 - u, panels(U_GATE, 2, t, u + 1))
                    act.wait_ge(s_z, 2 * t + (u + 1))
                    sigmoid(rstd[:, u, :]).then_inc(s_sg, 1)
                    for n in (range(2) if u == 0 else range(2, 3)):
                        x_high(3 * t + (X_RKV + n), xl[n][:, 0, bass.ds(t, 1), :], n % 2)
            repeat(act, CI // 2 - 1, gate, o, 4)
            gate(CI // 2 - 1)

            def mix(j):
                n0 = 4 * j + U_MIX
                w_high(n0 + 1, 1, panels(U_MIX, 4, j, 1))
                act.wait_ge(s_zw, j + 1)
                sigmoid(zw[:]).then_inc(s_sw, 1)
                act.wait_ge(s_free[0], 2 * j + (FREE_MIX + 1))
                sigmoid(za[:]).then_inc(s_sa, 1)
                w_high(n0 + 2, 0, panels(U_MIX, 4, j, 2))
                act.wait_ge(s_kk, j + 1)
                A(sqk[:], kk[:], ACT.Square).then_inc(s_sqk, 1)
                act.wait_ge(s_cs, j + 1)
                act.wait_ge(s_spill, j * SPILL_TILE + SPILL_MIX)
                o(A(pw[:], cs[:], ACT.Exp))
                A(o_pc[:], cs[:, :, C], ACT.Exp)
                A(pinv[:], cs[:], ACT.Exp, scale=-1.0).then_inc(s_pw, 1)
                w_high(n0 + 3, 1, panels(U_MIX, 4, j, 3))
                act.wait_ge(s_n2m, j + 1)
                o(A(n2[:], n2[:], ACT.Ln, scale=float(2 ** NSHIFT)))
                A(rn[:], n2[:], ACT.Exp, scale=-0.5, bias=eps[:, 2:3]).then_inc(s_rn, 1)
                w_high(n0 + 4, 0, panels(U_MIX, 4, j, 4))
                act.wait_ge(s_unit, n0 + 4)
                A(o_v[:], bank[1][:], ACT.Copy).then_inc(s_free[1], 1)
            repeat(act, CI - 1, mix, o, 6)
            mix(CI - 1)
            recurrence_scalar(act, o)

            act.wait_ge(R["y_finished"], CI)
            for k in range(CI):
                A(xl[k // DK][:, 0, k % DK, :], Y[:, k, :], ACT.Copy).then_inc(s_xhi, 1)

            def ahead(base, per, t, u, last=False):
                n = panels(base, per, t, u + 1) if not last else panels_by(base + per * t + u + 1)
                w_high(per * t + (base + u + 1), (u + 1) % 2, n)

            def even(base, turns, x=None, n=None, final=False):
                def turn(t, last=False):
                    for u in range(2):
                        if not (last and u == 1):
                            ahead(base, 2, t, u)
                        if x is not None:
                            act.wait_ge(s_free[u], t + (base // 2 + 1))
                            act.wait_ge(s_sqa, 2 * t + (n * DK + u - 1))
                            A(sq[:, u, :], x[:, bass.ds(2 * t + u, 1), :], ACT.Square).then_inc(s_sq, 1)
                repeat(act, turns - final, turn)
                if final:
                    turn(turns - 1, last=True)
            even(U_OUT1, DK // 2)
            even(U_OUT1 + DK, DK // 2, xT2, 1)

            norm(1, None)
            for k in range(DK):
                x_high(X_H2 + k, xl[2][:, 0, k, :], k % 2)
            for half in range(2):
                base = U_CONV + half * (4 * KB + DK)

                def conv(t):
                    for u in range(4):
                        ahead(base, 4, t, u)
                        if u == 2:
                            act.wait_ge(s_zc, t + (KB * half + 1))
                            sigmoid(gate3[:]).then_inc(s_sc, 1)
                    act.wait_ge(s_free[1], 2 * t + (base // 2 + 2))
                    A(xl[half][:, 0, bass.ds(t, 1), :], tmp[:, 0, :], ACT.Copy).then_inc(s_xhi, 1)
                repeat(act, KB, conv, o, 2)
                even(base + 4 * KB, DK // 2, *((xT2, 2) if half else ()))

            norm(2, None)
            norm(3, xT2, lambda k: (s_xn, k + 1))
            for k in range(DK):
                x_high(X_H3 + k, xh[:, 0, k, :], k % 2)
            for j in range(CT):
                ahead(U_GLU, 2, j, 0)
                ahead(U_GLU, 2, j, 1)
                act.wait_ge(s_free[1], U_GLU // 2 + j + 1)
                sigmoid(rstd[:, j % 2, :]).then_inc(s_glu, 1)
            for n in range(3 * AT):
                ahead(U_QKV, 2, n // 2, n % 2)
            for q in range(NT):
                act.wait_ge(s_vt, q + 1)
                A(vtok[:, q, :], bank[2 + q][:], ACT.Copy).then_inc(s_vtok, 1)
            for n in range(2 * DK):
                ahead(U_GATES2, 2, n // 2, n % 2, last=True)
                act.wait_ge(s_free[n % 2], U_GATES2 // 2 + n // 2 + 1)
                sigmoid(gates[:, n % 2, n // 2, :]).then_inc(s_gate2, 1)
            for j in range(CT):
                act.wait_ge(s_cen, j + 1)
                if j >= 2:
                    act.wait_ge(s_lacc, j - 1)
                A(sq[:, j % 2, :], dconv[:, j, :], ACT.Square).then_inc(s_lsq, 1)
            act.wait_ge(s_lnm, 2)
            o(A(rstd[:, 0, :], bank[4][:], ACT.Ln, bias=eps[:, 0:1], scale=2.0))
            A(rstd[:, 1, :], rstd[:, 0, :], ACT.Exp, scale=-0.5).then_inc(s_lrs, 1)
            for j in range(CT):
                act.wait_ge(s_lz, j + 1)
                sigmoid(sq[:, j % 2, :]).then_inc(s_ls, 1)
                x_high(X_UC + j, uc[:, 0, j, :], j % 2)
            attention_scalar(act, o, x_high)
            for n in range(DK):
                ahead(U_MERGE, 2, n // 2, n % 2, last=True)
                x_high(X_MG + n, xh[:, 0, n, :], n % 2)
            even(U_WOUT2, DK // 2, mixed, 4)
            norm(4, None)
            norm(5, xT2, lambda k: (s_mg, k + 1))
            for k in range(DK):
                x_high(X_H4 + k, xl[0][:, 0, k, :], k % 2)
            base = U_FFN
            for part, (j0, n) in enumerate(FPARTS):
                dst = xl[1 + part % 2]

                def ffn(t):
                    ahead(base, 2, t, 0)
                    act.wait_ge(s_ug, t + (j0 + 1))
                    sigmoid(rstd[:, 0, :]).then_inc(s_us, 1)
                    ahead(base, 2, t, 1)
                    act.wait_ge(s_free[1], t + (base // 2 + 1))
                    A(dst[:, 0, bass.ds(t, 1), :], tmp[:, 0, :], ACT.Copy).then_inc(s_xhi, 1)
                repeat(act, n, ffn, o, 2)
                last = part == len(FPARTS) - 1
                even(base + 2 * n, DK // 2, *((ffo, 6) if last else ()), final=last)
                base += 2 * n + DK
            norm(6, None)
            for k in range(NT):
                act.wait_ge(s_yt, 2 * k + 2)
                A(staged[:, k, T:D], bank[(2 * k + 1) % 8][:], ACT.Copy).then_inc(s_yc[1], 1)

        @block.tensor
        def _(pe):
            mm, tr = nc.tensor.matmul, nc.tensor.transpose

            def three(outp, wh, wl, xhi, xlo, start, stop):
                mm(outp, wh, xlo, start=start, stop=False)
                mm(outp, wl, xhi, start=False, stop=False)
                return mm(outp, wh, xhi, start=False, stop=stop)

            def unit(n, slot, x, nkb=KB, m=P, kx=0, xcount=None, free=None):
                pe.wait_ge(s_lo, n + 1)
                if not (isinstance(n, int) and n < 2):
                    pe.wait_ge(s_free[slot], free)
                for k in range(nkb):
                    if xcount is not None:
                        pe.wait_ge(s_xlo, xcount(k))
                    last = three(bank[slot][0:m, :], w_hi[:, slot, k, 0:m], w_lo[:, slot, k, 0:m],
                                 x[:, 0, kx + k, :], x[:, 1, kx + k, :], k == 0, k == nkb - 1)
                last.then_inc(s_unit, 1)

            def norm(n):
                pe.wait_ge(s_sqa, (n + 1) * DK)
                mm(bank[4][:], mean_d[:], acc[:], start=True, stop=True).then_inc(s_ms, 1)

            pe.wait_ge(s_const, 1)
            pe.wait_ge(s_xin, 16)
            for k in range(DK):
                if k >= 4:
                    pe.wait_ge(s_xt, k - 3)
                for q in range(4):
                    last = tr(bank[k % 4][:, q * P:(q + 1) * P], x_raw[:, q, k * P:(k + 1) * P], ident[:])
                last.then_inc(s_tr, 1)
            pe.wait_ge(s_par, 16 * sum(len(rows) for rows in PARAMS))
            for t in range(4):
                n = PAR_ROWS[t]
                last = tr(bank[5][:, t * P:t * P + n], par_raw[0:n, t, :], ident[0:n, 0:n])
            last.then_inc(s_part, 1)
            norm(0)
            for n in range(2):
                unit(n, n, xl[n], m=LORA, xcount=lambda k: 2 * k + n + 1)

            def phase(base, per, turns, x, ready, nkb=KB):
                for u in range(per):
                    unit(base + u, u % 2, x, nkb=nkb, xcount=None if u else lambda k: ready + k + 1,
                         free=base // 2 + u // 2)

                def turn(t):
                    for u in range(per):
                        unit(per * t + (base + per + u), u % 2, x, nkb=nkb,
                             free=per // 2 * t + (base // 2 + per // 2 + u // 2))
                repeat(pe, turns - 1, turn)

            phase(U_GATE, 2, CI // 2, xh, X_G)

            def mix(j):
                n0 = 4 * j + U_MIX
                pe.wait_ge(s_lo, n0 + 1)
                pe.wait_ge(s_free[0], 2 * j + FREE_MIX)
                for n in range(2):
                    last = three(bank[2 * n][:], w_hi[0:LORA, 0, n, :], w_lo[0:LORA, 0, n, :],
                                 lora[:, n, 0, :], lora[:, n, 1, :], True, True)
                last.then_inc(s_unit, 1)
                unit(n0 + 1, 1, xl[0], free=2 * j + FREE_MIX)
                unit(n0 + 2, 0, xl[1], free=2 * j + (FREE_MIX + 1))
                pe.wait_ge(s_sqk, j + 1)
                mm(bank[4][:], head_ones[:], sqk[:], start=True, stop=True).then_inc(s_n2, 1)
                unit(n0 + 3, 1, xl[2], free=2 * j + (FREE_MIX + 1))
                pe.wait_ge(s_rk, j + 1)
                mm(bank[5][:], head_rk[:], rk[:], start=True, stop=True).then_inc(s_bon, 1)
            pe.wait_ge(s_xlo, X_Y)
            pe.wait_ge(s_lt, 2)
            repeat(pe, CI, mix)
            recurrence_tensor(pe)

            for half in range(2):
                phase(U_OUT1 + half * DK, 2, DK // 2, xl[half], X_Y + DK * half)
            norm(1)
            for half in range(2):
                base = U_CONV + half * (4 * KB + DK)
                phase(base, 4, KB, xl[2], X_H2)
                phase(base + 4 * KB, 2, DK // 2, xl[half], X_YC + KB * half)
            norm(2)
            norm(3)
            phase(U_GLU, 2, CT + 3 * AT // 2, xh, X_H3)
            v_ch = [sq[:, 0, :], sq[:, 1, :], rstd[:, 0, :], rstd[:, 1, :]]
            pe.wait_ge(s_free[1], (U_GATES2 - 1) // 2 + 1)
            for q in range(NT):
                for n in range(AT):
                    last = tr(bank[2 + q][:, n * P:(n + 1) * P], v_ch[n][:, q * P:(q + 1) * P], ident[:])
                last.then_inc(s_vt, 1)
            phase(U_GATES2, 2, DK, xh, X_H3)
            pe.wait_ge(s_dc, 2)
            mm(bank[4][:], mean_d[:], acc[:], start=True, stop=True).then_inc(s_lnm, 1)
            pe.wait_ge(s_lacc, CT)
            mm(bank[4][:], mean_d[:], acc[:], start=True, stop=True).then_inc(s_lnm, 1)
            attention_tensor(pe)
            for n in range(DK):
                pe.wait_ge(s_lo, U_MERGE + n + 1)
                pe.wait_ge(s_free[n % 2], (U_MERGE + n) // 2)
                if n == 0:
                    pe.wait_ge(s_xlo, X_AT + AT)
                for part, (x, where) in enumerate(((uc, bank[n % 2]), (ah, bank[2 + n % 2]))):
                    for k in range(4):
                        kb = 4 * part + k
                        last = three(where[:], w_hi[:, n % 2, kb, :], w_lo[:, n % 2, kb, :], x[:, 0, k, :],
                                     x[:, 1, k, :], k == 0, k == 3)
                last.then_inc(s_unit, 1)
            phase(U_WOUT2, 2, DK // 2, xh, X_MG)
            norm(4)
            norm(5)
            base = U_FFN
            for part, (j0, n) in enumerate(FPARTS):
                phase(base, 2, n, xl[0], X_H4)
                phase(base + 2 * n, 2, DK // 2, xl[1 + part % 2], X_FF + j0, nkb=n)
                base += 2 * n + DK
            norm(6)
            pe.wait_ge(s_ffn, DK)
            for q in range(NT):
                for half in range(2):
                    b = 2 * q + half
                    if b == 4:
                        pe.wait_ge(s_rs, 7)
                    for k in range(4):
                        last = tr(bank[b][:, k * P:(k + 1) * P], xT2[:, 4 * half + k, q * P:(q + 1) * P], ident[:])
                    last.then_inc(s_yt, 1)

        @block.vector
        def _(dve):
            o = Order(dve, s_vseq)
            V = nc.vector

            def w_low(n, slot, ncol=P):
                dve.wait_ge(s_hi, n + 1)
                V.tensor_tensor(w_lo[:, slot, :, 0:ncol], w_raw[:, slot, :, 0:ncol],
                                w_hi[:, slot, :, 0:ncol].bitcast(F32), ALU.subtract).then_inc(s_lo, 1)

            def x_low(q, lo, hi, buf):
                dve.wait_ge(s_xhi, q + 1)
                V.tensor_tensor(lo, tmp[:, buf, :], hi.bitcast(F32), ALU.subtract).then_inc(s_xlo, 1)

            def norm(n, gain, dst, x=xT, summed=False):
                for k in range(0 if summed else DK):
                    dve.wait_ge(s_sq, n * DK + k + 1)
                    if k == 0:
                        V.tensor_copy(acc[:], sq[:, 0, :]).then_inc(s_sqa, 1)
                    else:
                        dve.wait_ge(s_sqa, n * DK + k)
                        V.tensor_tensor(acc[:], acc[:], sq[:, k % 2, :], ALU.add).then_inc(s_sqa, 1)
                dve.wait_ge(s_rs, n + 1)
                for k in range(DK):
                    dst(k, lambda where: V.scalar_tensor_tensor(
                        out=where, in0=x[:, k, :], scalar=col(gain, k), in1=rstd[:, 1, :], op0=ALU.mult, op1=ALU.mult))

            dve.wait_ge(s_part, 1)
            for t in range(4):
                o(V.tensor_copy(par[:, t, 0:PAR_ROWS[t]], bank[5][:, t * P:t * P + PAR_ROWS[t]]))
            t_ka, r_ka = PAR_AT["a_ka"]
            o(V.tensor_scalar(neg_ka[:], par[:, t_ka, r_ka:r_ka + CI], -1.0, 1.0, ALU.mult, ALU.add))
            dve.wait_ge(s_xt, DK)
            dve.wait_ge(s_const, 1)
            norm(0, "a_norm", lambda k, h: o(h(hT[:, k, 1:T + 1])))

            def lerp(k, mu, buf, done):
                if not (isinstance(done, int) and done < 1):
                    dve.wait_ge(s_xlo, done)
                V.scalar_tensor_tensor(out=tmp[:, buf, :], in0=acc[:], scalar=col("a_mu", k + mu * DK),
                                       in1=hT[:, bass.ds(k, 1), 1:T + 1], op0=ALU.mult,
                                       op1=ALU.add).then_inc(s_tmp, 1)

            def shift_difference(k):
                o(V.tensor_tensor(acc[:], hT[:, bass.ds(k, 1), 0:T], hT[:, bass.ds(k, 1), 1:T + 1], ALU.subtract))

            w_low(0, 0, LORA)
            w_low(1, 1, LORA)
            for k in range(DK):
                shift_difference(k)
                lerp(k, 1, 0, 2 * k - 1)
                lerp(k, 4, 1, 2 * k)
                x_low(2 * k, xl[0][:, 1, k, :], xl[0][:, 0, k, :], 0)
                x_low(2 * k + 1, xl[1][:, 1, k, :], xl[1][:, 0, k, :], 1)
            for k in range(DK):
                shift_difference(k)
                lerp(k, 5, k % 2, X_G + k - 1)
                x_low(X_G + k, xh[:, 1, k, :], xh[:, 0, k, :], k % 2)
            z = rstd[0:LORA, 0, :]
            dve.wait_ge(s_unit, 1)
            V.tensor_scalar(z, bank[0][0:LORA, :], 0.5 * CLAMP, None, ALU.max).then_inc(s_free[0], 1)
            dve.wait_ge(s_lsig, 1)
            V.tensor_scalar(z, z, 2.0, -1.0, ALU.mult, ALU.add).then_inc(s_lhid, 1)
            dve.wait_ge(s_unit, 2)
            V.tensor_copy(rstd[0:LORA, 1, :], bank[1][0:LORA, :]).then_inc(s_free[1], 1)
            w_low(U_GATE, 0)
            for n in range(2):
                dve.wait_ge(s_lhi, n + 1)
                V.tensor_tensor(lora[:, n, 1, :], rstd[0:LORA, n, :], lora[:, n, 0, :].bitcast(F32),
                                ALU.subtract).then_inc(s_lt, 1)

            def gate(t):
                n0 = 2 * t + U_GATE
                for u in range(2):
                    w_low(n0 + (u + 1), 1 - u)
                    dve.wait_ge(s_unit, n0 + (u + 1))
                    V.tensor_scalar(rstd[:, u, :], bank[u][:], CLAMP, None, ALU.max).then_inc(s_z, 1)
                    if u == 0:
                        shift_difference(t)
                    for n, mu in ((0, 2), (1, 0)) if u == 0 else ((2, 3),):
                        lerp(t, mu, n % 2, 3 * t + (X_RKV + n - (n > 0)))
                    for n in (range(2) if u == 0 else range(2, 3)):
                        x_low(3 * t + (X_RKV + n), xl[n][:, 1, bass.ds(t, 1), :], xl[n][:, 0, bass.ds(t, 1), :],
                              n % 2)
                    dve.wait_ge(s_sg, 2 * t + (u + 1))
                    dve.wait_ge(s_spill, 32 * t + 16)
                    V.tensor_tensor(sq[:, u, :], rstd[:, u, :], bank[u][:], ALU.mult).then_inc(s_free[u], 1)
            dve.wait_ge(s_lt, 2)
            repeat(dve, CI // 2, gate, o, 1)
            dve.wait_ge(s_const, 2)

            def by_chunk(x):
                return x.rearrange("p (c t) -> p c t", c=NCH)

            def mix(j):
                n0 = 4 * j + U_MIX
                w_low(n0 + 1, 1)
                dve.wait_ge(s_unit, n0 + 1)
                V.tensor_scalar(zw[:], bank[0][:], col("a_w0", j), CLAMP, ALU.add, ALU.max).then_inc(s_zw, 1)
                V.tensor_scalar(za[:], bank[2][:], col("a_a0", j), CLAMP, ALU.add, ALU.max).then_inc(s_free[0], 1)
                o(V.tensor_scalar(head_rk[:], head_ones[:], col("a_rk", j), None, ALU.mult))
                w_low(n0 + 2, 0)
                dve.wait_ge(s_unit, n0 + 2)
                V.tensor_scalar(kk[:], bank[1][:], col("a_kk", j), None, ALU.mult).then_inc(s_kk, 1)
                dve.wait_ge(s_sw, j + 1)
                o(V.tensor_scalar(lw[:, :, 1:W1], by_chunk(zw[:]), -EDECAY, None, ALU.mult))
                V.tensor_tensor_scan(out=cs[:].rearrange("p c t -> p (c t)"),
                                     data0=scanm[:].rearrange("p c t -> p (c t)"),
                                     data1=lw[:].rearrange("p c t -> p (c t)"), initial=0.0,
                                     op0=ALU.mult, op1=ALU.add).then_inc(s_cs, 1)
                dve.wait_ge(s_sa, j + 1)
                o(V.tensor_scalar(kp[:], za[:], col("a_ka", j), neg_ka[:, bass.ds(j, 1)], ALU.mult, ALU.add))
                V.tensor_tensor(kp[:], kp[:], bank[1][:], ALU.mult).then_inc(s_free[1], 1)
                w_low(n0 + 3, 1)
                dve.wait_ge(s_unit, n0 + 3)
                dve.wait_ge(s_free[1], 2 * j + (FREE_MIX + 1))
                V.tensor_tensor(rk[:], kp[:], bank[0][:], ALU.mult).then_inc(s_rk, 1)
                dve.wait_ge(s_pw, j + 1)
                dve.wait_ge(s_spill, j * SPILL_TILE + SPILL_MIX)
                V.tensor_tensor(by_chunk(o_r[:]), pw[:, :, 1:W1], by_chunk(bank[0][:]), ALU.mult).then_inc(s_free[0], 1)
                dve.wait_ge(s_n2, j + 1)
                V.tensor_scalar(n2[:], bank[4][:], 1e-24, None, ALU.max).then_inc(s_n2m, 1)
                w_low(n0 + 4, 0)
                dve.wait_ge(s_rn, j + 1)
                o(V.tensor_tensor(kn[:], kk[:], rn[:], ALU.mult))
                o(V.tensor_tensor(kka[:], kn[:], za[:], ALU.mult))
                V.tensor_tensor(by_chunk(o_q[:]), by_chunk(kn[:]), pw[:, :, 0:C], ALU.mult).then_inc(s_fin, 1)
                V.tensor_tensor(by_chunk(o_b[:]), by_chunk(kka[:]), pinv[:, :, 1:W1], ALU.mult).then_inc(s_fin, 1)
                V.tensor_tensor(by_chunk(o_c[:]), by_chunk(kp[:]), pinv[:, :, 1:W1], ALU.mult).then_inc(s_fin, 1)
                dve.wait_ge(s_bon, j + 1)
                dve.wait_ge(s_free[1], 2 * j + (FREE_MIX + 2))
                V.tensor_tensor(o_bv[:], o_v[:], bank[5][:], ALU.mult).then_inc(s_fin, 1)
            repeat(dve, CI, mix, o, 5)
            recurrence_vector(dve, o)

            for k in range(CI):
                dve.wait_ge(s_xhi, X_Y + k + 1)
                half = xl[k // DK]
                V.tensor_tensor(half[:, 1, k % DK, :], Y[:, k, :], half[:, 0, k % DK, :].bitcast(F32),
                                ALU.subtract).then_inc(s_xlo, 1)
            dve.wait_ge(s_back, 16)

            def even(base, turns, dst, add, n=None, final=False):
                if n is not None:
                    o(V.memset(acc[:], 0.0))

                def turn(t, last=False):
                    for u in range(2):
                        if not (last and u == 1):
                            w_low(2 * t + (base + u + 1), 1 - u)
                        dve.wait_ge(s_unit, 2 * t + (base + u + 1))
                        where = dst[:, bass.ds(2 * t + u, 1), :]
                        (V.tensor_tensor(where, where, bank[u][:], ALU.add) if add else
                         V.tensor_copy(where, bank[u][:])).then_inc(s_free[u], 1)
                        if n is not None:
                            dve.wait_ge(s_sq, 2 * t + (n * DK + u + 1))
                            dve.wait_ge(s_sqa, 2 * t + (n * DK + u))
                            V.tensor_tensor(acc[:], acc[:], sq[:, u, :], ALU.add).then_inc(s_sqa, 1)
                repeat(dve, turns - final, turn)
                if final:
                    turn(turns - 1, last=True)

            def split(x0, dst, n):
                def step(k, make):
                    if x0 + k >= 2:
                        dve.wait_ge(s_xlo, x0 + k - 1)
                    make(tmp[:, k % 2, :]).then_inc(s_tmp, 1)
                    if k:
                        x_low(x0 + k - 1, dst[:, 1, k - 1, :], dst[:, 0, k - 1, :], (k - 1) % 2)
                    if k == n - 1:
                        x_low(x0 + k, dst[:, 1, k, :], dst[:, 0, k, :], k % 2)
                return step

            for half in range(2):
                even(U_OUT1 + half * DK, DK // 2, xT2, True, n=1 if half else None)

            o(V.memset(cu[:, 0:2], 0.0))
            dve.wait_ge(s_xlo, X_H2)
            norm(1, "b_norm", split(X_H2, xl[2], DK), xT2, summed=True)
            for half in range(2):
                base = U_CONV + half * (4 * KB + DK)

                def conv(t):
                    n0 = 4 * t + base
                    w_low(n0 + 1, 1)
                    dve.wait_ge(s_unit, n0 + 1)
                    V.tensor_copy(c_sb[:], bank[0][:]).then_inc(s_free[0], 1)
                    w_low(n0 + 2, 0)
                    dve.wait_ge(s_unit, n0 + 2)
                    dve.wait_ge(s_free[0], 2 * t + (base // 2 + 1))
                    V.tensor_tensor(cu[:, 2:2 + T], c_sb[:], bank[1][:], ALU.mult).then_inc(s_free[1], 1)
                    dve.wait_ge(s_free[1], 2 * t + (base // 2 + 1))
                    ct = t + KB * half
                    o(V.tensor_scalar(conv3[:, 0, :], cu[:, 0:T], col("b_conv", ct), None, ALU.mult))
                    for tap in (1, 2):
                        o(V.scalar_tensor_tensor(out=conv3[:, tap % 2, :], in0=cu[:, tap:tap + T],
                                                 scalar=col("b_conv", ct + tap * CI), in1=conv3[:, 1 - tap % 2, :],
                                                 op0=ALU.mult, op1=ALU.add))
                    w_low(n0 + 3, 1)
                    dve.wait_ge(s_unit, n0 + 3)
                    V.tensor_scalar(gate3[:], bank[0][:], CLAMP, None, ALU.max).then_inc(s_zc, 1)
                    dve.wait_ge(s_sc, ct + 1)
                    V.tensor_tensor(gate3[:], gate3[:], bank[0][:], ALU.mult).then_inc(s_free[0], 1)
                    dve.wait_ge(s_free[0], 2 * t + (base // 2 + 2))
                    o(V.tensor_tensor(gate3[:], gate3[:], conv3[:, 0, :], ALU.mult))
                    w_low(n0 + 4, 0)
                    dve.wait_ge(s_unit, n0 + 4)
                    V.tensor_tensor(tmp[:, 0, :], gate3[:], bank[1][:], ALU.mult).then_inc(s_free[1], 1)
                    x_low(t + (X_YC + KB * half), xl[half][:, 1, bass.ds(t, 1), :], xl[half][:, 0, bass.ds(t, 1), :], 0)
                repeat(dve, KB, conv, o, 4)
                even(base + 4 * KB, DK // 2, xT2, True, n=2 if half else None)

            norm(2, "final_norm", lambda k, scaled: scaled(xT2[:, k, :]).then_inc(s_xn, 1), xT2,
                 summed=True)
            o(V.memset(glu[:, :, 0:PAD2], 0.0))
            norm(3, "norm_mix_pre_2", split(X_H3, xh, DK), xT2)
            for j in range(CT):
                n0 = U_GLU + 2 * j
                w_low(n0 + 1, 1)
                w_low(n0 + 2, 0)
                dve.wait_ge(s_unit, n0 + 2)
                if j >= 2:
                    dve.wait_ge(s_free[0], n0 // 2 - 1)
                V.tensor_scalar(rstd[:, j % 2, :], bank[1][:], CLAMP, None, ALU.max).then_inc(s_free[1], 1)
                dve.wait_ge(s_glu, j + 1)
                V.tensor_tensor(glu[:, j, PAD2:], rstd[:, j % 2, :], bank[0][:], ALU.mult).then_inc(s_free[0], 1)
            dve.wait_ge(s_free[0], U_QKV // 2)

            def taps():
                for j in range(CT - 1):
                    y = dconv[:, j, :]
                    o(V.tensor_scalar(y, glu[:, j, 0:T], col("conv_dw_w_2", j), col("conv_dw_b_2", j), ALU.mult,
                                      ALU.add))
                    yield
                    for tap in range(1, TAPS2):
                        o(V.scalar_tensor_tensor(out=y, in0=glu[:, j, tap:tap + T], scalar=col("conv_dw_w_2", tap * CT + j),
                                                 in1=y, op0=ALU.mult, op1=ALU.add))
                        yield
            tap = taps()
            v_ch = [sq[:, 0, :], sq[:, 1, :], rstd[:, 0, :], rstd[:, 1, :]]
            for n in range(3 * AT + 2 * DK):
                u = U_QKV + n
                w_low(u + 1, (n + 1) % 2)
                dve.wait_ge(s_unit, u + 1)
                src = bank[n % 2][:]
                if n < AT:
                    ins = V.tensor_scalar(qT[:, n, :], src, 0.125, None, ALU.mult)
                elif n < 2 * AT:
                    ins = V.tensor_copy(kT[:, n - AT, :], src)
                elif n < 3 * AT:
                    ins = V.tensor_copy(v_ch[n - 2 * AT], src)
                else:
                    m = n - 3 * AT
                    ins = V.tensor_scalar(gates[:, m % 2, m // 2, :], src, CLAMP, None, ALU.max)
                ins.then_inc(s_free[n % 2], 1)
                for _ in range(4):
                    next(tap, None)

            dve.wait_ge(s_vt, NT)
            dve.wait_ge(s_tap3, 1)
            o(V.tensor_tensor(acc[:], dconv[:, 0, :], dconv[:, 1, :], ALU.add))
            V.tensor_tensor(acc[:], acc[:], dconv[:, 2, :], ALU.add).then_inc(s_dc, 1)
            dve.wait_ge(s_dc, 1)
            V.tensor_tensor(acc[:], acc[:], dconv[:, 3, :], ALU.add).then_inc(s_dc, 1)
            dve.wait_ge(s_lnm, 1)
            for j in range(CT):
                V.scalar_tensor_tensor(out=dconv[:, j, :], in0=bank[4][:], scalar=-2.0, in1=dconv[:, j, :],
                                       op0=ALU.mult, op1=ALU.add).then_inc(s_cen, 1)
            for j in range(CT):
                dve.wait_ge(s_lsq, j + 1)
                if j == 0:
                    V.tensor_copy(acc[:], sq[:, 0, :]).then_inc(s_lacc, 1)
                else:
                    dve.wait_ge(s_lacc, j)
                    V.tensor_tensor(acc[:], acc[:], sq[:, j % 2, :], ALU.add).then_inc(s_lacc, 1)
            dve.wait_ge(s_lrs, 1)
            finish = split(X_UC, uc, CT)
            for j in range(CT):
                y = dconv[:, j, :]
                o(V.tensor_tensor(y, y, rstd[:, 1, :], ALU.mult))
                o(V.tensor_scalar(y, y, col("conv_ln_g_2", j), col("conv_ln_b_2", j), ALU.mult, ALU.add))
                V.tensor_scalar(sq[:, j % 2, :], y, CLAMP, None, ALU.max).then_inc(s_lz, 1)
                dve.wait_ge(s_ls, j + 1)
                finish(j, lambda where: V.tensor_tensor(where, y, sq[:, j % 2, :], ALU.mult))
            attention_vector(dve, o, split(X_AT, ah, AT))

            finish = split(X_MG, xh, DK)
            for n in range(DK):
                w_low(U_MERGE + n + 1, (n + 1) % 2)
                dve.wait_ge(s_unit, U_MERGE + n + 1)
                if n == 0:
                    dve.wait_ge(s_gate2, 2 * DK)
                o(V.scalar_tensor_tensor(out=sq[:, 0, :], in0=bank[n % 2][:], scalar=col("b_conv_branch_2", n),
                                         in1=gates[:, 0, n, :], op0=ALU.add, op1=ALU.mult))
                V.tensor_tensor(sq[:, 1, :], bank[2 + n % 2][:], gates[:, 1, n, :], ALU.mult).then_inc(s_free[n % 2], 1)
                dve.wait_ge(s_free[n % 2], (U_MERGE + n) // 2 + 1)
                finish(n, lambda where: V.tensor_tensor(where, sq[:, 0, :], sq[:, 1, :], ALU.add))
            even(U_WOUT2, DK // 2, mixed, False, n=4)

            def residual(n, gain, src, signal):
                def step(k, scaled):
                    scaled(src[:, k, :]).then_inc(s_scaled, 1)
                    for m in ([k - 1] if k else []) + ([k] if k == DK - 1 else []):
                        dve.wait_ge(s_scaled, (DK if n == 6 else 0) + m + 1)
                        V.tensor_tensor(xT2[:, m, :], xT2[:, m, :], src[:, m, :], ALU.add).then_inc(signal, 1)
                norm(n, gain, step, src, summed=True)
            residual(4, "norm_mix_post_2", mixed, s_mg)

            norm(5, "norm_ffn_pre_2", split(X_H4, xl[0], DK), xT2)
            base = U_FFN
            for part, (j0, n) in enumerate(FPARTS):
                dst = xl[1 + part % 2]

                def ffn(t):
                    n0 = 2 * t + base
                    w_low(n0 + 1, 1)
                    dve.wait_ge(s_unit, n0 + 1)
                    V.tensor_scalar(rstd[:, 0, :], bank[0][:], CLAMP, None, ALU.max).then_inc(s_ug, 1)
                    w_low(n0 + 2, 0)
                    dve.wait_ge(s_us, t + (j0 + 1))
                    V.tensor_tensor(rstd[:, 0, :], rstd[:, 0, :], bank[0][:], ALU.mult).then_inc(s_free[0], 1)
                    dve.wait_ge(s_unit, n0 + 2)
                    dve.wait_ge(s_free[0], t + (base // 2 + 1))
                    V.tensor_tensor(tmp[:, 0, :], rstd[:, 0, :], bank[1][:], ALU.mult).then_inc(s_free[1], 1)
                    x_low(t + (X_FF + j0), dst[:, 1, bass.ds(t, 1), :], dst[:, 0, bass.ds(t, 1), :], 0)
                repeat(dve, n, ffn)
                last = part == len(FPARTS) - 1
                even(base + 2 * n, DK // 2, ffo, part > 0, n=6 if last else None, final=last)
                base += 2 * n + DK
            residual(6, "norm_ffn_post_2", ffo, s_ffn)
            for q in range(NT):
                dve.wait_ge(s_yt, 2 * q + 1)
                V.tensor_copy(staged[:, q, 0:T], bank[(2 * q) % 8][:]).then_inc(s_yc[0], 1)


_INS = ['x', 'a_norm', 'a_mu', 'a_w_in', 'a_w0', 'a_w1', 'a_w2', 'a_a0', 'a_a1', 'a_a2', 'a_kk', 'a_ka', 'a_rk',
        'a_lnw', 'a_lnb', 'a_w_out', 'b_norm', 'b_w_in', 'b_conv', 'b_w_out', 'final_norm', 'norm_mix_pre_2',
        'w_in_2', 'conv_dw_w_2', 'conv_dw_b_2', 'conv_ln_g_2', 'conv_ln_b_2', 'w_conv_branch_2', 'b_conv_branch_2',
        'w_att_branch_2', 'w_out_2', 'norm_mix_post_2', 'norm_ffn_pre_2', 'w_ffn_up_2', 'w_ffn_down_2',
        'norm_ffn_post_2']


def kernel(**inputs):
    import numpy as _np
    import concourse.bacc as _bacc
    from concourse import mybir as _mybir
    from concourse.bass_utils import run_bass_kernel_spmd as _run

    nc = _bacc.Bacc("TRN2", target_bir_lowering=False, num_devices=1)
    arrays, args = {}, {}
    for name in _INS:
        a = _np.ascontiguousarray(inputs[name])
        arrays[f"in_{name}"] = a
        args[name] = nc.dram_tensor(f"in_{name}", a.shape, _mybir.dt.from_np(a.dtype), kind="ExternalInput").ap()
    out = nc.dram_tensor("out_0", (1, T, D), F32, kind="ExternalOutput").ap()
    program(nc, args, out)
    r = _run(nc, [arrays], core_ids=[0])
    return r.results[0]["out_0"]
```

```python
from contextlib import ExitStack

import concourse.bass as bass
from concourse import mybir

F32 = mybir.dt.float32
F32R = mybir.dt.float32r
F16 = mybir.dt.float16
ALU = mybir.AluOpType
ACT = mybir.ActivationFunctionType

P = 128
T = 512
D = 1024
DK = D // P
DI = 2048
CI = DI // P
LORA = 64
C = 64
NCH = T // C
W1 = C + 1
EDECAY = 0.6065306597126334
CLAMP = -43.0
LN2 = 0.6931471805599453
EXP_LN_SET = 6
NSHIFT = 30
RMS_EPS = 1e-6
GN_EPS = 64e-5
AD = 512
AT = AD // P
NHEAD2 = 8
CT = 4
TAPS2 = 31
PAD2 = TAPS2 - 1
FT = 22
NT = T // P
ATT_AT = [sum(T - P * m for m in range(n)) for n in range(NT + 1)]
ATT_COLS = ATT_AT[NT]
SUMMED_BY_PE = (3, 5)
KB = 8

PARAMS = [
    [("a_norm", 8), ("a_mu", 48), ("a_w0", 16), ("a_a0", 16), ("a_kk", 16), ("a_ka", 16)],
    [("a_rk", 16), ("a_lnw", 16), ("a_lnb", 16), ("b_norm", 8), ("b_conv", 48), ("final_norm", 8)],
    [("norm_mix_pre_2", 8), ("conv_dw_b_2", 4), ("conv_ln_g_2", 4), ("conv_ln_b_2", 4), ("b_conv_branch_2", 8),
     ("norm_mix_post_2", 8), ("norm_ffn_pre_2", 8), ("norm_ffn_post_2", 8)],
    [("conv_dw_w_2", 124)],
]
PAR_ROWS = [sum(n for _, n in rows) for rows in PARAMS]
PAR_AT = {name: (t, sum(n for _, n in rows[:i])) for t, rows in enumerate(PARAMS) for i, (name, _) in enumerate(rows)}

U_LORA1 = 0
U_GATE = U_LORA1 + 2
U_MIX = U_GATE + CI
U_OUT1 = U_MIX + 4 * CI
U_CONV = U_OUT1 + 2 * DK
U_GLU = U_CONV + 2 * (4 * 8 + DK)
U_QKV = U_GLU + 2 * CT
U_GATES2 = U_QKV + 3 * AT
U_MERGE = U_GATES2 + 2 * DK
U_WOUT2 = U_MERGE + DK
U_FFN = U_WOUT2 + DK
FPARTS = [(0, 8), (8, 8), (16, 6)]

X_LORA = 0
X_G = X_LORA + 2 * DK
X_RKV = X_G + DK
X_Y = X_RKV + 3 * DK
X_H2 = X_Y + CI
X_YC = X_H2 + DK
X_H3 = X_YC + CI
X_UC = X_H3 + DK
X_AT = X_UC + CT
X_MG = X_AT + AT
X_H4 = X_MG + DK
X_FF = X_H4 + DK


def made(q):
    if not isinstance(q, int) or q < X_Y:
        return q + 1
    if X_YC <= q < X_H3 or q < X_H2:
        return None
    return q + 1 - CI - (CI if q >= X_H3 else 0)


def panel_dmas(n):
    lora2 = U_MIX <= n < U_OUT1 and (n - U_MIX) % 4 == 1
    return 2 if lora2 or U_MERGE <= n < U_WOUT2 else 1


def panels_by(n):
    return 16 * sum(panel_dmas(m) for m in range(n % 2, n + 1, 2))


class Order:

    def __init__(self, eng, sem):
        self.eng, self.sem, self.base, self.k, self.i, self.per = eng, sem, 0, 0, None, 0

    def __call__(self, ins):
        ins.then_inc(self.sem, 1)
        self.k += 1
        n = self.base + self.k
        self.eng.wait_ge(self.sem, n if self.i is None else self.i * self.per + n)

    def enter(self, i, per):
        self.base, self.k, self.i, self.per = self.base + self.k, 0, i, per

    def leave(self, turns):
        assert self.k == self.per, (self.k, self.per)
        self.base, self.k, self.i = self.base + turns * self.per, 0, None


def program(nc, i, out):
    with ExitStack() as ctx:
        at = [16512]

        def place(name, shape, dt, where=None):
            size = 4 if dt in (F32, F32R) else 2
            for n in shape[1:]:
                size *= n
            size = (size + 31) // 32 * 32
            if where is None:
                where = at[0]
                at[0] += size
            return nc.alloc_sbuf_tensor_at(name, shape, dt, offset=where), where, where + size

        def sem(name):
            return ctx.enter_context(nc.semaphore(name))

        def dram(name, shape):
            return nc.dram_tensor(name, shape, F32, kind="Internal").ap()

        ident, _, _ = place("ident", [P, P], F32)
        mean_d, _, _ = place("mean_d", [P, P], F32)
        head_ones, _, _ = place("head_ones", [P, P], F32)
        head_rk, _, _ = place("head_rk", [P, P], F32)
        masks, _, _ = place("masks", [P, P + C], F32)
        par, _, _ = place("par", [P, 4, P], F32)
        neg_ka, _, _ = place("neg_ka", [P, CI], F32)
        eps, _, _ = place("eps", [P, 4], F32)
        w_raw, _, _ = place("w_raw", [P, 2, KB, P], F32)
        w_hi, _, _ = place("w_hi", [P, 2, KB, P], F32R)
        w_lo, _, _ = place("w_lo", [P, 2, KB, P], F32R)
        tmp, _, _ = place("tmp", [P, 2, T], F32)
        sq, _, _ = place("sq", [P, 2, T], F32)
        acc, _, _ = place("acc", [P, T], F32)
        rstd, _, _ = place("rstd", [P, 2, T], F32)
        att_from, _, _ = place("att_from", [P, P], F32)
        att_ones, _, _ = place("att_ones", [P, P], F32)
        att_keep, _, _ = place("att_keep", [P, P], F32)
        att_drop, _, _ = place("att_drop", [P, P], F32)
        xT, x_at, _ = place("xT", [P, DK, T], F32)
        xh, xh_at, _ = place("xh", [P, 2, DK, T], F32R)
        big_at = at[0]
        xl = [place(f"xl{n}", [P, 2, DK, T], F32R)[0] for n in range(3)]
        free_at = at[0]
        hT, hT_at, hT_end = place("hT", [P, DK, T + 1], F32)
        assert at[0] <= nc.sbuf_usable_end, (at[0], nc.sbuf_usable_end)
        x_raw, _, _ = place("x_raw", [P, 4, D], F32, big_at + 2 * 32768)
        par_raw, _, _ = place("par_raw", [P, 4, P], F32, big_at + 2 * 32768 + 16384)
        lora, lora_at, lora_end = place("lora", [LORA, 2, 2, T], F32R, x_at)
        spot = xh_at

        def over(name, shape, dt=F32):
            nonlocal spot
            t, a, spot = place(name, shape, dt, spot)
            return t

        zw, za = over("zw", [P, T]), over("za", [P, T])
        kk, kn, rn = over("kk", [P, T]), over("kn", [P, T]), over("rn", [P, T])
        kp, kka, rk = over("kp", [P, T]), over("kka", [P, T]), over("rk", [P, T])
        n2, sqk, kraw = over("n2", [P, T]), over("sqk", [P, T]), over("kraw", [P, T])
        o_r, o_v, o_bv = over("o_r", [P, T]), over("o_v", [P, T]), over("o_bv", [P, T])
        o_q, o_pc = over("o_q", [P, T]), over("o_pc", [P, NCH])
        assert spot <= xh_at + 32768
        spot = hT_at
        lw, cs = over("lw", [P, NCH, W1]), over("cs", [P, NCH, W1])
        pw, pinv = over("pw", [P, NCH, W1]), over("pinv", [P, NCH, W1])
        o_b, o_c = over("o_b", [P, T]), over("o_c", [P, T])
        scanm = over("scanm", [P, NCH, W1])
        assert spot <= hT_end

        spot = lora_end
        bmask = over("bmask", [P, 5, P])
        eyes = over("eyes", [P, NCH, C])
        eyes16 = over("eyes16", [P, 4, P], F16)
        two16 = over("two16", [P, P], F16)
        one16 = over("one16", [P, P], F16)
        center = over("center", [P, P])
        head_mean = over("head_mean", [P, P])
        assert spot <= xh_at
        spot = xh_at
        Y = over("Y", [P, CI, T])
        st_q = [over(f"st_q{n}", [P, NCH, 3, C]) for n in range(3)]
        st_bc = [over(f"st_bc{n}", [P, NCH, 2, C]) for n in range(2)]
        st_v = [over(f"st_v{n}", [P, (NCH + 1) * C]) for n in range(2)]
        st_pc = [over(f"st_pc{n}", [P, NCH]) for n in range(3)]
        assert spot <= big_at + 32768
        st_bv = [over(f"st_bv{n}", [P, T]) for n in range(2)]
        st_g = [over(f"st_g{n}", [P, T]) for n in range(2)]
        ra = [over(f"ra{n}", [P, NCH, 2, C]) for n in range(2)]
        bt = [over(f"bt{n}", [P, NCH, P]) for n in range(2)]
        sv = [over(f"sv{n}", [P, NCH, 2, C]) for n in range(2)]
        tt = [over(f"tt{n}", [P, NCH, P]) for n in range(2)]
        nix, nixe = over("nix", [P, NCH, C]), over("nixe", [P, NCH, C])
        nix16, nixlo16, w16 = (over(n, [P, NCH, P], F16) for n in ("nix16", "nixlo16", "w16"))
        inv16, inv_t16 = over("inv16", [P, NCH, P], F16), over("inv_t16", [P, NCH, P], F16)
        rhs = over("rhs", [P, C])
        y0, yc, ysq, yr, y2 = (over(n, [P, T]) for n in ("y0", "yc", "ysq", "yr", "y2"))
        assert spot <= nc.sbuf_usable_end, (spot, nc.sbuf_usable_end)

        xT2, _, _ = place("xT2", [P, DK, T], F32, hT_at)
        spot = xh_at
        c_sb, cu, conv3 = over("c_sb", [P, T]), over("cu", [P, 2 + T]), over("conv3", [P, 2, T])
        gate3 = over("gate3", [P, T])
        spot = big_at
        gates = over("gates", [P, 2, DK, T])
        uc = over("uc", [P, 2, CT, T], F32R)
        ah = over("ah", [P, 2, AT, T], F32R)
        vtok = over("vtok", [P, NT, AD])
        tail_at = spot
        glu = over("glu", [P, CT, PAD2 + T])
        dconv, tapped = over("dconv", [P, CT, T]), over("tapped", [P, T])
        spot = tail_at
        att_sp, att_a = over("att_sp", [P, 2, ATT_COLS]), over("att_a", [P, 2, ATT_COLS])
        att_zz = over("att_zz", [P, 2, T])
        att_z = [rstd[:, 0, :], rstd[:, 1, :], att_zz[:, 0, :], att_zz[:, 1, :]]
        assert spot <= hT_at, (spot, hT_at)
        spot = x_at
        qT, kT = over("qT", [P, AT, T]), over("kT", [P, AT, T])
        mixed, _, _ = place("mixed", [P, DK, T], F32, x_at)
        ffo, _, _ = place("ffo", [P, DK, T], F32, xh_at)
        staged, _, _ = place("staged", [P, T // P, D], F32, x_at)

        bank = [ctx.enter_context(nc.psum_tensor(f"bank{n}", [P, T], F32)) for n in range(8)]

        d_x = dram("d_x", [P, DK, T])
        d_g = dram("d_g", [CI, P, T])
        d_q, d_r, d_b, d_c, d_v, d_bv = (dram(f"d_{n}", [CI, P, T]) for n in ("q", "r", "b", "c", "v", "bv"))
        d_pc = dram("d_pc", [CI, P, NCH])

        def col(name, j):
            t, row = PAR_AT[name]
            return par[:, t, bass.ds(row + j, 1)]

        s_xin = sem("x_loaded")
        s_par = sem("params_loaded")
        s_const = sem("constants_made")
        s_part = sem("params_transposed")
        s_tr = sem("x_transposed")
        s_xt = sem("xT_copied")
        s_raw = [sem("panel_in_slot0"), sem("panel_in_slot1")]
        s_hi = sem("panel_hi_made")
        s_lo = sem("panel_lo_made")
        s_unit = sem("unit_summed")
        s_free = [sem("unit_bank0_read"), sem("unit_bank1_read")]
        s_sq = sem("squares_made")
        s_sqa = sem("squares_added")
        s_ms = sem("mean_square_summed")
        s_rs = sem("rstd_made")
        s_tmp = sem("activation_made")
        s_xhi = sem("activation_hi_made")
        s_xlo = sem("activation_lo_made")
        s_hT = sem("first_norm_applied")
        s_dif1 = sem("token_differences_made")
        s_spill = sem("spilled")
        s_lsig = sem("lora_sigmoid_made")
        s_lhid = sem("lora_hidden_made")
        s_lhi = sem("lora_hidden_hi_made")
        s_lt = sem("lora_hidden_lo_made")
        s_z = sem("gate_arg_made")
        s_sg = sem("gate_sigmoid_made")
        s_zw = sem("decay_arg_made")
        s_sw = sem("decay_sigmoid_made")
        s_sa = sem("rate_sigmoid_made")
        s_kk = sem("kk_made")
        s_sqk = sem("kk_squared")
        s_n2 = sem("kk_norm_summed")
        s_n2m = sem("kk_norm_clamped")
        s_rn = sem("kk_rnorm_made")
        s_cs = sem("log_decay_summed")
        s_pw = sem("decay_powers_made")
        s_rk = sem("bonus_terms_made")
        s_bon = sem("bonus_summed")
        s_fin = sem("tile_finished")
        s_vseq, s_aseq, s_gseq = sem("vector_order"), sem("scalar_order"), sem("gpsimd_order")
        s_back = sem("xT_reloaded")
        s_zc = sem("conv_gate_arg_made")
        s_sc = sem("conv_gate_sigmoid_made")
        s_xn = sem("final_norm_applied")
        s_glu = sem("glu_sigmoid_made")
        s_gluok = sem("glu_made")
        s_gate2 = sem("branch_gate_made")
        s_vt = sem("v_turned")
        s_vtok = sem("v_turned_copied")
        s_tap = sem("tap_added")
        s_tap0 = sem("gpsimd_channels_convolved")
        s_dc = sem("depthwise_conv_summed")
        s_lnm = sem("layernorm_sum_made")
        s_cen = sem("layernorm_centered")
        s_lsq = sem("layernorm_squared")
        s_lacc = sem("layernorm_squares_added")
        s_lrs = sem("layernorm_rstd_made")
        s_lz = sem("layernorm_silu_arg_made")
        s_ls = sem("layernorm_silu_sigmoid_made")
        s_sc2 = sem("scores_summed")
        s_neg = sem("scores_copied")
        s_log = sem("log_term_made")
        s_sp = sem("softplus_made")
        s_cum = sem("softplus_summed")
        s_dif = sem("log_weights_made")
        s_wt = sem("weights_made")
        s_o = sem("attention_summed")
        s_scaled = sem("mixed_or_ffn_scaled")
        s_mg = sem("mixed_added")
        s_ug = sem("ffn_gate_arg_made")
        s_us = sem("ffn_gate_sigmoid_made")
        s_ffn = sem("ffn_added")
        s_yt = sem("output_turned")
        s_yc = sem("output_copied")
        s_out = sem("output_written")
        R = {n: sem(n) for n in (
            "products_summed", "products_masked", "turned", "turned_copied", "nix_made", "nix16_made", "q0_made", "r0_summed", "r0_copied",
            "low_made", "v_summed", "v_copied", "rq_summed", "rq_copied", "q1_copied", "e_summed", "t_summed",
            "rhs_summed", "u_summed", "s_summed", "y_summed", "y_bank_read", "centered",
            "centered_copied", "y_squared", "var_summed", "y_rstd_made", "y_finished")}
        for n in ("e_copied", "inverse_made", "state_zeroed", "tiles_loaded", "ends_loaded", "rhs_copied", "u_copied", "s_copied"):
            R[n] = [sem(f"{n}{h}") for h in range(2)]

        block = ctx.enter_context(nc.Block())

        def repeat(eng, turns, body, order=None, per=0):
            with eng.Fori(0, turns) as n:
                if order is not None:
                    order.enter(n, per)
                body(n)
            if order is not None:
                order.leave(turns)

        w_in = i["a_w_in"].rearrange("a s d e -> (a s) d e")
        LOADS = 16 * 10
        SPILL_MIX = 16 + 16 * CI
        SPILL_TILE = 16 * 7
        FREE_MIX = 1 + CI // 2

        def panels(first, units, n, u):
            if isinstance(n, int):
                return panels_by(first + units * n + u)
            step = panels_by(first + units + u - 2 * (u == units)) - panels_by(first + u - 2 * (u == units))
            return n * step + panels_by(first + u)


        S_NEWTON = 10

        def when(turn, last):
            return 0 <= turn < last

        def recurrence_tensor(pe):
            mm, tr = nc.tensor.matmul, nc.tensor.transpose
            rows = [slice(0, C), slice(C, P)]

            def state_output(j, b, c):
                for h in range(2):
                    mm(bank[7][rows[h], c * C:(c + 1) * C], sv[b][rows[h], c, h, :], st_q[j % 3][rows[h], c, 1, :],
                       start=True, stop=False)

            def chain(j, b, c, phase):
                if phase == 0:
                    if c == 0:
                        for g in range(2):
                            pe.wait_ge(R["inverse_made"][g], j + 1)
                    for h in range(2):
                        pe.wait_ge(*((R["s_copied"][h], (NCH - 1) * j + c) if c else (R["state_zeroed"][h], j + 1)))
                    for h in range(2):
                        last = mm(bank[5][rows[h], 0:C], st_q[j % 3][:, c, 2 * h, :], sv[b][:, c, h, :],
                                  start=True, stop=True)
                    last.then_inc(R["rhs_summed"], 1)
                    if c:
                        state_output(j, b, c)
                    for h in range(2):
                        mm(bank[6][rows[h], 0:C], ident[rows[h], rows[h]], sv[b][rows[h], c, h, :],
                           start=True, stop=False)
                elif phase == 1:
                    if c == 0:
                        if j:
                            pe.wait_ge(R["y_bank_read"], j)
                        state_output(j, b, c)
                    for h in range(2):
                        pe.wait_ge(R["rhs_copied"][h], NCH * j + c + 1)
                    mm(bank[5][:, C:2 * C], tt[b][:, c, :], rhs[:], start=True, stop=True).then_inc(R["u_summed"], 1)
                else:
                    for h in range(2):
                        pe.wait_ge(R["u_copied"][h], NCH * j + c + 1)
                        last = mm(bank[6][rows[h], 0:C], bt[b][:, c, rows[h]], sv[b][:, c, h, :],
                                  start=False, stop=True)
                    last.then_inc(R["s_summed"], 1)
                    for h in range(2):
                        last = mm(bank[7][rows[h], c * C:(c + 1) * C], sv[b][:, c, h, :], ra[b][:, c, h, :],
                                  start=False, stop=True)
                    if c == NCH - 1:
                        last.then_inc(R["y_summed"], 1)

            def products(j, b, c):
                if c == 0:
                    pe.wait_ge(R["tiles_loaded"][b], LOADS * (j // 2 + 1))
                    if j:
                        for g in range(2):
                            pe.wait_ge(R["inverse_made"][g], j)
                elif c == 4:
                    pe.wait_ge(R["products_masked"], 2 * j + 1)
                    pe.wait_ge(R["turned_copied"], 2 * j + 1)
                for h in range(2):
                    last = mm(bank[2 + h][:, (c % 4) * P:(c % 4 + 1) * P], st_bc[b][rows[h], c, :, :],
                              st_q[j % 3][rows[h], c, h:h + 2, :], start=True, stop=True)
                if c % 4 == 3:
                    last.then_inc(R["products_summed"], 1)
                tr(bank[0][:, (c % 4) * P:(c % 4 + 1) * P], st_bc[b][:, c, :, :], ident[:])
                last = tr(bank[1][:, (c % 4) * P:(c % 4 + 1) * P], st_v[b][:, c * C:(c + 2) * C], ident[:])
                if c % 4 == 3:
                    last.then_inc(R["turned"], 1)

            eyes4 = eyes16[:].rearrange("p c t -> p (c t)")
            pair = [(1, 2), (0, 3)]

            def each(bk, g, lhsT, rhs_, start=True, stop=True):
                for c in range(4):
                    last = mm(bank[bk][:, c * P:(c + 1) * P], lhsT[:, 4 * g + c, :], rhs_[:, c if rhs_ is eyes16 else
                              4 * g + c, :], start=start, stop=stop, skip_group_check=True)
                return last

            def first_inverse(j):
                pe.wait_ge(R["turned_copied"], 2 * j + 2)
                for g in range(2):
                    pe.wait_ge(R["q0_made"], 2 * j + g + 1)
                    if g == 1:
                        pe.wait_ge(R["products_masked"], 2 * j + 2)
                    each(1 + g, g, inv_t16, eyes16).then_inc(R["r0_summed"], 1)

            def newton_v(j, level):
                for g in range(2):
                    if level == 1:
                        pe.wait_ge(R["r0_copied"], 2 * j + g + 1)
                    else:
                        pe.wait_ge(R["rq_copied"], 15 * j + 3 * (level - 2) + (1, 3)[g])
                    bk = pair[level % 2][g]
                    mm(bank[bk][:], two16[:], eyes4, start=True, stop=False, skip_group_check=True)
                    each(bk, g, nix16, inv16, start=False).then_inc(R["v_summed"], 1)

            def newton_r(j, level):
                for g in range(2):
                    pe.wait_ge(R["v_copied"], 10 * j + 2 * (level - 1) + g + 1)
                    if g == 0 and level == 1:
                        pe.wait_ge(R["r0_copied"], 2 * j + 2)
                    if g == 0 and level > 1:
                        pe.wait_ge(R["rq_copied"], 15 * j + 3 * (level - 1))
                        pe.wait_ge(R["q1_copied"], 5 * j + level - 1)
                    banks = pair[(level + 1 + g) % 2]
                    if g == 1:
                        pe.wait_ge(R["v_copied"], 10 * j + 2 * level)
                    each(banks[0], g, inv_t16, w16).then_inc(R["rq_summed"], 1)
                    each(banks[1], g, w16, inv_t16).then_inc(R["rq_summed"], 1)

            def residual(j):
                pe.wait_ge(R["low_made"], 2 * j + 2)
                for g in range(2):
                    pe.wait_ge(R["rq_copied"], 15 * j + (14, 15)[g])
                    mm(bank[1 + g][:], one16[:], eyes4, start=True, stop=False, skip_group_check=True)
                    each(1 + g, g, nixlo16, inv16, start=False, stop=False)
                    each(1 + g, g, nix16, inv16, start=False).then_inc(R["e_summed"], 1)

            def last_inverse(j):
                pe.wait_ge(R["q1_copied"], 5 * j + 5)
                for g in range(2):
                    pe.wait_ge(R["e_copied"][g], j + 1)
                    for c in range(4):
                        where = bank[3 * g][:, c * P:(c + 1) * P]
                        mm(where, inv16[:, 4 * g + c, :], eyes16[:, 0, :], start=True, stop=False)
                        last = mm(where, w16[:, 4 * g + c, :], inv_t16[:, 4 * g + c, :], start=False, stop=True)
                    last.then_inc(R["t_summed"], 1)

            pe.wait_ge(s_const, 3)
            pe.wait_ge(s_free[0], U_OUT1 // 2)
            pe.wait_ge(s_free[1], U_OUT1 // 2)
            for j in range(CI + 2):
                for s in range(3 * NCH):
                    if when(j - 1, CI):
                        chain(j - 1, (j - 1) % 2, s // 3, s % 3)
                    if when(j, CI):
                        if s in (0, 1, 4, 5):
                            for c in range(2):
                                products(j, j % 2, 2 * (s % 4) + 4 * (s // 4) + c)
                        elif s == S_NEWTON - 1:
                            first_inverse(j)
                        elif S_NEWTON <= s < S_NEWTON + 10:
                            (newton_r if (s - S_NEWTON) % 2 else newton_v)(j, (s - S_NEWTON) // 2 + 1)
                        elif s == S_NEWTON + 10:
                            residual(j)
                        elif s == S_NEWTON + 11:
                            last_inverse(j)
                    if when(j - 2, CI):
                        if s == 3:
                            pe.wait_ge(R["y_bank_read"], j - 1)
                            mm(bank[4][:], center[:], y0[:], start=True, stop=True).then_inc(R["centered"], 1)
                        if s == 7:
                            pe.wait_ge(R["centered_copied"], j - 1)
                            pe.wait_ge(R["y_squared"], j - 1)
                            mm(bank[4][:], head_mean[:], ysq[:], start=True, stop=True).then_inc(R["var_summed"], 1)

        def recurrence_evac(eng, h, j, b, c, phase):
            hs = slice(h * C, (h + 1) * C)
            scaled = (lambda o_, i_, f: nc.vector.tensor_scalar(o_, i_, f, None, ALU.mult)) if h == 0 else \
                     (lambda o_, i_, f: nc.scalar.activation(o_, i_, ACT.Copy, scale=f))
            if phase == 0:
                eng.wait_ge(R["rhs_summed"], NCH * j + c + 1)
                scaled(rhs[hs, :], bank[5][hs, 0:C], 1.0).then_inc(R["rhs_copied"][h], 1)
            elif phase == 1:
                eng.wait_ge(R["u_summed"], NCH * j + c + 1)
                scaled(sv[b][hs, c, h, :], bank[5][hs, C:2 * C], -1.0).then_inc(R["u_copied"][h], 1)
            elif c < NCH - 1:
                eng.wait_ge(R["s_summed"], NCH * j + c + 1)
                scaled(sv[b][hs, c + 1, h, :], bank[6][hs, 0:C], st_pc[j % 3][hs, c:c + 1]).then_inc(R["s_copied"][h], 1)

        def blocks(bk):
            return bank[bk][:].rearrange("p (c k) -> p c k", c=4)

        def recurrence_scalar(act, o):
            A = nc.scalar.activation
            act.wait_ge(s_const, 3)
            for j in range(CI + 2):
                b = j % 2
                if j == 1:
                    act.wait_ge(s_spill, SPILL_MIX + SPILL_TILE * CI)
                for s in range(3 * NCH):
                    if s == 0 and when(j - 2, CI):
                        act.wait_ge(R["y_summed"], j - 1)
                        A(y0[:], bank[7][:], ACT.Copy).then_inc(R["y_bank_read"], 1)
                    if when(j - 1, CI):
                        recurrence_evac(act, 1, j - 1, 1 - b, s // 3, s % 3)
                    if when(j, CI):
                        if s in (1, 5):
                            g = s // 4
                            act.wait_ge(R["turned"], 2 * j + g + 1)
                            o(A(bt[b][:, 4 * g:4 * g + 4, :], blocks(0), ACT.Copy))
                        elif s in (2, 6):
                            g = (s - 2) // 4
                            v = blocks(1)
                            o(A(sv[b][0:C, 4 * g:4 * g + 4, 1, :], v[0:C, :, C:P], ACT.Copy))
                            n = 4 - g
                            copy = A(sv[b][C:P, 4 * g + 1:4 * g + 1 + n, 0, :], v[C:P, 0:n, 0:C], ACT.Copy)
                            if g == 1:
                                o(copy)
                                copy = A(sv[b][C:P, 0, 0, :], v[C:P, 3, 0:C], ACT.Copy)
                            copy.then_inc(R["turned_copied"], 1)
                        elif s == 8:
                            act.wait_ge(R["turned_copied"], 2 * j + 2)
                            A(sv[b][C:P, 0, 1, :], sv[b][C:P, 0, 0, :], ACT.Copy, scale=0.0).then_inc(
                                R["state_zeroed"][1], 1)
                        elif s == S_NEWTON - 1:
                            for g in range(2):
                                act.wait_ge(R["r0_summed"], 2 * j + g + 1)
                                A(inv16[:, 4 * g:4 * g + 4, :], blocks(1 + g), ACT.Copy).then_inc(R["r0_copied"], 1)
                        elif S_NEWTON <= s < S_NEWTON + 10 and (s - S_NEWTON) % 2:
                            level = (s - S_NEWTON + 1) // 2
                            first, second = ((1, 2), (0, 3)) if level % 2 else ((0, 3), (1, 2))
                            for n, (dst, bk) in enumerate(((inv16[:, 0:4, :], first[0]), (inv_t16[:, 0:4, :], first[1]),
                                                           (inv16[:, 4:8, :], second[0]))):
                                act.wait_ge(R["rq_summed"], 20 * j + 4 * (level - 1) + n + 1)
                                A(dst, blocks(bk), ACT.Copy).then_inc(R["rq_copied"], 1)
                        elif s == S_NEWTON + 10:
                            act.wait_ge(R["e_summed"], 2 * j + 1)
                            A(w16[:, 0:4, :], blocks(1), ACT.Copy).then_inc(R["e_copied"][0], 1)
                        elif s == S_NEWTON + 11:
                            act.wait_ge(R["t_summed"], 2 * j + 1)
                            A(tt[b][:, 0:4, :], blocks(0), ACT.Copy).then_inc(R["inverse_made"][0], 1)
                    if when(j - 2, CI):
                        if s == 3:
                            act.wait_ge(R["centered"], j - 1)
                            if j >= 3:
                                act.wait_ge(R["y_finished"], j - 2)
                            A(yc[:], bank[4][:], ACT.Copy).then_inc(R["centered_copied"], 1)
                            act.wait_ge(R["centered_copied"], j - 1)
                            A(ysq[:], yc[:], ACT.Square).then_inc(R["y_squared"], 1)
                        if s == 8:
                            act.wait_ge(R["var_summed"], j - 1)
                            o(A(yr[:], bank[4][:], ACT.Ln, bias=eps[:, 1:2]))
                            A(yr[:], yr[:], ACT.Exp, scale=-0.5).then_inc(R["y_rstd_made"], 1)

        def recurrence_vector(dve, o):
            V = nc.vector
            incl, strict = masks[:, 0:C], masks[:, P:P + C]
            dve.wait_ge(s_const, 4)

            def wide(m, lo, hi, n):
                return m[lo:hi].unsqueeze(1).to_broadcast([hi - lo, n, C])

            for j in range(CI + 2):
                b = j % 2
                if j == 1:
                    dve.wait_ge(s_spill, SPILL_MIX + SPILL_TILE * CI)
                for s in range(3 * NCH):
                    if when(j - 1, CI):
                        recurrence_evac(dve, 0, j - 1, 1 - b, s // 3, s % 3)
                    if not when(j, CI):
                        continue
                    TT = V.tensor_tensor
                    g = int(s >= 5)
                    cr = slice(4 * g, 4 * g + 4)
                    p0, p1 = (bank[2 + h][:].rearrange("p (c a k) -> p c a k", c=4, a=2) for h in range(2))
                    if s in (1, 5):
                        dve.wait_ge(R["products_summed"], 2 * j + g + 1)
                        for hs, p in ((slice(0, C), p0[0:C, :, 0, :]), (slice(C, P), p1[C:P, :, 1, :])):
                            V.scalar_tensor_tensor(out=nix[hs, cr, :], in0=p, scalar=-1.0,
                                                   in1=wide(strict, hs.start, hs.stop, 4), op0=ALU.mult,
                                                   op1=ALU.mult).then_inc(R["nix_made"], 1)
                    if s in (2, 6):
                        for h in range(2):
                            hs = slice(h * C, (h + 1) * C)
                            dve.wait_ge(R["nix_made"], 4 * j + 2 * g + h + 1)
                            TT(nix16[hs, cr, hs], nix[hs, cr, :], eyes[hs, cr, :], ALU.subtract).then_inc(
                                R["nix16_made"], 1)
                    if s in (4, 7):
                        g = s // 7
                        cr = slice(4 * g, 4 * g + 4)
                        dve.wait_ge(R["nix16_made"], 4 * j + 2 * g + 2)
                        TT(inv_t16[:, cr, :], nix16[:, cr, :],
                           bmask[:, 0, :].unsqueeze(1).to_broadcast([P, 4, P]), ALU.mult).then_inc(R["q0_made"], 1)
                    if s in (2, 8):
                        TT(st_q[j % 3][C:P, cr, 0, :], p0[C:P, :, 0, :], wide(strict, C, P, 4), ALU.mult)
                        TT(st_q[j % 3][0:C, cr, 2, :], p1[0:C, :, 1, :], wide(strict, 0, C, 4), ALU.mult)
                    if s in (3, 8):
                        TT(ra[b][:, cr, 0, :], p0[:, :, 1, :], wide(incl, 0, P, 4), ALU.mult)
                        TT(ra[b][:, cr, 1, :], p1[:, :, 0, :], wide(incl, 0, P, 4), ALU.mult).then_inc(
                            R["products_masked"], 1)
                    if s == 8:
                        dve.wait_ge(R["products_masked"], 2 * j + 2)
                        V.memset(sv[b][0:C, 0, 0, :], 0.0).then_inc(R["state_zeroed"][0], 1)
                    if S_NEWTON <= s < S_NEWTON + 10 and (s - S_NEWTON) % 2 == 0:
                        level = (s - S_NEWTON) // 2 + 1
                        for g in range(2):
                            dve.wait_ge(R["v_summed"], 10 * j + 2 * (level - 1) + g + 1)
                            src = blocks(((1, 2), (0, 3))[level % 2][g])
                            dst = w16[:, 4 * g:4 * g + 4, :]
                            (TT(dst, src, bmask[:, level, :].unsqueeze(1).to_broadcast([P, 4, P]), ALU.mult)
                             if level < 5 else V.tensor_copy(dst, src)).then_inc(R["v_copied"], 1)
                    elif S_NEWTON <= s < S_NEWTON + 10:
                        level = (s - S_NEWTON + 1) // 2
                        dve.wait_ge(R["rq_summed"], 20 * j + 4 * level)
                        V.tensor_copy(inv_t16[:, 4:8, :], blocks(3 if level % 2 else 2)).then_inc(R["q1_copied"], 1)
                    elif s == S_NEWTON + 10:
                        dve.wait_ge(R["e_summed"], 2 * j + 2)
                        V.tensor_copy(w16[:, 4:8, :], blocks(2)).then_inc(R["e_copied"][1], 1)
                    elif s == S_NEWTON + 11:
                        dve.wait_ge(R["t_summed"], 2 * j + 2)
                        V.tensor_copy(tt[b][:, 4:8, :], blocks(3)).then_inc(R["inverse_made"][1], 1)

        def recurrence_gpsimd(gp, o):
            G = nc.gpsimd
            for j in range(CI + 2):
                b = j % 2
                if when(j - 2, CI):
                    gp.wait_ge(R["y_rstd_made"], j - 1)
                    gp.wait_ge(R["ends_loaded"][b], 32 * (j // 2))
                    o(G.tensor_tensor(y2[:], yc[:], yr[:], ALU.mult))
                    o(G.tensor_scalar(y2[:], y2[:], col("a_lnw", j - 2), col("a_lnb", j - 2), ALU.mult, ALU.add))
                    o(G.tensor_tensor(y2[:], y2[:], st_bv[b][:], ALU.add))
                    G.tensor_tensor(Y[:, j - 2, :], y2[:], st_g[b][:], ALU.mult).then_inc(R["y_finished"], 1)
                    gp.wait_ge(R["y_finished"], j - 1)
                if when(j, CI):
                    gp.wait_ge(R["q0_made"], 2 * j + 2)
                    o(G.tensor_tensor(nixe[:], nix[:], eyes[:], ALU.subtract))
                    for h in range(2):
                        hs = slice(h * C, (h + 1) * C)
                        G.tensor_tensor(nixlo16[hs, :, hs], nixe[hs], nix16[hs, :, hs], ALU.subtract).then_inc(
                            R["low_made"], 1)
                        gp.wait_ge(R["low_made"], 2 * j + h + 1)

        ITEMS = NHEAD2 * NT

        def item(m):
            h, n = m // NT, NT - 1 - m % NT
            return h, n, slice((h % 2) * C, (h % 2 + 1) * C), slice(n * P, T), slice(ATT_AT[n], ATT_AT[n + 1])

        LN_AT = 2
        GATES_FIRST = LN_AT + 7

        def gate_at(s):
            n = GATES_FIRST + (s - 1) // 4
            return n if s >= 1 and (s - 1) % 4 == 0 and n < 2 * DK else None

        def attention_tensor(pe, gate):
            mm = nc.tensor.matmul

            def scores(m):
                h, n, rows, seen, _ = item(m)
                if m == 0:
                    pe.wait_ge(s_vtok, NT)
                    pe.wait_ge(s_lrs, 1)
                if m >= 2:
                    pe.wait_ge(s_neg, m - 1)
                mm(bank[2 + m % 2][:, seen], kT[rows, h // 2, n * P:(n + 1) * P], qT[rows, h // 2, seen], start=True,
                   stop=True).then_inc(s_sc2, 1)

            def sums(m):
                h, n, _, seen, cols = item(m)
                pe.wait_ge(s_sp, m + 1)
                if m >= 2:
                    pe.wait_ge(s_dif, m - 1)
                last = mm(bank[4 + m % 2][:, seen], att_from[:], att_sp[:, h % 2, cols], start=True, stop=n == NT - 1)
                for later in range(n + 1, NT):
                    last = mm(bank[4 + m % 2][:, later * P:T], att_ones[:],
                              att_sp[:, h % 2, ATT_AT[later]:ATT_AT[later + 1]], start=False, stop=later == NT - 1)
                last.then_inc(s_cum, 1)

            def values(h):
                pe.wait_ge(s_wt, NT * (h + 1))
                if h >= 4:
                    pe.wait_ge(s_tmp, made(X_AT + h // 2 - 2))
                for n in range(NT):
                    last = mm(bank[6 + h // 2 % 2][(h % 2) * C:(h % 2 + 1) * C, n * P:T], vtok[:, n, h * C:(h + 1) * C],
                              att_a[:, h % 2, ATT_AT[n]:ATT_AT[n + 1]], start=n == 0, stop=n == NT - 1)
                last.then_inc(s_o, 1)

            for s in range(-1, ITEMS + 5):
                if when(s + 1, ITEMS):
                    scores(s + 1)
                if when(s - 1, ITEMS):
                    sums(s - 1)
                if when(s - 3, ITEMS) and (s - 3) % NT == NT - 1:
                    values((s - 3) // NT)
                gate(gate_at(s))

        def attention_scalar(act, o, x_high, gate):
            A = nc.scalar.activation
            for s in range(ITEMS + 5):
                if when(s, ITEMS):
                    seen = item(s)[3]
                    z, t = att_z[s % 4][:, seen], sq[:, s % 2, seen]
                    act.wait_ge(s_sc2, s + 1)
                    if s >= 4:
                        act.wait_ge(s_dif, s - 3)
                    A(z, bank[2 + s % 2][:, seen], ACT.Copy).then_inc(s_neg, 1)
                    act.wait_ge(s_neg, s + 1)
                    if s >= 2:
                        act.wait_ge(s_sp, s - 1)
                    o(A(t, z, ACT.Abs))
                    o(A(t, t, ACT.Exp, scale=-1.0))
                    A(t, t, ACT.Ln, bias=1.0).then_inc(s_log, 1)
                if when(s - 2, ITEMS):
                    h, n, _, seen, cols = item(s - 2)
                    t = att_a[:, h % 2, cols]
                    act.wait_ge(s_dif, s - 1)
                    A(t, t, ACT.Exp).then_inc(s_wt, 1)
                if when(s - 4, ITEMS) and (s - 4) % (2 * NT) == 2 * NT - 1:
                    pair = (s - 4) // (2 * NT)
                    x_high(X_AT + pair, ah[:, 0, pair, :], pair % 2)
                gate(gate_at(s))

        def attention_vector(dve, o, finish, gate):
            V = nc.vector
            for s in range(ITEMS + 5):
                if when(s - 1, ITEMS):
                    m = s - 1
                    h, n, rows, seen, cols = item(m)
                    dve.wait_ge(s_log, m + 1)
                    o(V.scalar_tensor_tensor(out=att_sp[:, h % 2, cols], in0=att_z[m % 4][:, seen], scalar=0.0,
                                             in1=sq[:, m % 2, seen], op0=ALU.max, op1=ALU.add))
                    t = att_sp[:, h % 2, ATT_AT[n]:ATT_AT[n] + P]
                    V.tensor_tensor(t, t, att_keep[:], ALU.mult).then_inc(s_sp, 1)
                if when(s - 2, ITEMS):
                    m = s - 2
                    h, n, rows, seen, cols = item(m)
                    dve.wait_ge(s_cum, m + 1)
                    if m % NT == 0 and h >= 2:
                        dve.wait_ge(s_o, h - 1)
                    o(V.tensor_tensor(att_a[:, h % 2, cols], att_z[m % 4][:, seen], bank[4 + m % 2][:, seen],
                                      ALU.subtract))
                    t = att_a[:, h % 2, ATT_AT[n]:ATT_AT[n] + P]
                    V.scalar_tensor_tensor(out=t, in0=t, scalar=0.0, in1=att_drop[:], op0=ALU.min,
                                           op1=ALU.add).then_inc(s_dif, 1)
                if when(s - 4, ITEMS) and (s - 4) % (2 * NT) == 2 * NT - 1:
                    pair = (s - 4) // (2 * NT)
                    dve.wait_ge(s_o, 2 * pair + 2)
                    finish(pair, lambda where: V.tensor_copy(where, bank[6 + pair % 2][:]))
                gate(gate_at(s))

        def later_panels(sp, panel):
            sp.wait_ge(R["y_finished"], CI)
            sp.dma_start(xT2[:], d_x).then_inc(s_back, 16)
            w_out1, w_conv, w_out_conv = i["a_w_out"][0], i["b_w_in"][0], i["b_w_out"][0]

            def even(base, turns, mat, row, nkb, col0, first=0):
                def turn(t):
                    for u in range(2):
                        panel(2 * t + (base + u + 2 * first), u, mat, row, nkb, t * (2 * P) + (col0 + (u + 2 * first) * P))
                repeat(sp, turns - first, turn)

            def pairs(base, turns, mat, nkb, col_a, col_b):
                def turn(t):
                    for u, c0 in enumerate((col_a, col_b)):
                        panel(2 * t + (base + u), u, mat, 0, nkb, t * P + c0)
                repeat(sp, turns, turn)

            even(U_OUT1, DK // 2, w_out1, 0, KB, 0, first=1)
            even(U_OUT1 + DK, DK // 2, w_out1, D, KB, 0)
            for half in range(2):
                base = U_CONV + half * (4 * KB + DK)

                def conv(t):
                    for u, part in enumerate((0, 2, 3, 1)):
                        panel(4 * t + (base + u), u % 2, w_conv, 0, KB, t * P + (part * DI + half * D))
                repeat(sp, KB, conv)
                even(base + 4 * KB, DK // 2, w_out_conv, half * D, KB, 0)
            w2 = i["w_in_2"]
            pairs(U_GLU, CT, w2, KB, 0, CT * P)
            even(U_QKV, 3 * AT // 2, w2, 0, KB, 2 * CT * P)
            gate_col = 2 * CT * P + 3 * AD
            pairs(U_GATES2, DK, w2, KB, gate_col, gate_col + D)

            def merge(t):
                for u in range(2):
                    n, c0 = 2 * t + (U_MERGE + u), t * (2 * P) + u * P
                    panel(n, u, i["w_conv_branch_2"], 0, CT, c0)
                    panel(n, u, i["w_att_branch_2"], 0, AT, c0, kb0=CT, first=False)
            repeat(sp, DK // 2, merge)
            even(U_WOUT2, DK // 2, i["w_out_2"], 0, KB, 0)
            base = U_FFN
            for j0, n in FPARTS:
                pairs(base, n, i["w_ffn_up_2"], KB, j0 * P, (FT + j0) * P)
                even(base + 2 * n, DK // 2, i["w_ffn_down_2"], j0 * P, n, 0)
                base += 2 * n + DK
            for k in range(0, DK, 2):
                sp.wait_ge(s_yc, k + 2)
                cols = slice(k * P, (k + 2) * P)
                sp.dma_start(out[0, :, cols].rearrange("(q p) d -> p q d", p=P), staged[:, :, cols]).then_inc(s_out, 16)
            sp.wait_ge(s_out, 16 * DK // 2)

        @block.sync
        def _(sp):
            def panel(n, slot, mat, row, nkb, col, ncol=P, kb0=0, first=True, rows=P):
                src = mat[row:row + nkb * rows, bass.ds(col, ncol)].rearrange("(k p) c -> p k c", p=rows)
                if first and not (isinstance(n, int) and n < 2):
                    sp.wait_ge(s_lo, n - 1)
                sp.dma_start(w_raw[0:rows, slot, kb0:kb0 + nkb, 0:ncol], src).then_inc(s_raw[slot], 16)

            sp.dma_start(x_raw[:], i["x"].rearrange("b (q p) d -> p (b q) d", p=P)).then_inc(s_xin, 16)
            panel(0, 0, i["a_w1"][0], 0, KB, 0, LORA)
            panel(1, 1, i["a_a1"][0], 0, KB, 0, LORA)

            def gate(t, u):
                panel(2 * t + (U_GATE + u), u, w_in[3], 0, KB, t * (2 * P) + u * P)

            def spill_gate(t, u):
                sp.wait_ge(s_free[u], t + 2)
                sp.dma_start(d_g[2 * t + u], sq[:, u, :]).then_inc(s_spill, 16)

            def mix(j, u, c0=0):
                if u == 1:
                    panel(4 * j + (U_MIX + 1), 1, i["a_w2"][0], 0, 1, c0, rows=LORA)
                    panel(4 * j + (U_MIX + 1), 1, i["a_a2"][0], 0, 1, c0, kb0=1, first=False, rows=LORA)
                else:
                    panel(4 * j + (U_MIX + u), u % 2, w_in[(1, None, 0, 2)[u]], 0, KB, c0 if u == 2 else j * P)

            def spill_mix(j):
                sp.wait_ge(s_free[0], 2 * j + (FREE_MIX + 2))
                sp.dma_start(d_r[j], o_r[:]).then_inc(s_spill, 16)
                sp.dma_start(d_pc[j], o_pc[:]).then_inc(s_spill, 16)
                for n, (dst, src) in enumerate(((d_q, o_q), (d_b, o_b), (d_c, o_c))):
                    sp.wait_ge(s_fin, 4 * j + (n + 1))
                    sp.dma_start(dst[j], src[:]).then_inc(s_spill, 16)
                sp.wait_ge(s_free[1], 2 * j + (FREE_MIX + 2))
                sp.dma_start(d_v[j], o_v[:]).then_inc(s_spill, 16)
                sp.wait_ge(s_fin, 4 * j + 4)
                sp.dma_start(d_bv[j], o_bv[:]).then_inc(s_spill, 16)

            sp.wait_ge(s_xt, DK)
            sp.dma_start(d_x, xT[:]).then_inc(s_spill, 16)
            for u in range(4):
                gate(u // 2, u % 2)

            def gate_turn(t):
                for u in range(2):
                    spill_gate(t, u)
                    gate(t + 2, u)
            repeat(sp, CI // 2 - 2, gate_turn)
            for u in range(4):
                spill_gate(CI // 2 - 2 + u // 2, u % 2)
                mix(0, u)

            def mix_turn(j):
                for u in range(4):
                    if u == 3:
                        spill_mix(j)
                    mix(j + 1, u, j * P + P)
            repeat(sp, CI - 1, mix_turn)
            panel(U_OUT1, 0, i["a_w_out"][0], 0, KB, 0)

            def load(j):
                b, b3 = j % 2, j % 3
                if j >= 2:
                    sp.wait_ge(R["turned"], 2 * (j - 1))
                if j >= 3:
                    sp.wait_ge(R["y_summed"], j - 2)
                half = lambda a, h: a[j, h * C:(h + 1) * C, :].rearrange("p (c t) -> p c t", c=NCH)
                for h, (slot_b, slot_c) in enumerate(((0, 1), (1, 0))):
                    hs = slice(h * C, (h + 1) * C)
                    for dst, src in ((st_q[b3][hs, :, 2 * h, :], d_q), (st_bc[b][hs, :, slot_b, :], d_b),
                                     (st_bc[b][hs, :, slot_c, :], d_c)):
                        sp.dma_start(dst, half(src, h)).then_inc(R["tiles_loaded"][b], 16)
                whole = d_r[j].rearrange("p (c t) -> p c t", c=NCH)
                for dst, src in ((st_q[b3][:, :, 1, :], whole), (st_v[b][:, 0:T], d_v[j]),
                                 (st_v[b][:, T:T + C], d_v[j, :, 0:C]), (st_pc[b3][:], d_pc[j])):
                    sp.dma_start(dst, src).then_inc(R["tiles_loaded"][b], 16)

            sp.wait_ge(s_spill, SPILL_MIX + SPILL_TILE * (CI - 1))
            sp.wait_ge(s_unit, U_MIX + 4 * (CI - 1) + 1)
            load(0)
            load(1)
            spill_mix(CI - 1)
            panel(U_OUT1 + 1, 1, i["a_w_out"][0], 0, KB, P)
            sp.wait_ge(s_spill, SPILL_MIX + SPILL_TILE * CI)
            sp.wait_ge(s_unit, U_OUT1)
            for j in range(CI):
                if j >= 2:
                    sp.wait_ge(R["y_finished"], j - 1)
                sp.dma_start(st_bv[j % 2][:], d_bv[j]).then_inc(R["ends_loaded"][j % 2], 16)
                sp.dma_start(st_g[j % 2][:], d_g[j]).then_inc(R["ends_loaded"][j % 2], 16)
                if j + 2 < CI:
                    load(j + 2)
            later_panels(sp, panel)

        @block.gpsimd
        def _(gp):
            o = Order(gp, s_gseq)
            gt = nc.gpsimd
            o(gt.memset(ident[:], 0.0))
            o(gt.affine_select(out=ident[:], in_=ident[:], compare_op=ALU.not_equal, fill=1.0, base=0,
                               pattern=[[-1, P]], channel_multiplier=1))
            o(gt.memset(mean_d[:], 1.0 / D))
            o(gt.memset(head_ones[:], 0.0))
            o(gt.memset(head_ones[0:C, 0:C], 1.0))
            o(gt.memset(head_ones[C:P, C:P], 1.0))
            o(gt.memset(eps[:, 0:1], RMS_EPS))
            o(gt.memset(eps[:, 1:2], GN_EPS))
            o(gt.memset(eps[:, 2:3], 0.5 * NSHIFT * LN2))
            o(gt.memset(masks[:], 1.0))
            for m in (att_ones, att_from, att_keep, att_drop):
                o(gt.memset(m[:], 0.0 if m is att_drop else 1.0))
            o(gt.affine_select(out=att_from[:], in_=att_from[:], compare_op=ALU.is_ge, fill=0.0, base=0,
                               pattern=[[-1, P]], channel_multiplier=1))
            o(gt.affine_select(out=att_keep[:], in_=att_keep[:], compare_op=ALU.is_gt, fill=0.0, base=0,
                               pattern=[[1, P]], channel_multiplier=-1))
            o(gt.affine_select(out=att_drop[:], in_=att_drop[:], compare_op=ALU.is_gt, fill=-1e30, base=0,
                               pattern=[[1, P]], channel_multiplier=-1))
            for h in range(2):
                hs = slice(h * C, (h + 1) * C)
                incl = masks[hs, 0:P].rearrange("p (a t) -> p a t", a=2)
                o(gt.affine_select(out=incl, in_=incl, compare_op=ALU.is_ge, fill=0.0, base=0,
                                   pattern=[[0, 2], [1, C]], channel_multiplier=-1))
                o(gt.affine_select(out=masks[hs, P:P + C], in_=masks[hs, P:P + C], compare_op=ALU.is_gt,
                                   fill=0.0, base=0, pattern=[[1, C]], channel_multiplier=-1))
            gt.memset(hT[:, :, 0:1], 0.0).then_inc(s_const, 1)
            gp.wait_ge(s_ms, 1)
            for n in range(2 * DK):
                gp.wait_ge(s_hT, n % DK + 1)
                if n >= 2:
                    gp.wait_ge(s_tmp, 2 * (n - 1) if n - 2 < DK else n - 1 + DK)
                gt.tensor_tensor(sq[:, n % 2, :], hT[:, n % DK, 0:T], hT[:, n % DK, 1:T + 1], ALU.subtract).then_inc(
                    s_dif1, 1)
            gp.wait_ge(s_xlo, X_Y)
            o(gt.memset(scanm[:], 1.0))
            o(gt.memset(scanm[:, :, 0:1], 0.0))
            gt.memset(lw[:, :, 0:1], 0.0).then_inc(s_const, 1)

            gp.wait_ge(s_spill, 16)
            o(gt.memset(bmask[:], 1.0))
            for n, m in enumerate((2, 4, 8, 16, 32)):
                v = bmask[:, n, :].rearrange("p (a b) -> p a b", b=m)
                o(gt.affine_select(out=v, in_=v, compare_op=ALU.is_ge, fill=0.0, base=0,
                                   pattern=[[-m, P // m], [0, m]], channel_multiplier=1))
                o(gt.affine_select(out=v, in_=v, compare_op=ALU.is_ge, fill=0.0, base=m - 1,
                                   pattern=[[m, P // m], [0, m]], channel_multiplier=-1))
            o(gt.affine_select(out=bmask[:, 0, :], in_=bmask[:, 0, :], compare_op=ALU.not_equal, fill=-1.0, base=0,
                               pattern=[[-1, P]], channel_multiplier=1))
            o(gt.memset(eyes[:], 0.0))
            for h in range(2):
                v = eyes[h * C:(h + 1) * C]
                o(gt.affine_select(out=v, in_=v, compare_op=ALU.not_equal, fill=1.0, base=0,
                                   pattern=[[0, NCH], [-1, C]], channel_multiplier=1))
            for c in range(4):
                o(gt.tensor_copy(eyes16[:, c, :], ident[:]))
            o(gt.tensor_copy(one16[:], ident[:]))
            o(gt.tensor_scalar(two16[:], ident[:], 2.0, 0.0, ALU.mult, ALU.add))
            o(gt.tensor_scalar(head_mean[:], head_ones[:], 1.0 / C, 0.0, ALU.mult, ALU.add))
            gt.tensor_tensor(center[:], ident[:], head_mean[:], ALU.subtract).then_inc(s_const, 1)
            gp.wait_ge(s_unit, U_OUT1)
            o(gt.memset(nix16[:], 0.0))
            gt.memset(nixlo16[:], 0.0).then_inc(s_const, 1)
            gp.wait_ge(s_spill, SPILL_MIX + SPILL_TILE * CI)
            recurrence_gpsimd(gp, o)
            gp.wait_ge(s_gluok, 1)
            y = dconv[:, 0, :]
            o(gt.tensor_scalar(y, glu[:, 0, 0:T], col("conv_dw_w_2", 0), col("conv_dw_b_2", 0), ALU.mult, ALU.add))
            for tap in range(1, TAPS2):
                o(gt.tensor_scalar(tapped[:], glu[:, 0, tap:tap + T], col("conv_dw_w_2", tap * CT), None, ALU.mult))
                ins = gt.tensor_tensor(y, y, tapped[:], ALU.add)
                ins.then_inc(s_tap0, 1) if tap == TAPS2 - 1 else o(ins)

        @block.scalar
        def _(act):
            o = Order(act, s_aseq)
            A = nc.scalar.activation
            nc.scalar.add_instruction(mybir.InstLoadActFuncSet(
                name=nc.get_next_instruction_name(), act_func_set_id=EXP_LN_SET, ins=[], outs=[]))
            for t, rows in enumerate(PARAMS):
                row = 0
                for name, n in rows:
                    src = i[name]
                    letters = " ".join("abcd"[:len(src.shape)])
                    flat = src.rearrange(f"{letters} -> ({letters})") if len(src.shape) > 1 else src
                    act.dma_start(par_raw[row:row + n, t, :], flat.rearrange("(r c) -> r c", c=P)).then_inc(s_par, 16)
                    row += n

            def w_high(n, slot, count, ncol=P, rows=P, nkb=KB):
                act.wait_ge(s_raw[slot], count)
                if not (isinstance(n, int) and n < 2):
                    act.wait_ge(s_unit, n - 1)
                A(w_hi[0:rows, slot, 0:nkb, 0:ncol], w_raw[0:rows, slot, 0:nkb, 0:ncol], ACT.Copy).then_inc(s_hi, 1)

            def x_high(q, hi, buf):
                act.wait_ge(s_tmp, made(q))
                A(hi, tmp[:, buf, :], ACT.Copy).then_inc(s_xhi, 1)

            def sigmoid(z):
                o(A(z, z, ACT.Exp, scale=-1.0))
                o(A(z, z, ACT.Ln, bias=1.0))
                return A(z, z, ACT.Exp, scale=-1.0)

            def norm(n, x=xT, ready=None):
                for k in range(DK if x is not None else 0):
                    if ready is not None:
                        act.wait_ge(*ready(k))
                    if n or k >= 2:
                        act.wait_ge(s_sqa, n * DK + k - 1)
                    A(sq[:, k % 2, :], x[:, k, :], ACT.Square).then_inc(s_sq, 1)
                if n in SUMMED_BY_PE:
                    act.wait_ge(s_sqa, (n + 1) * DK)
                else:
                    act.wait_ge(s_ms, n + 1 - sum(m < n for m in SUMMED_BY_PE))
                o(A(rstd[:, 0, :], bank[4][:], ACT.Ln, bias=eps[:, 0:1]))
                A(rstd[:, 1, :], rstd[:, 0, :], ACT.Exp, scale=-0.5).then_inc(s_rs, 1)

            for k in range(DK):
                act.wait_ge(s_tr, k + 1)
                A(xT[:, k, :], bank[k % 4][:], ACT.Copy).then_inc(s_xt, 1)
            act.wait_ge(s_const, 1)
            act.wait_ge(s_xt, DK)
            norm(0)
            w_high(0, 0, panels_by(0), LORA)
            w_high(1, 1, panels_by(1), LORA)
            for k in range(DK):
                x_high(2 * k, xl[0][:, 0, k, :], 0)
                x_high(2 * k + 1, xl[1][:, 0, k, :], 1)
            for k in range(DK):
                x_high(X_G + k, xh[:, 0, k, :], k % 2)
            act.wait_ge(s_free[0], 1)
            z = rstd[0:LORA, 0, :]
            o(A(z, z, ACT.Exp, scale=-2.0))
            o(A(z, z, ACT.Ln, bias=1.0))
            A(z, z, ACT.Exp, scale=-1.0).then_inc(s_lsig, 1)
            w_high(U_GATE, 0, panels_by(U_GATE))
            act.wait_ge(s_spill, 16)
            act.wait_ge(s_lhid, 1)
            A(lora[:, 0, 0, :], rstd[0:LORA, 0, :], ACT.Copy).then_inc(s_lhi, 1)
            act.wait_ge(s_free[1], 1)
            A(lora[:, 1, 0, :], rstd[0:LORA, 1, :], ACT.Copy).then_inc(s_lhi, 1)

            def gate(t):
                for u in range(2):
                    w_high(2 * t + (U_GATE + u + 1), 1 - u, panels(U_GATE, 2, t, u + 1))
                    act.wait_ge(s_z, 2 * t + (u + 1))
                    sigmoid(rstd[:, u, :]).then_inc(s_sg, 1)
                    for n in (range(2) if u == 0 else range(2, 3)):
                        x_high(3 * t + (X_RKV + n), xl[n][:, 0, bass.ds(t, 1), :], n % 2)
            repeat(act, CI // 2 - 1, gate, o, 4)
            gate(CI // 2 - 1)

            def mix(j):
                n0 = 4 * j + U_MIX
                w_high(n0 + 1, 1, panels(U_MIX, 4, j, 1), rows=LORA, nkb=2)
                w_high(n0 + 2, 0, panels(U_MIX, 4, j, 2))
                act.wait_ge(s_kk, j + 1)
                A(sqk[:], kk[:], ACT.Square).then_inc(s_sqk, 1)
                act.wait_ge(s_zw, j + 1)
                sigmoid(zw[:]).then_inc(s_sw, 1)
                act.wait_ge(s_free[1], 2 * j + (FREE_MIX + 1))
                sigmoid(za[:]).then_inc(s_sa, 1)
                w_high(n0 + 3, 1, panels(U_MIX, 4, j, 3))
                act.wait_ge(s_cs, j + 1)
                act.wait_ge(s_spill, j * SPILL_TILE + SPILL_MIX)
                o(A(pw[:], cs[:], ACT.Exp))
                A(o_pc[:], cs[:, :, C], ACT.Exp)
                A(pinv[:], cs[:], ACT.Exp, scale=-1.0).then_inc(s_pw, 1)
                act.wait_ge(s_n2m, j + 1)
                o(A(n2[:], n2[:], ACT.Ln, scale=float(2 ** NSHIFT)))
                A(rn[:], n2[:], ACT.Exp, scale=-0.5, bias=eps[:, 2:3]).then_inc(s_rn, 1)
                w_high(n0 + 4, 0, panels(U_MIX, 4, j, 4))
                act.wait_ge(s_unit, n0 + 4)
                A(o_v[:], bank[1][:], ACT.Copy).then_inc(s_free[1], 1)
            repeat(act, CI - 1, mix, o, 6)
            mix(CI - 1)
            recurrence_scalar(act, o)

            act.wait_ge(R["y_summed"], CI)
            for k in range(CI):
                if k in (0, DK):
                    act.wait_ge(R["y_finished"], CI - 1 if k == 0 else CI)
                A(xl[k // DK][:, 0, k % DK, :], Y[:, k, :], ACT.Copy).then_inc(s_xhi, 1)

            def ahead(base, per, t, u, last=False):
                n = panels(base, per, t, u + 1) if not last else panels_by(base + per * t + u + 1)
                w_high(per * t + (base + u + 1), (u + 1) % 2, n)

            def even(base, turns, x=None, n=None, final=False):
                def turn(t, last=False):
                    for u in range(2):
                        if not (last and u == 1):
                            ahead(base, 2, t, u)
                        if x is not None:
                            act.wait_ge(s_free[u], t + (base // 2 + 1))
                            act.wait_ge(s_sqa, 2 * t + (n * DK + u - 1))
                            A(sq[:, u, :], x[:, bass.ds(2 * t + u, 1), :], ACT.Square).then_inc(s_sq, 1)
                repeat(act, turns - final, turn)
                if final:
                    turn(turns - 1, last=True)
            even(U_OUT1, DK // 2)
            even(U_OUT1 + DK, DK // 2, xT2, 1)

            norm(1, None)
            for k in range(DK):
                x_high(X_H2 + k, xl[2][:, 0, k, :], k % 2)
            for half in range(2):
                base = U_CONV + half * (4 * KB + DK)

                def conv(t):
                    for u in range(4):
                        ahead(base, 4, t, u)
                        if u == 2:
                            act.wait_ge(s_zc, t + (KB * half + 1))
                            sigmoid(gate3[:]).then_inc(s_sc, 1)
                    act.wait_ge(s_free[1], 2 * t + (base // 2 + 2))
                    A(xl[half][:, 0, bass.ds(t, 1), :], tmp[:, 0, :], ACT.Copy).then_inc(s_xhi, 1)
                repeat(act, KB, conv, o, 2)
                even(base + 4 * KB, DK // 2, *((xT2, 2) if half else ()))

            norm(2, None)
            norm(3, xT2, lambda k: (s_xn, k + 1))
            for k in range(DK):
                x_high(X_H3 + k, xh[:, 0, k, :], k % 2)
            for j in range(CT):
                ahead(U_GLU, 2, j, 0)
                ahead(U_GLU, 2, j, 1)
                act.wait_ge(s_free[1], U_GLU // 2 + j + 1)
                sigmoid(rstd[:, j % 2, :]).then_inc(s_glu, 1)
            for n in range(3 * AT):
                ahead(U_QKV, 2, n // 2, n % 2)
            for q in range(NT):
                act.wait_ge(s_vt, q + 1)
                A(vtok[:, q, :], bank[2 + q][:], ACT.Copy).then_inc(s_vtok, 1)

            def gate2(n):
                if n is None:
                    return
                if n < 2 * DK:
                    ahead(U_GATES2, 2, n // 2, n % 2, last=True)
                if n:
                    m = n - 1
                    act.wait_ge(s_free[m % 2], U_GATES2 // 2 + m // 2 + 1)
                    sigmoid(gates[:, m % 2, m // 2, :]).then_inc(s_gate2, 1)

            def layer_norm(step):
                if step == 1:
                    for j in range(CT):
                        act.wait_ge(s_cen, j + 1)
                        if j >= 2:
                            act.wait_ge(s_lacc, j - 1)
                        A(sq[:, j % 2, :], dconv[:, j, :], ACT.Square).then_inc(s_lsq, 1)
                if step == 2:
                    act.wait_ge(s_lnm, 2)
                    o(A(rstd[:, 0, :], bank[4][:], ACT.Ln, bias=eps[:, 0:1], scale=2.0))
                    A(rstd[:, 1, :], rstd[:, 0, :], ACT.Exp, scale=-0.5).then_inc(s_lrs, 1)
                if step >= 3:
                    j = step - 3
                    act.wait_ge(s_lz, j + 1)
                    sigmoid(sq[:, j % 2, :]).then_inc(s_ls, 1)
                    x_high(X_UC + j, uc[:, 0, j, :], j % 2)
            for n in range(GATES_FIRST):
                gate2(n)
                layer_norm(n - LN_AT)
            attention_scalar(act, o, x_high, gate2)
            gate2(2 * DK)
            for n in range(DK):
                ahead(U_MERGE, 2, n // 2, n % 2, last=True)
                x_high(X_MG + n, xh[:, 0, n, :], n % 2)
            even(U_WOUT2, DK // 2, mixed, 4)
            norm(4, None)
            norm(5, xT2, lambda k: (s_mg, k + 1))
            for k in range(DK):
                x_high(X_H4 + k, xl[0][:, 0, k, :], k % 2)
            base = U_FFN
            for part, (j0, n) in enumerate(FPARTS):
                dst = xl[1 + part % 2]

                def ffn(t):
                    ahead(base, 2, t, 0)
                    act.wait_ge(s_ug, t + (j0 + 1))
                    sigmoid(rstd[:, 0, :]).then_inc(s_us, 1)
                    ahead(base, 2, t, 1)
                    act.wait_ge(s_free[1], t + (base // 2 + 1))
                    A(dst[:, 0, bass.ds(t, 1), :], tmp[:, 0, :], ACT.Copy).then_inc(s_xhi, 1)
                repeat(act, n, ffn, o, 2)
                last = part == len(FPARTS) - 1
                even(base + 2 * n, DK // 2, *((ffo, 6) if last else ()), final=last)
                base += 2 * n + DK
            norm(6, None)
            for k in range(DK):
                act.wait_ge(s_yt, k + 1)
                A(staged[:, :, k * P:(k + 1) * P], blocks(k), ACT.Copy).then_inc(s_yc, 1)

        @block.tensor
        def _(pe):
            mm, tr = nc.tensor.matmul, nc.tensor.transpose

            def three(outp, wh, wl, xhi, xlo, start, stop):
                mm(outp, wh, xlo, start=start, stop=False)
                mm(outp, wl, xhi, start=False, stop=False)
                return mm(outp, wh, xhi, start=False, stop=stop)

            def unit(n, slot, x, nkb=KB, m=P, kx=0, xcount=None, free=None):
                pe.wait_ge(s_lo, n + 1)
                if not (isinstance(n, int) and n < 2):
                    pe.wait_ge(s_free[slot], free)
                for k in range(nkb):
                    if xcount is not None:
                        pe.wait_ge(s_xlo, xcount(k))
                    last = three(bank[slot][0:m, :], w_hi[:, slot, k, 0:m], w_lo[:, slot, k, 0:m],
                                 x[:, 0, kx + k, :], x[:, 1, kx + k, :], k == 0, k == nkb - 1)
                last.then_inc(s_unit, 1)

            def norm(n):
                if n not in SUMMED_BY_PE:
                    pe.wait_ge(s_sqa, (n + 1) * DK)
                    mm(bank[4][:], mean_d[:], acc[:], start=True, stop=True).then_inc(s_ms, 1)
                else:
                    for k in range(DK):
                        pe.wait_ge(s_sq, n * DK + k + 1)
                        mm(bank[4][:], mean_d[:], sq[:, k % 2, :], start=k == 0, stop=k == DK - 1).then_inc(s_sqa, 1)

            pe.wait_ge(s_const, 1)
            pe.wait_ge(s_xin, 16)
            for k in range(DK):
                if k >= 4:
                    pe.wait_ge(s_xt, k - 3)
                for q in range(4):
                    last = tr(bank[k % 4][:, q * P:(q + 1) * P], x_raw[:, q, k * P:(k + 1) * P], ident[:])
                last.then_inc(s_tr, 1)
            pe.wait_ge(s_par, 16 * sum(len(rows) for rows in PARAMS))
            for t in range(4):
                n = PAR_ROWS[t]
                last = tr(bank[5][:, t * P:t * P + n], par_raw[0:n, t, :], ident[0:n, 0:n])
            last.then_inc(s_part, 1)
            norm(0)
            for n in range(2):
                unit(n, n, xl[n], m=LORA, xcount=lambda k: 2 * k + n + 1)

            def phase(base, per, turns, x, ready, nkb=KB):
                for u in range(per):
                    unit(base + u, u % 2, x, nkb=nkb, xcount=None if u else lambda k: ready + k + 1,
                         free=base // 2 + u // 2)

                def turn(t):
                    for u in range(per):
                        unit(per * t + (base + per + u), u % 2, x, nkb=nkb,
                             free=per // 2 * t + (base // 2 + per // 2 + u // 2))
                repeat(pe, turns - 1, turn)

            phase(U_GATE, 2, CI // 2, xh, X_G)

            def mix(j):
                n0 = 4 * j + U_MIX
                unit(n0, 0, xl[0], free=2 * j + FREE_MIX)
                pe.wait_ge(s_lo, n0 + 2)
                pe.wait_ge(s_free[1], 2 * j + FREE_MIX)
                for n in range(2):
                    last = three(bank[1 + 2 * n][:], w_hi[0:LORA, 1, n, :], w_lo[0:LORA, 1, n, :],
                                 lora[:, n, 0, :], lora[:, n, 1, :], True, True)
                last.then_inc(s_unit, 1)
                pe.wait_ge(s_sqk, j + 1)
                mm(bank[4][:], head_ones[:], sqk[:], start=True, stop=True).then_inc(s_n2, 1)
                unit(n0 + 2, 0, xl[1], free=2 * j + (FREE_MIX + 1))
                unit(n0 + 3, 1, xl[2], free=2 * j + (FREE_MIX + 1))
                pe.wait_ge(s_rk, j + 1)
                mm(bank[5][:], head_rk[:], rk[:], start=True, stop=True).then_inc(s_bon, 1)
            pe.wait_ge(s_xlo, X_Y)
            pe.wait_ge(s_lt, 2)
            repeat(pe, CI, mix)
            recurrence_tensor(pe)

            for half in range(2):
                phase(U_OUT1 + half * DK, 2, DK // 2, xl[half], X_Y + DK * half)
            norm(1)
            for half in range(2):
                base = U_CONV + half * (4 * KB + DK)
                phase(base, 4, KB, xl[2], X_H2)
                phase(base + 4 * KB, 2, DK // 2, xl[half], X_YC + KB * half)
            norm(2)
            norm(3)
            phase(U_GLU, 2, CT + 3 * AT // 2, xh, X_H3)
            v_ch = [sq[:, 0, :], sq[:, 1, :], rstd[:, 0, :], rstd[:, 1, :]]
            pe.wait_ge(s_free[1], (U_GATES2 - 1) // 2 + 1)
            for q in range(NT):
                for n in range(AT):
                    last = tr(bank[2 + q][:, n * P:(n + 1) * P], v_ch[n][:, q * P:(q + 1) * P], ident[:])
                last.then_inc(s_vt, 1)

            def gate2(n):
                if n is not None:
                    unit(U_GATES2 + n, n % 2, xh, free=(U_GATES2 + n) // 2)
            for n in range(GATES_FIRST):
                gate2(n)
                if n == LN_AT:
                    pe.wait_ge(s_dc, 2)
                    mm(bank[4][:], mean_d[:], acc[:], start=True, stop=True).then_inc(s_lnm, 1)
                if n == LN_AT + 2:
                    pe.wait_ge(s_lacc, CT)
                    mm(bank[4][:], mean_d[:], acc[:], start=True, stop=True).then_inc(s_lnm, 1)
            attention_tensor(pe, gate2)
            for n in range(DK):
                pe.wait_ge(s_lo, U_MERGE + n + 1)
                pe.wait_ge(s_free[n % 2], (U_MERGE + n) // 2)
                if n == 0:
                    pe.wait_ge(s_xlo, X_AT + AT)
                for part, (x, where) in enumerate(((uc, bank[n % 2]), (ah, bank[2 + n % 2]))):
                    for k in range(4):
                        kb = 4 * part + k
                        last = three(where[:], w_hi[:, n % 2, kb, :], w_lo[:, n % 2, kb, :], x[:, 0, k, :],
                                     x[:, 1, k, :], k == 0, k == 3)
                last.then_inc(s_unit, 1)
            phase(U_WOUT2, 2, DK // 2, xh, X_MG)
            norm(4)
            norm(5)
            base = U_FFN
            for part, (j0, n) in enumerate(FPARTS):
                phase(base, 2, n, xl[0], X_H4)
                phase(base + 2 * n, 2, DK // 2, xl[1 + part % 2], X_FF + j0, nkb=n)
                base += 2 * n + DK
            norm(6)
            for k in range(DK):
                pe.wait_ge(s_ffn, k + 1)
                for q in range(NT):
                    last = tr(bank[k][:, q * P:(q + 1) * P], xT2[:, k, q * P:(q + 1) * P], ident[:])
                last.then_inc(s_yt, 1)

        @block.vector
        def _(dve):
            o = Order(dve, s_vseq)
            V = nc.vector

            def w_low(n, slot, ncol=P, rows=P, nkb=KB):
                dve.wait_ge(s_hi, n + 1)
                part = (slice(0, rows), slot, slice(0, nkb), slice(0, ncol))
                V.tensor_tensor(w_lo[part], w_raw[part], w_hi[part].bitcast(F32), ALU.subtract).then_inc(s_lo, 1)

            def x_low(q, lo, hi, buf):
                dve.wait_ge(s_xhi, q + 1)
                V.tensor_tensor(lo, tmp[:, buf, :], hi.bitcast(F32), ALU.subtract).then_inc(s_xlo, 1)

            def norm(n, gain, dst, x=xT, summed=False):
                for k in range(0 if summed or n in SUMMED_BY_PE else DK):
                    dve.wait_ge(s_sq, n * DK + k + 1)
                    if k == 0:
                        V.tensor_copy(acc[:], sq[:, 0, :]).then_inc(s_sqa, 1)
                    else:
                        dve.wait_ge(s_sqa, n * DK + k)
                        V.tensor_tensor(acc[:], acc[:], sq[:, k % 2, :], ALU.add).then_inc(s_sqa, 1)
                dve.wait_ge(s_rs, n + 1)
                for k in range(DK):
                    dst(k, lambda where: V.scalar_tensor_tensor(
                        out=where, in0=x[:, k, :], scalar=col(gain, k), in1=rstd[:, 1, :], op0=ALU.mult, op1=ALU.mult))

            dve.wait_ge(s_part, 1)
            for t in range(4):
                o(V.tensor_copy(par[:, t, 0:PAR_ROWS[t]], bank[5][:, t * P:t * P + PAR_ROWS[t]]))
            t_ka, r_ka = PAR_AT["a_ka"]
            o(V.tensor_scalar(neg_ka[:], par[:, t_ka, r_ka:r_ka + CI], -1.0, 1.0, ALU.mult, ALU.add))
            dve.wait_ge(s_xt, DK)
            dve.wait_ge(s_const, 1)
            norm(0, "a_norm", lambda k, h: h(hT[:, k, 1:T + 1]).then_inc(s_hT, 1))
            dve.wait_ge(s_hT, DK)

            def lerp(k, mu, buf, done):
                if not (isinstance(done, int) and done < 1):
                    dve.wait_ge(s_xlo, done)
                V.scalar_tensor_tensor(out=tmp[:, buf, :], in0=acc[:], scalar=col("a_mu", k + mu * DK),
                                       in1=hT[:, bass.ds(k, 1), 1:T + 1], op0=ALU.mult,
                                       op1=ALU.add).then_inc(s_tmp, 1)

            def shift_difference(k):
                o(V.tensor_tensor(acc[:], hT[:, bass.ds(k, 1), 0:T], hT[:, bass.ds(k, 1), 1:T + 1], ALU.subtract))

            w_low(0, 0, LORA)
            w_low(1, 1, LORA)
            def first_lerp(n, k, mu, q):
                dve.wait_ge(s_dif1, n + 1)
                if q >= 2:
                    dve.wait_ge(s_xlo, q - 1)
                V.scalar_tensor_tensor(out=tmp[:, q % 2, :], in0=sq[:, n % 2, :], scalar=col("a_mu", k + mu * DK),
                                       in1=hT[:, k, 1:T + 1], op0=ALU.mult, op1=ALU.add).then_inc(s_tmp, 1)

            for k in range(DK):
                first_lerp(k, k, 1, 2 * k)
                if k:
                    x_low(2 * k - 1, xl[1][:, 1, k - 1, :], xl[1][:, 0, k - 1, :], 1)
                first_lerp(k, k, 4, 2 * k + 1)
                x_low(2 * k, xl[0][:, 1, k, :], xl[0][:, 0, k, :], 0)
            for k in range(DK):
                first_lerp(DK + k, k, 5, X_G + k)
                if k == 0:
                    x_low(X_G - 1, xl[1][:, 1, DK - 1, :], xl[1][:, 0, DK - 1, :], 1)
                else:
                    x_low(X_G + k - 1, xh[:, 1, k - 1, :], xh[:, 0, k - 1, :], (k - 1) % 2)
            x_low(X_G + DK - 1, xh[:, 1, DK - 1, :], xh[:, 0, DK - 1, :], 1)
            z = rstd[0:LORA, 0, :]
            dve.wait_ge(s_unit, 1)
            V.tensor_scalar(z, bank[0][0:LORA, :], 0.5 * CLAMP, None, ALU.max).then_inc(s_free[0], 1)
            dve.wait_ge(s_lsig, 1)
            V.tensor_scalar(z, z, 2.0, -1.0, ALU.mult, ALU.add).then_inc(s_lhid, 1)
            dve.wait_ge(s_unit, 2)
            V.tensor_copy(rstd[0:LORA, 1, :], bank[1][0:LORA, :]).then_inc(s_free[1], 1)
            w_low(U_GATE, 0)
            for n in range(2):
                dve.wait_ge(s_lhi, n + 1)
                V.tensor_tensor(lora[:, n, 1, :], rstd[0:LORA, n, :], lora[:, n, 0, :].bitcast(F32),
                                ALU.subtract).then_inc(s_lt, 1)

            def gate(t):
                n0 = 2 * t + U_GATE
                for u in range(2):
                    w_low(n0 + (u + 1), 1 - u)
                    dve.wait_ge(s_unit, n0 + (u + 1))
                    V.tensor_scalar(rstd[:, u, :], bank[u][:], CLAMP, None, ALU.max).then_inc(s_z, 1)
                    if u == 0:
                        shift_difference(t)
                    for n, mu in ((0, 2), (1, 0)) if u == 0 else ((2, 3),):
                        lerp(t, mu, n % 2, 3 * t + (X_RKV + n - (n > 0)))
                    for n in (range(2) if u == 0 else range(2, 3)):
                        x_low(3 * t + (X_RKV + n), xl[n][:, 1, bass.ds(t, 1), :], xl[n][:, 0, bass.ds(t, 1), :],
                              n % 2)
                    dve.wait_ge(s_sg, 2 * t + (u + 1))
                    dve.wait_ge(s_spill, 32 * t + 16)
                    V.tensor_tensor(sq[:, u, :], rstd[:, u, :], bank[u][:], ALU.mult).then_inc(s_free[u], 1)
            dve.wait_ge(s_lt, 2)
            repeat(dve, CI // 2, gate, o, 1)
            dve.wait_ge(s_const, 2)

            def by_chunk(x):
                return x.rearrange("p (c t) -> p c t", c=NCH)

            def mix(j):
                n0 = 4 * j + U_MIX
                w_low(n0 + 1, 1, rows=LORA, nkb=2)
                dve.wait_ge(s_unit, n0 + 1)
                V.tensor_scalar(kk[:], bank[0][:], col("a_kk", j), None, ALU.mult).then_inc(s_kk, 1)
                V.tensor_copy(kraw[:], bank[0][:]).then_inc(s_free[0], 1)
                w_low(n0 + 2, 0)
                dve.wait_ge(s_unit, n0 + 2)
                V.tensor_scalar(zw[:], bank[1][:], col("a_w0", j), CLAMP, ALU.add, ALU.max).then_inc(s_zw, 1)
                V.tensor_scalar(za[:], bank[3][:], col("a_a0", j), CLAMP, ALU.add, ALU.max).then_inc(s_free[1], 1)
                o(V.tensor_scalar(head_rk[:], head_ones[:], col("a_rk", j), None, ALU.mult))
                dve.wait_ge(s_n2, j + 1)
                V.tensor_scalar(n2[:], bank[4][:], 1e-24, None, ALU.max).then_inc(s_n2m, 1)
                dve.wait_ge(s_sw, j + 1)
                o(V.tensor_scalar(lw[:, :, 1:W1], by_chunk(zw[:]), -EDECAY, None, ALU.mult))
                V.tensor_tensor_scan(out=cs[:].rearrange("p c t -> p (c t)"),
                                     data0=scanm[:].rearrange("p c t -> p (c t)"),
                                     data1=lw[:].rearrange("p c t -> p (c t)"), initial=0.0,
                                     op0=ALU.mult, op1=ALU.add).then_inc(s_cs, 1)
                w_low(n0 + 3, 1)
                dve.wait_ge(s_sa, j + 1)
                o(V.tensor_scalar(kp[:], za[:], col("a_ka", j), neg_ka[:, bass.ds(j, 1)], ALU.mult, ALU.add))
                o(V.tensor_tensor(kp[:], kp[:], kraw[:], ALU.mult))
                dve.wait_ge(s_unit, n0 + 3)
                V.tensor_tensor(rk[:], kp[:], bank[0][:], ALU.mult).then_inc(s_rk, 1)
                dve.wait_ge(s_pw, j + 1)
                dve.wait_ge(s_spill, j * SPILL_TILE + SPILL_MIX)
                V.tensor_tensor(by_chunk(o_r[:]), pw[:, :, 1:W1], by_chunk(bank[0][:]), ALU.mult).then_inc(s_free[0], 1)
                w_low(n0 + 4, 0)
                dve.wait_ge(s_rn, j + 1)
                o(V.tensor_tensor(kn[:], kk[:], rn[:], ALU.mult))
                o(V.tensor_tensor(kka[:], kn[:], za[:], ALU.mult))
                V.tensor_tensor(by_chunk(o_q[:]), by_chunk(kn[:]), pw[:, :, 0:C], ALU.mult).then_inc(s_fin, 1)
                V.tensor_tensor(by_chunk(o_b[:]), by_chunk(kka[:]), pinv[:, :, 1:W1], ALU.mult).then_inc(s_fin, 1)
                V.tensor_tensor(by_chunk(o_c[:]), by_chunk(kp[:]), pinv[:, :, 1:W1], ALU.mult).then_inc(s_fin, 1)
                dve.wait_ge(s_bon, j + 1)
                dve.wait_ge(s_free[1], 2 * j + (FREE_MIX + 2))
                V.tensor_tensor(o_bv[:], o_v[:], bank[5][:], ALU.mult).then_inc(s_fin, 1)
            repeat(dve, CI, mix, o, 6)
            recurrence_vector(dve, o)

            for k in range(CI):
                dve.wait_ge(s_xhi, X_Y + k + 1)
                half = xl[k // DK]
                V.tensor_tensor(half[:, 1, k % DK, :], Y[:, k, :], half[:, 0, k % DK, :].bitcast(F32),
                                ALU.subtract).then_inc(s_xlo, 1)
            dve.wait_ge(s_back, 16)

            def even(base, turns, dst, add, n=None, final=False):
                if n is not None:
                    o(V.memset(acc[:], 0.0))

                def turn(t, last=False):
                    for u in range(2):
                        if not (last and u == 1):
                            w_low(2 * t + (base + u + 1), 1 - u)
                        dve.wait_ge(s_unit, 2 * t + (base + u + 1))
                        where = dst[:, bass.ds(2 * t + u, 1), :]
                        (V.tensor_tensor(where, where, bank[u][:], ALU.add) if add else
                         V.tensor_copy(where, bank[u][:])).then_inc(s_free[u], 1)
                        if n is not None:
                            dve.wait_ge(s_sq, 2 * t + (n * DK + u + 1))
                            dve.wait_ge(s_sqa, 2 * t + (n * DK + u))
                            V.tensor_tensor(acc[:], acc[:], sq[:, u, :], ALU.add).then_inc(s_sqa, 1)
                repeat(dve, turns - final, turn)
                if final:
                    turn(turns - 1, last=True)

            def split(x0, dst, n):
                def step(k, make):
                    if x0 + k >= 2:
                        dve.wait_ge(s_xlo, x0 + k - 1)
                    make(tmp[:, k % 2, :]).then_inc(s_tmp, 1)
                    if k:
                        x_low(x0 + k - 1, dst[:, 1, k - 1, :], dst[:, 0, k - 1, :], (k - 1) % 2)
                    if k == n - 1:
                        x_low(x0 + k, dst[:, 1, k, :], dst[:, 0, k, :], k % 2)
                return step

            for half in range(2):
                even(U_OUT1 + half * DK, DK // 2, xT2, True, n=1 if half else None)

            o(V.memset(cu[:, 0:2], 0.0))
            dve.wait_ge(s_xlo, X_H2)
            norm(1, "b_norm", split(X_H2, xl[2], DK), xT2, summed=True)
            for half in range(2):
                base = U_CONV + half * (4 * KB + DK)

                def conv(t):
                    n0 = 4 * t + base
                    w_low(n0 + 1, 1)
                    dve.wait_ge(s_unit, n0 + 1)
                    V.tensor_copy(c_sb[:], bank[0][:]).then_inc(s_free[0], 1)
                    w_low(n0 + 2, 0)
                    dve.wait_ge(s_unit, n0 + 2)
                    dve.wait_ge(s_free[0], 2 * t + (base // 2 + 1))
                    V.tensor_tensor(cu[:, 2:2 + T], c_sb[:], bank[1][:], ALU.mult).then_inc(s_free[1], 1)
                    dve.wait_ge(s_free[1], 2 * t + (base // 2 + 1))
                    ct = t + KB * half
                    o(V.tensor_scalar(conv3[:, 0, :], cu[:, 0:T], col("b_conv", ct), None, ALU.mult))
                    for tap in (1, 2):
                        o(V.scalar_tensor_tensor(out=conv3[:, tap % 2, :], in0=cu[:, tap:tap + T],
                                                 scalar=col("b_conv", ct + tap * CI), in1=conv3[:, 1 - tap % 2, :],
                                                 op0=ALU.mult, op1=ALU.add))
                    w_low(n0 + 3, 1)
                    dve.wait_ge(s_unit, n0 + 3)
                    V.tensor_scalar(gate3[:], bank[0][:], CLAMP, None, ALU.max).then_inc(s_zc, 1)
                    dve.wait_ge(s_sc, ct + 1)
                    V.tensor_tensor(gate3[:], gate3[:], bank[0][:], ALU.mult).then_inc(s_free[0], 1)
                    dve.wait_ge(s_free[0], 2 * t + (base // 2 + 2))
                    o(V.tensor_tensor(gate3[:], gate3[:], conv3[:, 0, :], ALU.mult))
                    w_low(n0 + 4, 0)
                    dve.wait_ge(s_unit, n0 + 4)
                    V.tensor_tensor(tmp[:, 0, :], gate3[:], bank[1][:], ALU.mult).then_inc(s_free[1], 1)
                    x_low(t + (X_YC + KB * half), xl[half][:, 1, bass.ds(t, 1), :], xl[half][:, 0, bass.ds(t, 1), :], 0)
                repeat(dve, KB, conv, o, 4)
                even(base + 4 * KB, DK // 2, xT2, True, n=2 if half else None)

            norm(2, "final_norm", lambda k, scaled: scaled(xT2[:, k, :]).then_inc(s_xn, 1), xT2,
                 summed=True)
            o(V.memset(glu[:, :, 0:PAD2], 0.0))
            norm(3, "norm_mix_pre_2", split(X_H3, xh, DK), xT2)
            def taps():
                a = [(1, n) for n in range(TAPS2)] + [(3, n) for n in range(TAPS2)]
                b = [(2, n) for n in range(TAPS2)]
                order = a[:6]
                for n in range(6, len(a)):
                    order += a[n:n + 1] + b[n - 6:n - 5]
                for n, (j, tap) in enumerate(order):
                    y, w = dconv[:, j, :], col("conv_dw_w_2", tap * CT + j)
                    if tap == 0:
                        V.tensor_scalar(y, glu[:, j, 0:T], w, col("conv_dw_b_2", j), ALU.mult, ALU.add).then_inc(s_tap, 1)
                    else:
                        dve.wait_ge(s_tap, order.index((j, tap - 1)) + 1)
                        V.scalar_tensor_tensor(out=y, in0=glu[:, j, tap:tap + T], scalar=w, in1=y, op0=ALU.mult,
                                               op1=ALU.add).then_inc(s_tap, 1)
                    yield
            tap = taps()
            for j in range(CT):
                n0 = U_GLU + 2 * j
                w_low(n0 + 1, 1)
                dve.wait_ge(s_unit, n0 + 1)
                V.tensor_copy(glu[:, j, PAD2:], bank[0][:]).then_inc(s_free[0], 1)
                w_low(n0 + 2, 0)
                for _ in range(6 if j >= 2 else 0):
                    next(tap)
                dve.wait_ge(s_unit, n0 + 2)
                V.tensor_scalar(rstd[:, j % 2, :], bank[1][:], CLAMP, None, ALU.max).then_inc(s_free[1], 1)
                dve.wait_ge(s_glu, j + 1)
                V.tensor_tensor(glu[:, j, PAD2:], rstd[:, j % 2, :], glu[:, j, PAD2:], ALU.mult).then_inc(s_gluok, 1)
                dve.wait_ge(s_gluok, j + 1)
            v_ch = [sq[:, 0, :], sq[:, 1, :], rstd[:, 0, :], rstd[:, 1, :]]
            for n in range(3 * AT):
                u = U_QKV + n
                w_low(u + 1, (n + 1) % 2)
                dve.wait_ge(s_unit, u + 1)
                src = bank[n % 2][:]
                if n < AT:
                    ins = V.tensor_scalar(qT[:, n, :], src, 0.125, None, ALU.mult)
                elif n < 2 * AT:
                    ins = V.tensor_copy(kT[:, n - AT, :], src)
                else:
                    ins = V.tensor_copy(v_ch[n - 2 * AT], src)
                ins.then_inc(s_free[n % 2], 1)
                for _ in range(6):
                    next(tap, None)
            def gate2(n):
                if n is None:
                    return
                if n:
                    m = n - 1
                    dve.wait_ge(s_unit, U_GATES2 + m + 1)
                    V.tensor_scalar(gates[:, m % 2, m // 2, :], bank[m % 2][:], CLAMP, None, ALU.max).then_inc(
                        s_free[m % 2], 1)
                if n < 2 * DK:
                    w_low(U_GATES2 + n + 1, (n + 1) % 2)

            finish = split(X_UC, uc, CT)

            def layer_norm(step):
                if step == 0:
                    dve.wait_ge(s_tap0, 1)
                    dve.wait_ge(s_tap, (CT - 1) * TAPS2)
                    o(V.tensor_tensor(acc[:], dconv[:, 0, :], dconv[:, 1, :], ALU.add))
                    V.tensor_tensor(acc[:], acc[:], dconv[:, 2, :], ALU.add).then_inc(s_dc, 1)
                    dve.wait_ge(s_dc, 1)
                    V.tensor_tensor(acc[:], acc[:], dconv[:, 3, :], ALU.add).then_inc(s_dc, 1)
                if step == 1:
                    dve.wait_ge(s_lnm, 1)
                    for j in range(CT):
                        V.scalar_tensor_tensor(out=dconv[:, j, :], in0=bank[4][:], scalar=-2.0, in1=dconv[:, j, :],
                                               op0=ALU.mult, op1=ALU.add).then_inc(s_cen, 1)
                    for j in range(CT):
                        dve.wait_ge(s_lsq, j + 1)
                        if j == 0:
                            V.tensor_copy(acc[:], sq[:, 0, :]).then_inc(s_lacc, 1)
                        else:
                            dve.wait_ge(s_lacc, j)
                            V.tensor_tensor(acc[:], acc[:], sq[:, j % 2, :], ALU.add).then_inc(s_lacc, 1)
                if step >= 3:
                    j = step - 3
                    y = dconv[:, j, :]
                    if j == 0:
                        dve.wait_ge(s_lrs, 1)
                    o(V.tensor_tensor(y, y, rstd[:, 1, :], ALU.mult))
                    o(V.tensor_scalar(y, y, col("conv_ln_g_2", j), col("conv_ln_b_2", j), ALU.mult, ALU.add))
                    V.tensor_scalar(sq[:, j % 2, :], y, CLAMP, None, ALU.max).then_inc(s_lz, 1)
                    dve.wait_ge(s_ls, j + 1)
                    finish(j, lambda where: V.tensor_tensor(where, y, sq[:, j % 2, :], ALU.mult))
            for n in range(GATES_FIRST):
                gate2(n)
                if n == LN_AT:
                    for _ in tap:
                        pass
                if n < LN_AT:
                    for _ in range(6):
                        next(tap, None)
                layer_norm(n - LN_AT)
            attention_vector(dve, o, split(X_AT, ah, AT), gate2)
            gate2(2 * DK)

            finish = split(X_MG, xh, DK)
            for n in range(DK):
                w_low(U_MERGE + n + 1, (n + 1) % 2)
                dve.wait_ge(s_unit, U_MERGE + n + 1)
                if n == 0:
                    dve.wait_ge(s_gate2, 2 * DK)
                o(V.scalar_tensor_tensor(out=sq[:, 0, :], in0=bank[n % 2][:], scalar=col("b_conv_branch_2", n),
                                         in1=gates[:, 0, n, :], op0=ALU.add, op1=ALU.mult))
                V.tensor_tensor(sq[:, 1, :], bank[2 + n % 2][:], gates[:, 1, n, :], ALU.mult).then_inc(s_free[n % 2], 1)
                dve.wait_ge(s_free[n % 2], (U_MERGE + n) // 2 + 1)
                finish(n, lambda where: V.tensor_tensor(where, sq[:, 0, :], sq[:, 1, :], ALU.add))
            even(U_WOUT2, DK // 2, mixed, False, n=4)

            def residual(n, gain, src, signal):
                def step(k, scaled):
                    scaled(src[:, k, :]).then_inc(s_scaled, 1)
                    for m in ([k - 1] if k else []) + ([k] if k == DK - 1 else []):
                        dve.wait_ge(s_scaled, (DK if n == 6 else 0) + m + 1)
                        V.tensor_tensor(xT2[:, m, :], xT2[:, m, :], src[:, m, :], ALU.add).then_inc(signal, 1)
                norm(n, gain, step, src, summed=True)
            residual(4, "norm_mix_post_2", mixed, s_mg)

            norm(5, "norm_ffn_pre_2", split(X_H4, xl[0], DK), xT2)
            base = U_FFN
            for part, (j0, n) in enumerate(FPARTS):
                dst = xl[1 + part % 2]

                def ffn(t):
                    n0 = 2 * t + base
                    w_low(n0 + 1, 1)
                    dve.wait_ge(s_unit, n0 + 1)
                    V.tensor_scalar(rstd[:, 0, :], bank[0][:], CLAMP, None, ALU.max).then_inc(s_ug, 1)
                    w_low(n0 + 2, 0)
                    dve.wait_ge(s_us, t + (j0 + 1))
                    V.tensor_tensor(rstd[:, 0, :], rstd[:, 0, :], bank[0][:], ALU.mult).then_inc(s_free[0], 1)
                    dve.wait_ge(s_unit, n0 + 2)
                    dve.wait_ge(s_free[0], t + (base // 2 + 1))
                    V.tensor_tensor(tmp[:, 0, :], rstd[:, 0, :], bank[1][:], ALU.mult).then_inc(s_free[1], 1)
                    x_low(t + (X_FF + j0), dst[:, 1, bass.ds(t, 1), :], dst[:, 0, bass.ds(t, 1), :], 0)
                repeat(dve, n, ffn)
                last = part == len(FPARTS) - 1
                even(base + 2 * n, DK // 2, ffo, part > 0, n=6 if last else None, final=last)
                base += 2 * n + DK
            residual(6, "norm_ffn_post_2", ffo, s_ffn)


_INS = ['x', 'a_norm', 'a_mu', 'a_w_in', 'a_w0', 'a_w1', 'a_w2', 'a_a0', 'a_a1', 'a_a2', 'a_kk', 'a_ka', 'a_rk',
        'a_lnw', 'a_lnb', 'a_w_out', 'b_norm', 'b_w_in', 'b_conv', 'b_w_out', 'final_norm', 'norm_mix_pre_2',
        'w_in_2', 'conv_dw_w_2', 'conv_dw_b_2', 'conv_ln_g_2', 'conv_ln_b_2', 'w_conv_branch_2', 'b_conv_branch_2',
        'w_att_branch_2', 'w_out_2', 'norm_mix_post_2', 'norm_ffn_pre_2', 'w_ffn_up_2', 'w_ffn_down_2',
        'norm_ffn_post_2']


def kernel(**inputs):
    import numpy as _np
    import concourse.bacc as _bacc
    from concourse import mybir as _mybir
    from concourse.bass_utils import run_bass_kernel_spmd as _run

    nc = _bacc.Bacc("TRN2", target_bir_lowering=False, num_devices=1)
    arrays, args = {}, {}
    for name in _INS:
        a = _np.ascontiguousarray(inputs[name])
        arrays[f"in_{name}"] = a
        args[name] = nc.dram_tensor(f"in_{name}", a.shape, _mybir.dt.from_np(a.dtype), kind="ExternalInput").ap()
    out = nc.dram_tensor("out_0", (1, T, D), F32, kind="ExternalOutput").ap()
    program(nc, args, out)
    r = _run(nc, [arrays], core_ids=[0])
    return r.results[0]["out_0"]
```
